# Optimizing a Trainium2 kernel written in Bass

```python
import jax, jax.numpy as jnp
from jax import lax
import numpy as np

D_MODEL = 1024
BATCH = 1
SEQ = 128
DEPTH = 1
DEC_BATCH = 1
DEC_SEQ = 512
PAST_LEN = 128

GRID_W = 64
MIX_WIDTH = D_MODEL
GLA_WIDTH = MIX_WIDTH // 2
GLA_HEADS = 4
GLA_DK = GLA_WIDTH // 2 // GLA_HEADS
GLA_DV = GLA_WIDTH // GLA_HEADS
GLA_QK = GLA_HEADS * GLA_DK
GLA_RANK = 16
GLA_NORMALIZER = 16.0
GLA_CHUNK = 64
RWKV_WIDTH = MIX_WIDTH - GLA_WIDTH
RWKV_N = 64
RWKV_HEADS = RWKV_WIDTH // RWKV_N
DECAY_RANK = 64
AAA_RANK = 64
GATE_RANK = 128
N_EXPERTS = 64
TOP_K = 8
N_GROUPS = 8
TOPK_GROUPS = 4
EXPERT_FF = D_MODEL // 4
ROUTED_SCALE = 2.5
MOE_BLOCK = 256
EPS = 1e-6
RWKV_LN_EPS = 64e-5
GLA_COLS = 2 * GLA_QK + 2 * GLA_WIDTH + 2 * GLA_RANK
RWKV_COLS = 3 * RWKV_WIDTH + 2 * DECAY_RANK + AAA_RANK + GATE_RANK
PROJ_COLS = GLA_COLS + RWKV_COLS

kernel_name = 'hybrid_gla_rwkv7_moe_diffusion_step'

def rmsnorm(x, g):
    xf = x.astype(jnp.float32)
    y = xf * lax.rsqrt(jnp.mean(xf * xf, axis=-1, keepdims=True) + EPS)
    return (y * g).astype(x.dtype)

def adaln_params(cvec, w, b):
    mod = jax.nn.silu(cvec) @ w + b
    return jnp.split(mod[..., None, :], 6, axis=-1)

def flip_t(a):
    return jnp.flip(a, axis=1)

def conv_latent(u, wconv):
    b, t, ch = u.shape
    rows = t // GRID_W
    img = u.reshape(b, rows, GRID_W, ch)
    out = lax.conv_general_dilated(img, wconv[:, :, None, :], window_strides=(1, 1), padding='SAME',
                                   dimension_numbers=('NHWC', 'HWIO', 'NHWC'), feature_group_count=ch)
    return out.reshape(b, t, ch)

def conv_context(u, wconv):
    ch = u.shape[-1]
    return lax.conv_general_dilated(u, wconv[1][:, None, :], window_strides=(1,), padding='SAME',
                                    dimension_numbers=('NWC', 'WIO', 'NWC'), feature_group_count=ch)

def gla_chunked(q, k, v, gk, s0):
    b, t, h, dk = q.shape
    dv = v.shape[-1]
    nc = t // GLA_CHUNK
    f32 = jnp.float32

    def to_chunks(a):
        return a.astype(f32).reshape(b, nc, GLA_CHUNK, h, a.shape[-1]).transpose(1, 0, 3, 2, 4)

    causal = jnp.tril(jnp.ones((GLA_CHUNK, GLA_CHUNK), dtype=bool))

    def step(s, xs):
        qc, kc, vc, gc = xs
        cum = jnp.cumsum(gc, axis=-2)
        o_inter = jnp.einsum('bhcd,bhde->bhce', qc * jnp.exp(cum), s)
        rel = jnp.where(causal[:, :, None], cum[..., :, None, :] - cum[..., None, :, :], -jnp.inf)
        attn = jnp.einsum('bhid,bhjd,bhijd->bhij', qc, kc, jnp.exp(rel))
        o = o_inter + jnp.einsum('bhij,bhje->bhie', attn, vc)
        s = jnp.exp(cum[..., -1, :])[..., None] * s + jnp.einsum('bhcd,bhce->bhde', kc * jnp.exp(cum[..., -1:, :] - cum), vc)
        return s, o

    s, o = lax.scan(step, s0.astype(f32), (to_chunks(q), to_chunks(k), to_chunks(v), to_chunks(gk)))
    return o.transpose(1, 0, 3, 2, 4).reshape(b, t, h, dv), s

def gla_mixer(u, s_fwd, s_bwd, w_dec, b_dec, norm_g):
    b, t, _ = u.shape
    f32 = jnp.float32
    q, k, v, g, z_f, z_b = jnp.split(u, np.cumsum([GLA_QK, GLA_QK, GLA_WIDTH, GLA_WIDTH, GLA_RANK]).tolist(), axis=-1)
    q = q.reshape(b, t, GLA_HEADS, GLA_DK) * (GLA_DK ** -0.5)
    k = k.reshape(b, t, GLA_HEADS, GLA_DK)
    v = v.reshape(b, t, GLA_HEADS, GLA_DV)

    def log_decay(z, w, bias):
        return (jax.nn.log_sigmoid((z @ w + bias).astype(f32)) / GLA_NORMALIZER).reshape(b, t, GLA_HEADS, GLA_DK)

    o_f, s_f = gla_chunked(q, k, v, log_decay(z_f, w_dec[0], b_dec[0]), s_fwd)
    o_b, s_b = gla_chunked(flip_t(q), flip_t(k), flip_t(v), flip_t(log_decay(z_b, w_dec[1], b_dec[1])), s_bwd)
    o = o_f + flip_t(o_b)
    o = o * lax.rsqrt(jnp.mean(o * o, axis=-1, keepdims=True) + EPS)
    o = o.reshape(b, t, GLA_WIDTH) * norm_g * jax.nn.silu(g.astype(f32))
    return o.astype(u.dtype), s_f, s_b

def rwkv_scan(r, w, k, v, kk, a, s0):
    def step(s, xs):
        rt, wt, kt, vt, kkt, at = xs
        sa = jnp.einsum('bhvk,bhk->bhv', s, -kkt)
        s = s * wt[:, :, None, :] + sa[..., None] * (kkt * at)[:, :, None, :] + vt[..., None] * kt[:, :, None, :]
        return s, jnp.einsum('bhvk,bhk->bhv', s, rt)

    xs = tuple(jnp.moveaxis(z, 1, 0) for z in (r, w, k, v, kk, a))
    s, y = lax.scan(step, s0.astype(jnp.float32), xs)
    return jnp.moveaxis(y, 0, 1), s

def rwkv_mixer(u, s_fwd, s_bwd, w2, w0, a2, a0, g2, k_k, k_a, r_k, ln_g, ln_b):
    b, t, _ = u.shape
    f32 = jnp.float32
    uf = u.astype(f32)
    r, k, v, z_wf, z_wb, z_a, z_g = jnp.split(uf, np.cumsum([RWKV_WIDTH] * 3 + [DECAY_RANK] * 2 + [AAA_RANK]).tolist(), axis=-1)

    def hd(z):
        return z.reshape(b, t, RWKV_HEADS, RWKV_N)

    def ph(p):
        return p.astype(f32).reshape(RWKV_HEADS, RWKV_N)

    def decay(z, w2d, w0d):
        w = -jax.nn.softplus(-(w0d.astype(f32) + jnp.tanh(z) @ w2d.astype(f32))) - 0.5
        return hd(jnp.exp(-jnp.exp(w)))

    a = hd(jax.nn.sigmoid(a0.astype(f32) + z_a @ a2.astype(f32)))
    g = jax.nn.sigmoid(z_g) @ g2.astype(f32)
    r, k, v = hd(r), hd(k), hd(v)
    kk = k * ph(k_k)
    kk = kk * lax.rsqrt(jnp.maximum(jnp.sum(kk * kk, axis=-1, keepdims=True), 1e-24))
    k = k * (1.0 + (a - 1.0) * ph(k_a))
    y_f, s_f = rwkv_scan(r, decay(z_wf, w2[0], w0[0]), k, v, kk, a, s_fwd)
    y_b, s_b = rwkv_scan(flip_t(r), flip_t(decay(z_wb, w2[1], w0[1])), flip_t(k), flip_t(v), flip_t(kk), flip_t(a), s_bwd)
    y = y_f + flip_t(y_b)
    mu = jnp.mean(y, axis=-1, keepdims=True)
    var = jnp.mean(jnp.square(y - mu), axis=-1, keepdims=True)
    y = (y - mu) * lax.rsqrt(var + RWKV_LN_EPS) * ph(ln_g) + ph(ln_b)
    bonus = jnp.sum(r * k * ph(r_k), axis=-1, keepdims=True) * v
    out = (y + bonus).reshape(b, t, RWKV_WIDTH) * g
    return out.astype(u.dtype), s_f, s_b

def swiglu(x, w1, w3, w2):
    return (jax.nn.silu(x @ w1) * (x @ w3)) @ w2

def route(xt, w_router, bias):
    t = xt.shape[0]
    f32 = jnp.float32
    scores = jax.nn.sigmoid(xt.astype(f32) @ w_router.astype(f32))
    sel = scores + bias.astype(f32)
    grp_top2, _ = lax.top_k(sel.reshape(t, N_GROUPS, N_EXPERTS // N_GROUPS), 2)
    _, gidx = lax.top_k(jnp.sum(grp_top2, axis=-1), TOPK_GROUPS)
    gmask = jnp.sum(jax.nn.one_hot(gidx, N_GROUPS, dtype=jnp.int32), axis=-2) > 0
    sel = jnp.where(jnp.repeat(gmask, N_EXPERTS // N_GROUPS, axis=-1), sel, -jnp.inf)
    _, idx = lax.top_k(sel, TOP_K)
    wts = jnp.take_along_axis(scores, idx, axis=-1)
    wts = wts / jnp.sum(wts, axis=-1, keepdims=True) * ROUTED_SCALE
    return idx, wts

def routed_experts(xt, idx, wts, w1, w3, w2):
    t, d = xt.shape
    n_assign = t * TOP_K
    n_blocks = -(-n_assign // MOE_BLOCK) + N_EXPERTS
    e_flat = idx.reshape(-1)
    tok_flat = jnp.arange(n_assign, dtype=jnp.int32) // TOP_K
    order = jnp.argsort(e_flat)
    e_sorted = e_flat[order]
    counts = jnp.bincount(e_flat, length=N_EXPERTS)
    padded = (counts + MOE_BLOCK - 1) // MOE_BLOCK * MOE_BLOCK
    pad_end = jnp.cumsum(padded)
    pad_start = pad_end - padded
    start = jnp.cumsum(counts) - counts
    dest = pad_start[e_sorted] + jnp.arange(n_assign, dtype=jnp.int32) - start[e_sorted]
    slot_tok = jnp.full((n_blocks * MOE_BLOCK,), t, jnp.int32).at[dest].set(tok_flat[order])
    slot_w = jnp.zeros((n_blocks * MOE_BLOCK,), xt.dtype).at[dest].set(wts.reshape(-1)[order].astype(xt.dtype))
    blk_e = jnp.minimum(jnp.searchsorted(pad_end, jnp.arange(n_blocks, dtype=jnp.int32) * MOE_BLOCK, side='right'), N_EXPERTS - 1)
    x_pad = jnp.concatenate([xt, jnp.zeros((1, d), xt.dtype)], axis=0)

    def step(y, blk):
        ids, wb, e = blk
        return y.at[ids].add(swiglu(x_pad[ids], w1[e], w3[e], w2[e]) * wb[:, None]), None

    y, _ = lax.scan(step, jnp.zeros_like(x_pad),
                    (slot_tok.reshape(n_blocks, MOE_BLOCK), slot_w.reshape(n_blocks, MOE_BLOCK), blk_e))
    return y[:t]

def moe(h, w_router, bias, w1, w3, w2, ws1, ws3, ws2):
    xt = h.reshape(-1, h.shape[-1])
    idx, wts = route(xt, w_router, bias)
    y = routed_experts(xt, idx, wts, w1, w3, w2) + swiglu(xt, ws1, ws3, ws2)
    return y.reshape(h.shape)

def layer_forward(x, mod, latent, s_gla, s_rwkv, p):
    sh1, sc1, g1, sh2, sc2, g2 = mod
    h = rmsnorm(x, p['norm1']) * (1.0 + sc1) + sh1
    u = h @ p['w_in']
    u_gla, u_rwkv = u[..., :GLA_COLS], u[..., GLA_COLS:]
    u_rwkv = conv_latent(u_rwkv, p['rwkv_conv']) if latent else conv_context(u_rwkv, p['rwkv_conv'])
    o_gla, sgf, sgb = gla_mixer(u_gla, s_gla[0], s_gla[1], p['gla_w_dec'], p['gla_b_dec'], p['gla_norm'])
    o_rwkv, srf, srb = rwkv_mixer(u_rwkv, s_rwkv[0], s_rwkv[1], p['rwkv_w2'], p['rwkv_w0'], p['rwkv_a2'], p['rwkv_a0'],
                                  p['rwkv_g2'], p['rwkv_k_k'], p['rwkv_k_a'], p['rwkv_r_k'], p['rwkv_ln_g'], p['rwkv_ln_b'])
    x = x + g1 * (jnp.concatenate([o_gla, o_rwkv], axis=-1) @ p['w_out'])
    h = rmsnorm(x, p['norm2']) * (1.0 + sc2) + sh2
    x = x + g2 * moe(h, p['router_w'], p['router_b'], p['exp_w1'], p['exp_w3'], p['exp_w2'], p['sh_w1'], p['sh_w3'], p['sh_w2'])
    return x, (sgf, sgb), (srf, srb)

def setup_inputs(seed: int = 0) -> dict:
    key = jax.random.key(seed)
    ks = iter(jax.random.split(key, 48))

    def nrm(shape, s):
        return s * jax.random.normal(next(ks), shape, jnp.float32)

    D, E, F = D_MODEL, N_EXPERTS, EXPERT_FF
    conv = nrm((DEPTH, 3, 3, RWKV_COLS), 0.2).at[:, 1, 1].add(1.0)
    return {
        'x_prompt': nrm((BATCH, SEQ, D), 1.0),
        'x_sample': nrm((DEC_BATCH, DEC_SEQ, D), 1.0),
        'c': nrm((DEC_BATCH, D), 1.0),
        'state_gla': nrm((DEC_BATCH, DEPTH, 2, GLA_HEADS, GLA_DK, GLA_DV), 0.5),
        'state_rwkv': nrm((DEC_BATCH, DEPTH, 2, RWKV_HEADS, RWKV_N, RWKV_N), 0.3),
        'c_ctx': nrm((D,), 1.0),
        'ada_w': nrm((DEPTH, D, 6 * D), 0.3 * D ** -0.5),
        'ada_b': nrm((DEPTH, 6 * D), 0.02),
        'norm1': 1.0 + nrm((DEPTH, D), 0.05),
        'norm2': 1.0 + nrm((DEPTH, D), 0.05),
        'norm_f': 1.0 + nrm((D,), 0.05),
        'w_in': nrm((DEPTH, D, PROJ_COLS), D ** -0.5),
        'w_out': nrm((DEPTH, MIX_WIDTH, D), MIX_WIDTH ** -0.5),
        'gla_w_dec': nrm((DEPTH, 2, GLA_RANK, GLA_QK), GLA_RANK ** -0.5),
        'gla_b_dec': nrm((DEPTH, 2, GLA_QK), 0.1),
        'gla_norm': 1.0 + nrm((DEPTH, GLA_WIDTH), 0.05),
        'rwkv_conv': conv,
        'rwkv_w2': nrm((DEPTH, 2, DECAY_RANK, RWKV_WIDTH), 0.5 * DECAY_RANK ** -0.5),
        'rwkv_w0': -1.0 + nrm((DEPTH, 2, RWKV_WIDTH), 0.5),
        'rwkv_a2': nrm((DEPTH, AAA_RANK, RWKV_WIDTH), AAA_RANK ** -0.5),
        'rwkv_a0': nrm((DEPTH, RWKV_WIDTH), 0.1),
        'rwkv_g2': nrm((DEPTH, GATE_RANK, RWKV_WIDTH), GATE_RANK ** -0.5),
        'rwkv_k_k': 0.85 + nrm((DEPTH, RWKV_WIDTH), 0.05),
        'rwkv_k_a': 1.0 + nrm((DEPTH, RWKV_WIDTH), 0.05),
        'rwkv_r_k': nrm((DEPTH, RWKV_WIDTH), 0.1),
        'rwkv_ln_g': 1.0 + nrm((DEPTH, RWKV_WIDTH), 0.05),
        'rwkv_ln_b': nrm((DEPTH, RWKV_WIDTH), 0.02),
        'router_w': nrm((DEPTH, D, E), D ** -0.5),
        'router_b': nrm((DEPTH, E), 0.01),
        'exp_w1': nrm((DEPTH, E, D, F), D ** -0.5),
        'exp_w3': nrm((DEPTH, E, D, F), D ** -0.5),
        'exp_w2': nrm((DEPTH, E, F, D), F ** -0.5),
        'sh_w1': nrm((DEPTH, D, F), D ** -0.5),
        'sh_w3': nrm((DEPTH, D, F), D ** -0.5),
        'sh_w2': nrm((DEPTH, F, D), F ** -0.5),
    }

def reference(x_prompt, x_sample, c, state_gla, state_rwkv, c_ctx, ada_w, ada_b, norm1, norm2, norm_f, w_in, w_out,
              gla_w_dec, gla_b_dec, gla_norm, rwkv_conv, rwkv_w2, rwkv_w0, rwkv_a2, rwkv_a0, rwkv_g2, rwkv_k_k, rwkv_k_a,
              rwkv_r_k, rwkv_ln_g, rwkv_ln_b, router_w, router_b, exp_w1, exp_w3, exp_w2, sh_w1, sh_w3, sh_w2):
    bp = x_prompt.shape[0]
    zero_gla = jnp.zeros((bp, GLA_HEADS, GLA_DK, GLA_DV), jnp.float32)
    zero_rwkv = jnp.zeros((bp, RWKV_HEADS, RWKV_N, RWKV_N), jnp.float32)
    xp, xs = x_prompt, x_sample
    new_gla, new_rwkv = [], []
    for l in range(DEPTH):
        p = {'norm1': norm1[l], 'norm2': norm2[l], 'w_in': w_in[l], 'w_out': w_out[l],
             'gla_w_dec': gla_w_dec[l], 'gla_b_dec': gla_b_dec[l], 'gla_norm': gla_norm[l],
             'rwkv_conv': rwkv_conv[l], 'rwkv_w2': rwkv_w2[l], 'rwkv_w0': rwkv_w0[l], 'rwkv_a2': rwkv_a2[l],
             'rwkv_a0': rwkv_a0[l], 'rwkv_g2': rwkv_g2[l], 'rwkv_k_k': rwkv_k_k[l], 'rwkv_k_a': rwkv_k_a[l],
             'rwkv_r_k': rwkv_r_k[l], 'rwkv_ln_g': rwkv_ln_g[l], 'rwkv_ln_b': rwkv_ln_b[l],
             'router_w': router_w[l], 'router_b': router_b[l], 'exp_w1': exp_w1[l], 'exp_w3': exp_w3[l],
             'exp_w2': exp_w2[l], 'sh_w1': sh_w1[l], 'sh_w3': sh_w3[l], 'sh_w2': sh_w2[l]}
        xp, s_g, s_r = layer_forward(xp, adaln_params(c_ctx, ada_w[l], ada_b[l]), False,
                                     (zero_gla, zero_gla), (zero_rwkv, zero_rwkv), p)
        new_gla.append(jnp.stack(s_g, axis=1))
        new_rwkv.append(jnp.stack(s_r, axis=1))
        xs, _, _ = layer_forward(xs, adaln_params(c, ada_w[l], ada_b[l]), True,
                                 (state_gla[:, l, 0], state_gla[:, l, 1]),
                                 (state_rwkv[:, l, 0], state_rwkv[:, l, 1]), p)
    y_prompt = rmsnorm(xp, norm_f)
    y_sample = rmsnorm(xs, norm_f)
    new_state_gla = jnp.stack(new_gla, axis=1)
    new_state_rwkv = jnp.stack(new_rwkv, axis=1)
    return (y_prompt, y_sample, new_state_gla, new_state_rwkv)


_drawn_inputs = setup_inputs


def setup_inputs(seed=0):
    import zlib

    import numpy as np

    out = dict(_drawn_inputs(seed))
    spreads = {}
    factors = {'state_gla': 8.0,
     'state_rwkv': 8.0,
     'gla_norm': 7.101,
     'rwkv_k_k': 18.209,
     'rwkv_ln_g': 8.0,
     'rwkv_ln_b': 38.486,
     'norm2': 2.833,
     'router_b': 2.819}
    for name, (base, spread) in spreads.items():
        noise = np.random.default_rng([zlib.crc32(name.encode()), seed]).standard_normal(out[name].shape)
        drawn = base * np.exp(spread * noise) if base else spread * noise
        out[name] = __import__('jax').numpy.asarray(drawn.astype(out[name].dtype))
    for name, factor in factors.items():
        out[name] = (out[name] * factor).astype(out[name].dtype)
    return out
```

```python
import math
from contextlib import ExitStack

import concourse.bass as bass
from concourse import mybir

ALU = mybir.AluOpType
ACT = mybir.ActivationFunctionType
AX = mybir.AxisListType.X
F32 = mybir.dt.float32
I32 = mybir.dt.int32
U32 = mybir.dt.uint32

P = 128
D = 1024
KD = D // P
CTX, LAT = 128, 512
TOK = CTX + LAT
NT = TOK // P
GRID_W, GRID_H = 64, LAT // 64
EPS = 1e-6
RWKV_LN_EPS = 64e-5
MOD = 6 * D
C = 64
NCH = TOK // C
CTX_CH, LAT_CH = CTX // C, LAT // C

GLA_H, GLA_DK, GLA_DV, GLA_RANK = 4, 64, 128, 16
GLA_QK, GLA_W = GLA_H * GLA_DK, GLA_H * GLA_DV
GLA_COLS = 2 * GLA_QK + 2 * GLA_W + 2 * GLA_RANK
RH, RN = 8, 64
RW = RH * RN
DECAY_RANK, AAA_RANK, GATE_RANK = 64, 64, 128
HP = RH // 2

NE, TOP_K, NG, TOPG = 64, 8, 8, 4
FF = D // 4
ROUTED_SCALE = 2.5


class Count:

    def __init__(self, sem):
        self.sem, self.n = sem, 0


class Chain:

    def __init__(self, eng, count):
        self.eng, self.count = eng, count

    def step(self, ins):
        self.count.n += 1
        ins.then_inc(self.count.sem, 1)
        self.eng.wait_ge(self.count.sem, self.count.n)


class Shared:
    pass


def build_constants(nc, g, pool, chain):
    chain.step(nc.gpsimd.memset(g.ones[:], 1.0))
    for n in range(7):
        size = 1 << n
        m = g.blocks[:, n, :]
        v = m.rearrange("p (a b) -> p a b", b=size)
        chain.step(nc.gpsimd.memset(m, 1.0))
        chain.step(nc.gpsimd.affine_select(out=v, in_=v, compare_op=ALU.is_ge, fill=0.0, base=0,
                                           pattern=[[-size, P // size], [0, size]], channel_multiplier=1))
        chain.step(nc.gpsimd.affine_select(out=v, in_=v, compare_op=ALU.is_ge, fill=0.0, base=size - 1,
                                           pattern=[[size, P // size], [0, size]], channel_multiplier=-1))
    for n in range(6):
        chain.step(nc.gpsimd.tensor_tensor(g.levels[:, n, :], g.blocks[:, n + 1, :], g.blocks[:, n, :],
                                           ALU.subtract))
    for d in range(2):
        for kind in range(2):
            sign = 1 if d == 0 else -1
            chain.step(nc.gpsimd.affine_select(out=g.tri[:, d, kind, :], in_=g.blocks[:, 6, :],
                                               compare_op=ALU.is_ge, fill=0.0, base=kind - 1,
                                               pattern=[[sign, P]], channel_multiplier=-sign))


def stage_modulation(nc, g, w):
    NB, NBUF = MOD // 512, 3
    with ExitStack() as ctx:
        def sb(name, shape, dt=F32):
            return ctx.enter_context(nc.sbuf_tensor(name, shape, dt))

        def sem(name):
            return ctx.enter_context(nc.semaphore(name))

        aw = sb("ada_w_sb", [P, NBUF, KD, 512])
        cT = sb("cT", [P, 2, KD])
        scT = sb("silu_cT", [P, KD, 2])
        modrow = sb("modrow", [2, MOD])
        adab = sb("adab", [2, MOD])
        nrm = sb("normrows", [2, 2, D])
        x = sb("x_sb", [P, NT, D])
        sq = sb("sq", [P, D])
        ss = sb("ss", [P, NT])
        rms = sb("rms", [P, NT])
        rstd = sb("rstd", [P, NT])
        wb = sb("wb", [P, 2, D])
        shb = sb("shb", [P, 2, D])
        hx = sb("hx", [P, 2, D])

        s_c, s_rows, s_x = sem("m_c"), sem("m_rows"), sem("m_x")
        s_aw = [sem(f"m_aw{n}") for n in range(NBUF)]
        s_silu, s_mm, s_ev = sem("m_silu"), sem("m_mm"), sem("m_ev")
        s_mod, s_st, s_bc = sem("m_mod"), sem("m_st"), sem("m_bc")
        s_sq, s_ms, s_rt, s_rstd = sem("m_sq"), sem("m_ms"), sem("m_rt"), sem("m_rstd")
        s_hx, s_tr, s_hT = sem("m_hx"), sem("m_tr"), sem("m_hT")
        s_const = sem("m_const")

        ada = w["ada_w"][0].rearrange("(p k) n -> p k n", k=KD)
        block = ctx.enter_context(nc.Block())

        @block.sync
        def _(sp):
            sp.dma_start(cT[:, 0, :], w["c_ctx"].rearrange("(p k) -> p k", k=KD)).then_inc(s_c, 16)
            sp.dma_start(cT[:, 1, :], w["c"][0].rearrange("(p k) -> p k", k=KD)).then_inc(s_c, 16)
            for n in range(NB):
                if n >= NBUF:
                    sp.wait_ge(s_mm, n - NBUF + 1)
                sp.dma_start(aw[:, n % NBUF], ada[:, :, n * 512:(n + 1) * 512]).then_inc(s_aw[n % NBUF], 16)
            sp.wait_ge(s_mod, 1)
            sp.dma_start(g.mod_dram, modrow[:, :]).then_inc(s_st, 16)
            sp.wait_ge(s_st, 16)
            for s in range(2):
                sp.dma_start(wb[:, s], g.mod_dram[s:s + 1, D:2 * D].to_broadcast([P, D])).then_inc(s_bc, 16)
                sp.dma_start(shb[:, s], g.mod_dram[s:s + 1, 0:D].to_broadcast([P, D])).then_inc(s_bc, 16)

        @block.gpsimd
        def _(pool):
            for s in range(2):
                pool.dma_start(adab[s:s + 1, :], w["ada_b"]).then_inc(s_rows, 16)
                pool.dma_start(nrm[s:s + 1, 0, :], w["norm1"]).then_inc(s_rows, 16)
                pool.dma_start(nrm[s:s + 1, 1, :], w["norm2"]).then_inc(s_rows, 16)
            build_constants(nc, g, pool, Chain(pool, g.pool_steps))
            nc.gpsimd.nop().then_inc(s_const, 1)

        @block.scalar
        def _(act):
            act.dma_start(x[:, 0, :], w["x_prompt"][0]).then_inc(s_x, 16)
            act.dma_start(x[:, 1:NT, :], w["x_sample"][0].rearrange("(t p) d -> p t d", p=P)).then_inc(s_x, 16)
            act.wait_ge(s_c, 32)
            nc.scalar.activation(scT[:].rearrange("p k s -> p s k"), cT[:], ACT.Silu).then_inc(s_silu, 1)
            act.wait_ge(s_x, 32)
            for t in range(NT):
                if t:
                    act.wait_ge(s_sq, t)
                nc.scalar.activation(sq[:], x[:, t, :], ACT.Square, accum_out=ss[:, t:t + 1]).then_inc(s_sq, 1)
            act.wait_ge(s_ms, 1)
            nc.scalar.activation(rms[:], rms[:], ACT.Sqrt).then_inc(s_rt, 1)
            for t in range(NT):
                for half in range(2):
                    n = 2 * t + half
                    act.wait_ge(s_tr, n + 1)
                    nc.scalar.copy(g.hT[:, 4 * half:4 * half + 4, t * P:(t + 1) * P],
                                   g.ps[:, 4 + n % 4, :].rearrange("p (k m) -> p k m", k=4)).then_inc(s_hT, 1)

        @block.vector
        def _(dve):
            chain = Chain(dve, g.dve_steps)
            dve.wait_ge(s_rows, 16 * 6)
            for n in range(NB):
                dve.wait_ge(s_mm, n + 1)
                nc.vector.tensor_tensor(modrow[:, n * 512:(n + 1) * 512], g.ps[0:2, n % 4, :],
                                        adab[:, n * 512:(n + 1) * 512], ALU.add).then_inc(s_ev, 1)
            dve.wait_ge(s_ev, NB)
            for n, part in enumerate((1, 4)):
                row = modrow[:, part * D:(part + 1) * D]
                chain.step(nc.vector.scalar_tensor_tensor(row, row, 1.0, nrm[:, n, :], ALU.add, ALU.mult))
            nc.vector.nop().then_inc(s_mod, 1)
            dve.wait_ge(s_sq, NT)
            nc.vector.tensor_scalar(rms[:], ss[:], 1.0 / D, EPS, ALU.mult, ALU.add).then_inc(s_ms, 1)
            dve.wait_ge(s_rt, 1)
            chain.step(nc.vector.reciprocal(rstd[:], rms[:]))
            dve.wait_ge(s_bc, 64)
            for t in range(NT):
                s = min(t, 1)
                if t >= 2:
                    dve.wait_ge(s_tr, 2 * (t - 1))
                chain.step(nc.vector.scalar_tensor_tensor(hx[:, t % 2], x[:, t, :], rstd[:, t:t + 1], wb[:, s],
                                                          ALU.mult, ALU.mult))
                nc.vector.tensor_tensor(hx[:, t % 2], hx[:, t % 2], shb[:, s], ALU.add).then_inc(s_hx, 1)

        @block.tensor
        def _(pe):
            pe.wait_ge(s_silu, 1)
            for n in range(NB):
                pe.wait_ge(s_aw[n % NBUF], 16 * (n // NBUF + 1))
                if n >= 4:
                    pe.wait_ge(s_ev, n - 3)
                for k in range(KD):
                    last = nc.tensor.matmul(g.ps[0:2, n % 4, :], scT[:, k, :], aw[:, n % NBUF, k, :],
                                            start=k == 0, stop=k == KD - 1)
                last.then_inc(s_mm, 1)
            pe.wait_ge(s_const, 1)
            for t in range(NT):
                pe.wait_ge(s_hx, t + 1)
                for half in range(2):
                    n = 2 * t + half
                    if n >= 4:
                        pe.wait_ge(s_hT, n - 3)
                    for k in range(4):
                        kk = 4 * half + k
                        last = nc.tensor.transpose(g.ps[:, 4 + n % 4, k * P:(k + 1) * P],
                                                   hx[:, t % 2, kk * P:(kk + 1) * P], g.blocks[:, 0, :])
                    last.then_inc(s_tr, 1)


class Steps:

    def __init__(self, sem, *names):
        self.sem, self.names, self.n = sem, names, len(names)

    def prime(self, ins):
        ins.then_inc(self.sem, self.n)

    def before(self, it, name):
        return it * self.n + self.names.index(name) + 1

    def at(self, it, name):
        return it * self.n + self.n + self.names.index(name) + 1


def wait_apart(eng, sem, value, ready):
    value = eng.snap(value)
    eng.wait_ge(ready, 1)
    eng.wait_ge(sem, value)


def log_decay_to_steps(nc, chain, dd, cum, reset, lw, mid):
    chain.step(nc.vector.tensor_tensor_scan(cum, reset, lw, 0.0, ALU.mult, ALU.add))
    cumc = cum.rearrange("p (c t) -> p c t", t=C)
    middle = cumc[:, :, mid:mid + 1]
    chain.step(nc.vector.tensor_tensor(dd[:, :, 1:C + 1], cumc, middle.to_broadcast([P, NCH, C]), ALU.subtract))
    chain.step(nc.vector.tensor_scalar(dd[:, :, 0:1], middle, -1.0, None, ALU.mult))


def stage_gla(nc, g, w):
    PAIRS, S = GLA_H // 2, 1.0 / 16.0
    with ExitStack() as ctx:
        def sb(name, shape, dt=F32):
            return ctx.enter_context(nc.sbuf_tensor(name, shape, dt))

        def sem(name):
            return ctx.enter_context(nc.semaphore(name))

        win = sb("gla_w", [P, 2, KD, 512])
        wz = sb("gla_wz", [P, KD, 2 * GLA_RANK])
        wdec = sb("gla_wdec", [2 * GLA_RANK, 2, GLA_QK])
        bdec = sb("gla_bdec", [P, 2, PAIRS])
        ng = sb("gla_ng", [P, GLA_H])
        z = sb("gla_z", [2 * GLA_RANK, TOK])
        q = sb("gla_q", [P, PAIRS, TOK])
        k = sb("gla_k", [P, PAIRS, TOK])
        v = sb("gla_v", [P, GLA_H, TOK])
        gate = sb("gla_gate", [P, GLA_H, TOK])
        tmp = sb("gla_tmp", [P, 4, TOK])
        xmin = sb("gla_xmin", [P, 4, TOK])
        reset = sb("gla_reset", [P, TOK])
        dd = sb("gla_dd", [P, 2, PAIRS, NCH, C + 1])
        ends = sb("gla_ends", [P, 2, 2, PAIRS, NCH])
        qs = sb("gla_qs", [P, 2, PAIRS, P])
        ks = sb("gla_ks", [P, 2, PAIRS, P])
        vs = sb("gla_vs", [P, 2, GLA_H, C])
        ktok = sb("gla_ktok", [P, 2, PAIRS, P])
        vtok = sb("gla_vtok", [P, 2, PAIRS, P])
        att = sb("gla_att", [P, 2, PAIRS, P])
        m0 = sb("gla_m0", [P, 2, PAIRS, GLA_DV])
        mraw = sb("gla_mraw", [P, 2, PAIRS, GLA_DV])
        msum = sb("gla_msum", [P, 2, PAIRS, GLA_DV])
        o = g.oT[:, 0:GLA_H, :]

        tiles = [("z", 0)] + [("q", p) for p in range(2)] + [("k", p) for p in range(2)] + \
                [("dec", n) for n in range(4)] + [("v", h) for h in range(4)] + [("g", h) for h in range(4)]
        by_act = [t for t in tiles if t[0] in "qkvg" or t[0] == "dec"]
        by_dve = [t for t in tiles if t[0] in ("z", "dec")]
        s_w = [sem("gla_s_w0"), sem("gla_s_w1")]
        s_small, s_init, s_ps = sem("gla_s_small"), sem("gla_s_init"), sem("gla_s_ps")
        s_eva, s_evd, s_ln = sem("gla_s_eva"), sem("gla_s_evd"), sem("gla_s_ln")
        s_dd, s_ends = sem("gla_s_dd"), sem("gla_s_ends")
        s_st, s_ld, s_zero = sem("gla_s_st"), sem("gla_s_ld"), sem("gla_s_zero")
        s_osq, s_oms, s_ort, s_orms = sem("gla_s_osq"), sem("gla_s_oms"), sem("gla_s_ort"), sem("gla_s_orms")
        PE = Steps(sem("gla_pe"), "ktok", "vtok", "scores", "out", "state")
        DV = Steps(sem("gla_dv"), "ks", "qs", "att", "out_f", "out", "msum", "mraw")
        AC = Steps(sem("gla_ac"), "exp_k", "exp_q", "ktok", "vtok")
        PO = Steps(sem("gla_po"), "m0", "vs")
        loops = ((0, CTX_CH, 0), (CTX_CH, LAT_CH, CTX_CH))

        def evacuated(eng, m):
            name = tiles[m]
            if name in by_act:
                eng.wait_ge(s_eva, by_act.index(name) + 1)
            if name in by_dve:
                eng.wait_ge(s_evd, by_dve.index(name) + 1)

        def slot(m):
            return g.ps[:, 2 * (m % 4):2 * (m % 4) + 2, 0:TOK // 2]

        w_in = w["w_in"][0].rearrange("(k p) n -> p k n", p=P)
        block = ctx.enter_context(nc.Block())

        @block.sync
        def _(sp):
            sp.dma_start(wz[:], w_in[:, :, GLA_COLS - 2 * GLA_RANK:GLA_COLS]).then_inc(s_small, 16)
            for d in range(2):
                sp.dma_start(bdec[:, d, :], w["gla_b_dec"][0, d].rearrange("(p c) -> c p", c=P), allow_slow_non_contiguous=True).then_inc(s_small, 16)
            sp.dma_start(ng[:], w["gla_norm"][0].rearrange("(h c) -> c h", c=P), allow_slow_non_contiguous=True).then_inc(s_small, 16)
            sp.wait_ge(s_zero, 1)
            for d in range(2):
                sp.dma_start(wdec[GLA_RANK * d:GLA_RANK * (d + 1), d, :], w["gla_w_dec"][0, d]).then_inc(s_small, 16)
            for b in range(3):
                if b == 2:
                    sp.wait_ge(s_ps, tiles.index(("k", 1)) + 1)
                sp.dma_start(win[:, b % 2], w_in[:, :, 512 * b:512 * (b + 1)]).then_inc(s_w[b % 2], 16)
            sp.wait_ge(DV.sem, DV.at(CTX_CH - 1, "mraw"))
            for d in range(2):
                for p in range(PAIRS):
                    sp.dma_start(w["new_state_gla"][0, 0, d, 2 * p:2 * p + 2].rearrange("h k v -> (h k) v"),
                                 mraw[:, d, p, :]).then_inc(s_st, 16)
            sp.wait_ge(s_st, 16 * 4)
            for d in range(2):
                for p in range(PAIRS):
                    sp.dma_start(mraw[:, d, p, :],
                                 w["state_gla"][0, 0, d, 2 * p:2 * p + 2].rearrange("h k v -> (h k) v")).then_inc(s_ld, 16)

        @block.tensor
        def _(pe):
            for m, (kind, n) in enumerate(tiles):
                if m >= 4:
                    evacuated(pe, m - 4)
                if (kind, n) == ("z", 0):
                    pe.wait_ge(s_small, 16 * 6)
                if n == 0 and kind in "qvg":
                    b = "qvg".index(kind)
                    pe.wait_ge(s_w[b % 2], 16 * (b // 2 + 1))
                if kind == "dec":
                    if n == 0:
                        evacuated(pe, 0)
                    for half in range(2):
                        last = nc.tensor.matmul(slot(m)[:, half], wdec[:, n // 2, (n % 2) * P:(n % 2 + 1) * P],
                                                z[:, half * 320:half * 320 + 320], start=True, stop=True)
                else:
                    for half in range(2):
                        for kt in range(KD):
                            if kind == "z":
                                lhsT, out = wz[:, kt, :], slot(m)[0:2 * GLA_RANK, half]
                            else:
                                c0 = (n + (2 if kind == "k" else 0)) * P
                                b = {"q": 0, "k": 0, "v": 1, "g": 2}[kind]
                                lhsT, out = win[:, b % 2, kt, c0:c0 + P], slot(m)[:, half]
                            last = nc.tensor.matmul(out, lhsT, g.hT[:, kt, half * 320:half * 320 + 320],
                                                    start=kt == 0, stop=kt == KD - 1)
                last.then_inc(s_ps, 1)
            PE.prime(nc.tensor.nop())
            for m in range(len(tiles) - 4, len(tiles)):
                evacuated(pe, m)
            pe.wait_ge(s_ends, 1)
            for it0, count, _ in loops:
                with pe.Fori(0, count) as i:
                    it = i + it0
                    units = [(d, p) for d in range(2) for p in range(PAIRS)]
                    pe.wait_ge(DV.sem, DV.at(it, "ks"))
                    pe.wait_ge(AC.sem, AC.before(it, "ktok"))
                    for n, (d, p) in enumerate(units):
                        last = nc.tensor.transpose(g.ps[:, 0, n * P:(n + 1) * P], ks[:, d, p], g.blocks[:, 0, :])
                    last.then_inc(PE.sem, 1)
                    pe.wait_ge(PO.sem, PO.at(it, "vs"))
                    pe.wait_ge(AC.sem, AC.before(it, "vtok"))
                    for n, (d, p) in enumerate(units):
                        last = nc.tensor.transpose(g.ps[:, 1, n * P:(n + 1) * P], vs[:, d, 2 * p:2 * p + 2, :],
                                                   g.blocks[:, 0, :])
                    last.then_inc(PE.sem, 1)
                    pe.wait_ge(DV.sem, DV.at(it, "qs"))
                    pe.wait_ge(DV.sem, DV.before(it, "att"))
                    for n, (d, p) in enumerate(units):
                        last = nc.tensor.matmul(g.ps[:, 2, n * P:(n + 1) * P], ks[:, d, p], qs[:, d, p],
                                                start=True, stop=True)
                    last.then_inc(PE.sem, 1)
                    pe.wait_ge(AC.sem, AC.at(it, "vtok"))
                    pe.wait_ge(DV.sem, DV.at(it, "att"))
                    pe.wait_ge(PO.sem, PO.at(it, "m0"))
                    for n, (d, p) in enumerate(units):
                        nc.tensor.matmul(g.ps[:, 3, n * P:(n + 1) * P], vtok[:, d, p], att[:, d, p],
                                         start=True, stop=False)
                        last = nc.tensor.matmul(g.ps[:, 3, n * P:(n + 1) * P], m0[:, d, p], qs[:, d, p],
                                                start=False, stop=True)
                    last.then_inc(PE.sem, 1)
                    pe.wait_ge(AC.sem, AC.at(it, "ktok"))
                    for n, (d, p) in enumerate(units):
                        last = nc.tensor.matmul(g.ps[:, 4, n * P:(n + 1) * P], ktok[:, d, p], vtok[:, d, p],
                                                start=True, stop=True)
                    last.then_inc(PE.sem, 1)
            for h in range(GLA_H):
                pe.wait_ge(s_osq, h + 1)
                if h >= 2:
                    pe.wait_ge(s_oms, h - 1)
                for half in range(2):
                    last = nc.tensor.matmul(g.ps[:, 2 * (h % 2) + half, 0:320], g.ones[:],
                                            tmp[:, h, half * 320:half * 320 + 320], start=True, stop=True)
                last.then_inc(s_orms, 1)

        @block.scalar
        def _(act):
            chain = Chain(act, g.act_steps)
            act.wait_ge(s_small, 16 * 6)
            dests = {"q": q, "k": k, "v": v, "g": gate}
            for m, (kind, n) in enumerate(tiles):
                if kind == "z":
                    continue
                act.wait_ge(s_ps, m + 1)
                src = slot(m)
                if kind == "dec":
                    dst = tmp[:, n, :].rearrange("p (a b) -> p a b", a=2)
                    nc.scalar.activation(dst, src, ACT.Abs, bias=bdec[:, n // 2, n % 2:n % 2 + 1]).then_inc(s_eva, 1)
                    if n == 3:
                        act.wait_ge(s_eva, by_act.index(("dec", 3)) + 1)
                        chain.step(nc.scalar.activation(tmp[:], tmp[:], ACT.Exp, scale=-1.0))
                        nc.scalar.activation(tmp[:], tmp[:], ACT.Ln, bias=1.0).then_inc(s_ln, 1)
                else:
                    dst = dests[kind][:, n, :].rearrange("p (a b) -> p a b", a=2)
                    nc.scalar.activation(dst, src, ACT.Silu if kind == "g" else ACT.Copy,
                                         scale=GLA_DK ** -0.5 if kind == "q" else 1.0).then_inc(s_eva, 1)
            act.wait_ge(s_dd, 1)
            for d in range(2):
                for n in range(2):
                    off, sign = ((0, -1.0), (C, 1.0))[n ^ d]
                    last = nc.scalar.activation(ends[:, d, n], dd[:, d, :, :, off], ACT.Exp, scale=sign * S)
            last.then_inc(s_ends, 1)
            AC.prime(nc.scalar.nop())
            act.wait_ge(s_init, 1)
            for it0, count, c0 in loops:
                with act.Fori(0, count) as i:
                    it = i + it0
                    wait_apart(act, PE.sem, PE.before(it, "out"), s_dd)
                    chunk = (act.snap(i + c0), act.snap(c0 + count - 1 - i))
                    for which, dst, name in ((0, ks, "exp_k"), (1, qs, "exp_q")):
                        for d in range(2):
                            off = (1, 0)[d]
                            sign = (-1.0, 1.0)[which ^ d]
                            for h in range(2):
                                r = slice(64 * h, 64 * h + 64)
                                src = dd[r, d, :, bass.ds(chunk[d], 1), off:off + C]
                                last = nc.scalar.activation(dst[r, d, :, 64 * h:64 * h + 64],
                                                            src.rearrange("p a o t -> p a (o t)"), ACT.Exp,
                                                            scale=sign * S)
                        last.then_inc(AC.sem, 1)
                    act.wait_ge(PE.sem, PE.at(it, "ktok"))
                    nc.scalar.copy(ktok[:].rearrange("p d a b -> p (d a b)"), g.ps[:, 0, :]).then_inc(AC.sem, 1)
                    act.wait_ge(PE.sem, PE.at(it, "vtok"))
                    nc.scalar.copy(vtok[:].rearrange("p d a b -> p (d a b)"), g.ps[:, 1, :]).then_inc(AC.sem, 1)
            act.wait_ge(DV.sem, DV.at(NCH - 1, "out"))
            for h in range(GLA_H):
                nc.scalar.activation(tmp[:, h, :], o[:, h, :], ACT.Square).then_inc(s_osq, 1)
            for h in range(GLA_H):
                act.wait_ge(s_oms, h + 1)
                nc.scalar.activation(tmp[:, h, :], tmp[:, h, :], ACT.Sqrt).then_inc(s_ort, 1)

        @block.gpsimd
        def _(pool):
            chain = Chain(pool, g.pool_steps)
            chain.step(nc.gpsimd.memset(wdec[:], 0.0))
            nc.gpsimd.nop().then_inc(s_zero, 1)
            for t in (qs, ks):
                chain.step(nc.gpsimd.memset(t[:], 0.0))
            chain.step(nc.gpsimd.memset(mraw[:], 0.0))
            chain.step(nc.gpsimd.memset(o, 0.0))
            nc.gpsimd.nop().then_inc(s_init, 1)
            PO.prime(nc.gpsimd.nop())
            pool.wait_ge(s_ends, 1)
            pool.wait_ge(s_eva, len(by_act))
            for it0, count, c0 in loops:
                if it0:
                    pool.wait_ge(s_ld, 64)
                with pool.Fori(0, count) as i:
                    it = i + it0
                    chunk = (pool.snap(i + c0), pool.snap(c0 + count - 1 - i))
                    col = (pool.snap((i + c0) * C), pool.snap((c0 + count - 1 - i) * C))
                    wait_apart(pool, DV.sem, DV.before(it, "mraw"), s_ends)
                    for d in range(2):
                        e = ends[:, d, 0, :, bass.ds(chunk[d], 1)].to_broadcast([P, PAIRS, GLA_DV])
                        last = nc.gpsimd.tensor_tensor(m0[:, d], mraw[:, d], e, ALU.mult)
                    last.then_inc(PO.sem, 1)
                    wait_apart(pool, PE.sem, PE.before(it, "vtok"), s_ends)
                    for d in range(2):
                        last = nc.gpsimd.tensor_copy(vs[:, d], v[:, :, bass.ds(col[d], C)])
                    last.then_inc(PO.sem, 1)

        @block.vector
        def _(dve):
            chain = Chain(dve, g.dve_steps)
            chain.step(nc.vector.memset(reset[:], 1.0))
            chain.step(nc.vector.memset(reset[:].rearrange("p (c t) -> p c t", t=C)[:, :, 0:1], 0.0))
            dve.wait_ge(s_ps, 1)
            nc.vector.tensor_copy(z[:].rearrange("p (a b) -> p a b", a=2),
                                  slot(0)[0:2 * GLA_RANK]).then_inc(s_evd, 1)
            dve.wait_ge(s_small, 16 * 6)
            for n in range(4):
                m = tiles.index(("dec", n))
                dve.wait_ge(s_eva, by_act.index(("dec", n)) + 1)
                nc.vector.tensor_scalar(xmin[:, n].rearrange("p (a b) -> p a b", a=2), slot(m),
                                        bdec[:, n // 2, n % 2:n % 2 + 1], 0.0, ALU.add,
                                        ALU.min).then_inc(s_evd, 1)
            dve.wait_ge(s_evd, 5)
            dve.wait_ge(s_ln, 1)
            for n in range(4):
                chain.step(nc.vector.tensor_tensor(xmin[:, n], xmin[:, n], tmp[:, n, :], ALU.subtract))
                log_decay_to_steps(nc, chain, dd[:, n // 2, n % 2], tmp[:, n, :], reset[:], xmin[:, n], C // 2 - 1)
            nc.vector.nop().then_inc(s_dd, 1)
            DV.prime(nc.vector.nop())
            dve.wait_ge(s_init, 1)
            dve.wait_ge(s_eva, len(by_act))
            for it0, count, c0 in loops:
                with dve.Fori(0, count) as i:
                    it = i + it0
                    chunk = (dve.snap(i + c0), dve.snap(c0 + count - 1 - i))
                    col = (dve.snap((i + c0) * C), dve.snap((c0 + count - 1 - i) * C))
                    for buf, src, name in ((ks, k, "exp_k"), (qs, q, "exp_q")):
                        dve.wait_ge(AC.sem, AC.at(it, name))
                        for d in range(2):
                            for h in range(2):
                                r = slice(64 * h, 64 * h + 64)
                                dst = buf[r, d, :, 64 * h:64 * h + 64]
                                last = nc.vector.tensor_tensor(dst, dst, src[r, :, bass.ds(col[d], C)], ALU.mult)
                        last.then_inc(DV.sem, 1)
                    dve.wait_ge(PE.sem, PE.at(it, "scores"))
                    dve.wait_ge(PE.sem, PE.before(it, "out"))
                    nc.vector.tensor_tensor(att[:], g.ps[:, 2, :].rearrange("p (d a b) -> p d a b", d=2, a=2),
                                            g.tri[:, :, 1:2, :].to_broadcast([P, 2, PAIRS, P]),
                                            ALU.mult).then_inc(DV.sem, 1)
                    dve.wait_ge(PE.sem, PE.at(it, "out"))
                    for d in range(2):
                        dst = o[:, :, bass.ds(col[d], C)]
                        src = g.ps[:, 3, 256 * d:256 * d + 256].rearrange("p (h t) -> p h t", t=C)
                        if d == 1:
                            dve.wait_ge(DV.sem, DV.at(it, "out_f"))
                        nc.vector.tensor_tensor(dst, dst, src, ALU.add).then_inc(DV.sem, 1)
                    dve.wait_ge(PE.sem, PE.at(it, "state"))
                    nc.vector.tensor_tensor(msum[:], m0[:],
                                            g.ps[:, 4, :].rearrange("p (d a b) -> p d a b", d=2, a=2),
                                            ALU.add).then_inc(DV.sem, 1)
                    dve.wait_ge(DV.sem, DV.at(it, "msum"))
                    for d in range(2):
                        e = ends[:, d, 1, :, bass.ds(chunk[d], 1)].to_broadcast([P, PAIRS, GLA_DV])
                        last = nc.vector.tensor_tensor(mraw[:, d], msum[:, d], e, ALU.mult)
                    last.then_inc(DV.sem, 1)
            for h in range(GLA_H):
                dve.wait_ge(s_orms, h + 1)
                nc.vector.tensor_scalar(tmp[:, h, :].rearrange("p (a b) -> p a b", a=2),
                                        g.ps[:, 2 * (h % 2):2 * (h % 2) + 2, 0:320], 1.0 / GLA_DV, EPS,
                                        ALU.mult, ALU.add).then_inc(s_oms, 1)
                dve.wait_ge(s_ort, h + 1)
                chain.step(nc.vector.reciprocal(tmp[:, h, :], tmp[:, h, :]))
                chain.step(nc.vector.tensor_tensor(o[:, h, :], o[:, h, :], tmp[:, h, :], ALU.mult))
                chain.step(nc.vector.scalar_tensor_tensor(o[:, h, :], o[:, h, :], ng[:, h:h + 1], gate[:, h, :],
                                                          ALU.mult, ALU.mult))


def halves(t):
    return t.rearrange("p (a b) -> p a b", a=2)


def stage_rwkv_inputs(nc, g, w, r):
    with ExitStack() as ctx:
        def sb(name, shape, dt=F32):
            return ctx.enter_context(nc.sbuf_tensor(name, shape, dt))

        def sem(name):
            return ctx.enter_context(nc.semaphore(name))

        RCOLS = 3 * RW + 2 * DECAY_RANK + AAA_RANK + GATE_RANK
        ZCOLS = RCOLS - 3 * RW
        tiles = [(n, i, P, b, i * P, b * RW + i * P) for b, n in enumerate("rkv") for i in range(HP)]
        tiles = [("zw", 0, P, 3, 0, 3 * RW), ("za", 0, AAA_RANK, 3, P, 3 * RW + P),
                 ("zg", 0, P, 3, P + AAA_RANK, 3 * RW + P + AAA_RANK)] + tiles
        blocks = [3, 0, 1, 2]
        NPAD = 3
        win = sb("rw_w", [P, 2, KD, 512])
        convrow = sb("rw_convrow", [9, RCOLS])
        conv = sb("rw_conv", [P, len(tiles), 9])
        params = sb("rw_params", [8, RW])
        cpad = sb("rw_cpad", [P, NPAD, CTX + 2])
        lpad = sb("rw_lpad", [P, NPAD, GRID_H + 2, GRID_W + 2])
        zw = sb("rw_zw", [P, TOK])
        za = sb("rw_za", [AAA_RANK, TOK])
        w2 = sb("rw_w2", [P, RW])
        a2 = sb("rw_a2", [AAA_RANK, RW])
        omk = sb("rw_omk", [P, HP])
        reset = sb("rw_reset", [P, TOK])
        sig = sb("rw_sig", [P, 2, TOK])
        cum = sb("rw_cum", [P, TOK])
        a = sb("rw_a", [P, 2, TOK])
        sq = sb("rw_sq", [P, 2, TOK])

        s_w = [sem("rw_s_w0"), sem("rw_s_w1")]
        s_small, s_pad, s_ps, s_ev = sem("rw_s_small"), sem("rw_s_pad"), sem("rw_s_ps"), sem("rw_s_ev")
        s_trow, s_prm, s_conv = sem("rw_s_trow"), sem("rw_s_prm"), sem("rw_s_conv")
        s_z, s_pd, s_sig, s_dd = sem("rw_s_z"), sem("rw_s_pd"), sem("rw_s_sig"), sem("rw_s_dd")
        s_pa, s_a, s_sq, s_pk, s_kk, s_rt = (sem("rw_s_pa"), sem("rw_s_a"), sem("rw_s_sq"), sem("rw_s_pk"),
                                             sem("rw_s_kk"), sem("rw_s_rt"))
        s_kd = sem("rw_s_kd")
        w_in = w["w_in"][0].rearrange("(k p) n -> p k n", p=P)
        dests = {"r": r.r, "k": r.k, "v": r.v}

        def dest(m):
            name, i, width = tiles[m][:3]
            return {"zw": zw[:], "za": za[:], "zg": r.zg[:]}[name] if name[0] == "z" else dests[name][:, i, :]

        def slot(n):
            return g.ps[:, 2 * (n % 4):2 * (n % 4) + 2, 0:TOK // 2]

        block = ctx.enter_context(nc.Block())

        @block.sync
        def _(sp):
            sp.dma_start(convrow[:], w["rwkv_conv"][0].rearrange("a b c -> (a b) c")).then_inc(s_small, 16)
            for n, name in enumerate(("rwkv_a0", "rwkv_k_k", "rwkv_k_a", "rwkv_r_k", "rwkv_ln_g", "rwkv_ln_b")):
                sp.dma_start(params[n:n + 1, :], w[name]).then_inc(s_small, 16)
            sp.dma_start(params[6:8, :], w["rwkv_w0"][0]).then_inc(s_small, 16)
            for n, b in enumerate(blocks):
                if n >= 2:
                    sp.wait_ge(s_ps, 3 if n == 2 else 3 + HP)
                width = ZCOLS if b == 3 else 512
                c0 = GLA_COLS + 512 * b
                sp.dma_start(win[:, n % 2, :, 0:width], w_in[:, :, c0:c0 + width]).then_inc(s_w[n % 2], 16)
                if n == 0:
                    sp.dma_start(w2[:], w["rwkv_w2"][0].rearrange("d r n -> (d r) n")).then_inc(s_small, 16)
                    sp.dma_start(a2[:], w["rwkv_a2"][0]).then_inc(s_small, 16)

        @block.gpsimd
        def _(pool):
            chain = Chain(pool, g.pool_steps)
            chain.step(nc.gpsimd.memset(cpad[:], 0.0))
            chain.step(nc.gpsimd.memset(lpad[:], 0.0))
            nc.gpsimd.nop().then_inc(s_pad, 1)

        @block.tensor
        def _(pe):
            pe.wait_ge(s_small, 16 * 10)
            for m, (_, _, width, _, _, c) in enumerate(tiles):
                nc.tensor.transpose(g.ps[0:width, 6, 9 * m:9 * m + 9], convrow[:, c:c + width], g.blocks[0:9, 0, 0:9])
            for n in range(HP):
                last = nc.tensor.transpose(g.ps[:, 7, 8 * n:8 * n + 8], params[:, n * P:(n + 1) * P],
                                           g.blocks[0:8, 0, 0:8])
            last.then_inc(s_trow, 1)
            for m, (name, i, width, b, c, _) in enumerate(tiles):
                n = blocks.index(b)
                if i == 0:
                    pe.wait_ge(s_w[n % 2], 16 * (n // 2 + 1))
                if m == 3:
                    pe.wait_ge(s_prm, 1)
                if m >= 4:
                    pe.wait_ge(s_ev, m - 3)
                for half in range(2):
                    for kt in range(KD):
                        last = nc.tensor.matmul(slot(m)[0:width, half], win[:, n % 2, kt, c:c + width],
                                                g.hT[:, kt, half * 320:half * 320 + 320],
                                                start=kt == 0, stop=kt == KD - 1)
                last.then_inc(s_ps, 1)
            pe.wait_ge(s_ev, len(tiles))
            pe.wait_ge(s_conv, 2)
            pe.wait_ge(s_z, 1)
            for n in range(2 * HP):
                if n < HP:
                    if n >= 2:
                        pe.wait_ge(s_kd, n - 1)
                    for half in range(2):
                        last = nc.tensor.matmul(slot(n % 2)[:, half], a2[:, n * P:(n + 1) * P],
                                                za[:, half * 320:half * 320 + 320], start=True, stop=True)
                    last.then_inc(s_pa, 1)
                if n >= 2:
                    pe.wait_ge(s_sig, n - 1)
                rows = slice(64 * (n // HP), 64 * (n // HP) + 64)
                for half in range(2):
                    last = nc.tensor.matmul(slot(2 + n % 2)[:, half], w2[rows, (n % HP) * P:(n % HP + 1) * P],
                                            zw[rows, half * 320:half * 320 + 320], start=True, stop=True)
                last.then_inc(s_pd, 1)
                if n < HP:
                    pe.wait_ge(s_sq, n + 1)
                    pe.wait_ge(s_a, n + 1)
                    for half in range(2):
                        last = nc.tensor.matmul(slot(n % 2)[:, half], g.blocks[:, 6, :],
                                                sq[:, n % 2, half * 320:half * 320 + 320], start=True, stop=True)
                    last.then_inc(s_pk, 1)

        @block.scalar
        def _(act):
            act.wait_ge(s_pad, 1)
            for m, (name, i, width, _, _, _) in enumerate(tiles):
                act.wait_ge(s_ps, m + 1)
                if m >= NPAD:
                    act.wait_ge(s_conv, m - NPAD + 1)
                b, s = m % NPAD, slice(0, width)
                nc.scalar.copy(cpad[s, b, 1:CTX + 1], slot(m)[s, 0, 0:CTX])
                nc.scalar.copy(lpad[s, b, 1:4, 1:GRID_W + 1],
                               slot(m)[s, 0, CTX:320].rearrange("p (y x) -> p y x", x=GRID_W))
                nc.scalar.copy(lpad[s, b, 4:9, 1:GRID_W + 1],
                               slot(m)[s, 1].rearrange("p (y x) -> p y x", x=GRID_W)).then_inc(s_ev, 1)
            act.wait_ge(s_conv, 3)
            nc.scalar.activation(zw[:], zw[:], ACT.Tanh).then_inc(s_z, 1)
            nc.scalar.activation(r.zg[:], r.zg[:], ACT.Sigmoid).then_inc(s_z, 1)
            act.wait_ge(s_conv, len(tiles))
            for n in range(2 * HP):
                if n < HP:
                    act.wait_ge(s_pa, n + 1)
                    if n >= 2:
                        act.wait_ge(s_kk, n - 1)
                        act.wait_ge(s_pk, n - 1)
                    nc.scalar.activation(halves(a[:, n % 2]), slot(n % 2), ACT.Sigmoid,
                                         bias=r.prm[:, n, 0:1]).then_inc(s_a, 1)
                    nc.scalar.activation(sq[:, n % 2], r.k[:, n, :], ACT.Square,
                                         scale=r.prm[:, n, 1:2]).then_inc(s_sq, 1)
                act.wait_ge(s_pd, n + 1)
                if n >= 2:
                    act.wait_ge(s_dd, n - 1)
                nc.scalar.activation(halves(sig[:, n % 2]), slot(2 + n % 2), ACT.Sigmoid,
                                     bias=r.prm[:, n % HP, 6 + n // HP:7 + n // HP]).then_inc(s_sig, 1)
                if n < HP:
                    act.wait_ge(s_kd, n + 1)
                    nc.scalar.activation(r.kk[:, n, :], r.kk[:, n, :], ACT.Sqrt).then_inc(s_rt, 1)
            act.wait_ge(s_dd, 2 * HP)
            for d in range(2):
                for n in range(2):
                    off, sign = ((0, -1.0), (C, 1.0))[n ^ d]
                    nc.scalar.activation(r.ends[:, d, n], r.dd[:, d, :, :, off], ACT.Exp, scale=sign * r.S)

        @block.vector
        def _(dve):
            chain = Chain(dve, g.dve_steps)
            chain.step(nc.vector.memset(reset[:], 1.0))
            chain.step(nc.vector.memset(reset[:].rearrange("p (c t) -> p c t", t=C)[:, :, 0:1], 0.0))
            dve.wait_ge(s_trow, 1)
            for m, (_, _, width, _, _, _) in enumerate(tiles):
                last = nc.vector.tensor_copy(conv[0:width, m, :], g.ps[0:width, 6, 9 * m:9 * m + 9])
            chain.step(last)
            chain.step(nc.vector.tensor_copy(r.prm[:], g.ps[:, 7, 0:8 * HP].rearrange("p (a b) -> p a b", b=8)))
            nc.vector.nop().then_inc(s_prm, 1)
            chain.step(nc.vector.tensor_scalar(omk[:], r.prm[:, :, 2], -1.0, 1.0, ALU.mult, ALU.add))
            for m, (_, _, width, _, _, _) in enumerate(tiles):
                dve.wait_ge(s_ev, m + 1)
                s, b = slice(0, width), m % NPAD
                out = dest(m)[s]
                lat = out[:, CTX:TOK].rearrange("p (y x) -> p y x", x=GRID_W)
                for tap in range(9):
                    y, x = tap // 3, tap % 3
                    src, wt = lpad[s, b, y:y + GRID_H, x:x + GRID_W], conv[s, m, tap:tap + 1]
                    if tap == 0:
                        chain.step(nc.vector.tensor_scalar(lat, src, wt, None, ALU.mult))
                    else:
                        chain.step(nc.vector.scalar_tensor_tensor(lat, src, wt, lat, ALU.mult, ALU.add))
                    if y == 1:
                        src = cpad[s, b, x:x + CTX]
                        if x == 0:
                            chain.step(nc.vector.tensor_scalar(out[:, 0:CTX], src, wt, None, ALU.mult))
                        else:
                            chain.step(nc.vector.scalar_tensor_tensor(out[:, 0:CTX], src, wt, out[:, 0:CTX],
                                                                      ALU.mult, ALU.add))
                nc.vector.nop().then_inc(s_conv, 1)
            for n in range(2 * HP):
                if n < HP:
                    dve.wait_ge(s_pk, n + 1)
                    nc.vector.tensor_scalar(halves(r.kk[:, n, :]), slot(n % 2), 1e-24, None,
                                            ALU.max).then_inc(s_kd, 1)
                    dve.wait_ge(s_rt, n + 1)
                    chain.step(nc.vector.reciprocal(r.kk[:, n, :], r.kk[:, n, :]))
                    chain.step(nc.vector.scalar_tensor_tensor(r.kk[:, n, :], r.k[:, n, :], r.prm[:, n, 1:2],
                                                              r.kk[:, n, :], ALU.mult, ALU.mult))
                    dve.wait_ge(s_a, n + 1)
                    chain.step(nc.vector.scalar_tensor_tensor(r.nb[:, n, :], r.kk[:, n, :], -1.0, a[:, n % 2],
                                                              ALU.mult, ALU.mult))
                    chain.step(nc.vector.tensor_scalar(a[:, n % 2], a[:, n % 2], r.prm[:, n, 2:3],
                                                       omk[:, n:n + 1], ALU.mult, ALU.add))
                    nc.vector.tensor_tensor(r.k[:, n, :], r.k[:, n, :], a[:, n % 2], ALU.mult).then_inc(s_kk, 1)
                dve.wait_ge(s_sig, n + 1)
                log_decay_to_steps(nc, chain, r.dd[:, n // HP, n % HP], cum[:], reset[:], sig[:, n % 2], C // 2 - 1)
                nc.vector.nop().then_inc(s_dd, 1)


def stage_rwkv_scan(nc, g, w, r):
    LV = 6
    y = g.oT[:, 4:8, :]
    with ExitStack() as ctx:
        def sb(name, shape, dt=F32):
            return ctx.enter_context(nc.sbuf_tensor(name, shape, dt))

        def sem(name):
            return ctx.enter_context(nc.semaphore(name))

        D2 = range(2)
        big = g.hT[:].rearrange("p a b -> p (a b)")
        lq = [big[:, n * 1024:(n + 1) * 1024].rearrange("p (a b) -> p a b", a=HP) for n in (0, 1)]
        pq = [big[:, n * 1024:(n + 1) * 1024].rearrange("p (a b) -> p a b", a=HP) for n in (2, 3)]
        m0 = [big[:, n * 512:(n + 1) * 512].rearrange("p (a b) -> p a b", a=HP) for n in (8, 9)]
        ex = [sb(f"ex{d}", [P, 3, HP, C]) for d in D2]
        ar = [sb(f"ar{d}", [P, HP, 2, P]) for d in D2]
        bk = [sb(f"bk{d}", [P, HP, 2, P]) for d in D2]
        vs = [sb(f"vs{d}", [P, HP, P]) for d in D2]
        btok = [sb(f"btok{d}", [P, HP, P]) for d in D2]
        ktok = [sb(f"ktok{d}", [P, HP, P]) for d in D2]
        vtok = [sb(f"vtok{d}", [P, HP, P]) for d in D2]
        pa = [sb(f"pa{d}", [P, HP, 2, P]) for d in D2]
        uw = [sb(f"uw{d}", [P, HP, 2, P]) for d in D2]
        G = [sb(f"G{d}", [P, HP, P]) for d in D2]
        T = [sb(f"T{d}", [P, HP, P]) for d in D2]
        TT = [sb(f"TT{d}", [P, HP, P]) for d in D2]
        mraw = [sb(f"mraw{d}", [P, HP, P]) for d in D2]

        levels = [f"{x}{j}" for j in range(LV) for x in ("G", "TT", "T")][:-1]
        PE = [Steps(sem(f"rs_pe{d}"), "lq", "pq", "atok", "btok", "ktok", "vtok", "pv", *levels,
                    "uw", "ry", "psi", "y", "m") for d in D2]
        DV = [Steps(sem(f"rs_dv{d}"), "ar", "bk", "lq", "pq", *[x for x in levels if x[1:] in "012345" and x[0] == "G" or x[:2] == "TT"],
                    "ry", "psi", "y", "m") for d in D2]
        AC = [Steps(sem(f"rs_ac{d}"), "ex", "vs", "atok", "btok", "ktok", "vtok", "pv",
                    *[f"T{j}" for j in range(LV - 1)], "uw") for d in D2]
        PO = [Steps(sem(f"rs_po{d}"), "m0") for d in D2]
        s_init, s_st, s_ld, s_tr, s_sc, s_bk = (sem("rs_init"), sem("rs_st"), sem("rs_ld"), sem("rs_tr"),
                                               sem("rs_sc"), sem("rs_bk"))
        loops = ((0, CTX_CH, 0), (CTX_CH, LAT_CH, CTX_CH))

        def bank(d, n):
            return g.ps[:, 4 * d + n, :].rearrange("p (a b) -> p a b", a=HP)

        def banks(d, n):
            return g.ps[:, 4 * d + n:4 * d + n + 2, :].rearrange("p n (a b) -> p (n a) b", a=2)

        ident = g.blocks[:, 0, :]
        block = ctx.enter_context(nc.Block())

        @block.sync
        def _(sp):
            def heads(t, d):
                return t[0, 0, d].rearrange("(p e) v k -> e v p k", e=2)
            sp.wait_ge(s_sc, 2)
            for d in D2:
                for e in range(2):
                    s = slice(64 * e, 64 * e + 64)
                    sp.dma_start(heads(w["new_state_rwkv"], d)[e], uw[d][s, :, 0, 64 * e:64 * e + 64]).then_inc(s_st, 16)
            sp.wait_ge(s_st, 64)
            for d in D2:
                for e in range(2):
                    s = slice(64 * e, 64 * e + 64)
                    sp.dma_start(uw[d][s, :, 0, 64 * e:64 * e + 64], heads(w["state_rwkv"], d)[e]).then_inc(s_ld, 16)

        @block.gpsimd
        def _(pool):
            chain = Chain(pool, g.pool_steps)
            for d in D2:
                for t in (ar[d], bk[d], vs[d], mraw[d]):
                    chain.step(nc.gpsimd.memset(t[:], 0.0))
            chain.step(nc.gpsimd.memset(y, 0.0))
            nc.gpsimd.nop().then_inc(s_init, 1)
            for d in D2:
                PO[d].prime(nc.gpsimd.nop())
            for it0, count, c0 in loops:
                if it0:
                    pool.wait_ge(s_bk, 2)
                with pool.Fori(0, count) as i:
                    it = i + it0
                    chunk = (pool.snap(i + c0), pool.snap(c0 + count - 1 - i))
                    for d in D2:
                        wait_apart(pool, DV[d].sem, DV[d].before(it, "m"), s_init)
                        wait_apart(pool, PE[d].sem, PE[d].before(it, "m"), s_init)
                        e = r.ends[:, d, 0, :, bass.ds(chunk[d], 1)].to_broadcast([P, HP, P])
                        nc.gpsimd.tensor_tensor(m0[d], mraw[d][:], e, ALU.mult).then_inc(PO[d].sem, 1)

        @block.scalar
        def _(act):
            for d in D2:
                AC[d].prime(nc.scalar.nop())
            act.wait_ge(s_init, 1)
            for it0, count, c0 in loops:
                with act.Fori(0, count) as i:
                    it = i + it0
                    chunk = (act.snap(i + c0), act.snap(c0 + count - 1 - i))
                    for d in D2:
                        wait_apart(act, DV[d].sem, DV[d].before(it, "bk"), s_init)
                        excl, incl, sign = ((0, 1, 1.0), (1, 0, -1.0))[d]
                        for n, (off, sg) in enumerate(((excl, sign), (incl, sign), (incl, -sign))):
                            src = r.dd[:, d, :, bass.ds(chunk[d], 1), off:off + C]
                            last = nc.scalar.activation(ex[d][:, n], src.rearrange("p a o t -> p a (o t)"),
                                                        ACT.Exp, scale=sg * r.S)
                        last.then_inc(AC[d].sem, 1)
                    for d in D2:
                        wait_apart(act, PE[d].sem, PE[d].before(it, "vtok"), s_init)
                        col = act.snap(chunk[d] * C)
                        for h in range(2):
                            s = slice(64 * h, 64 * h + 64)
                            last = nc.scalar.copy(vs[d][s, :, 64 * h:64 * h + 64], r.v[s, :, bass.ds(col, C)])
                        last.then_inc(AC[d].sem, 1)
                    for name, dst, n in (("atok", lambda d: pa[d][:, :, 1, :], 0), ("btok", lambda d: btok[d][:], 1),
                                         ("ktok", lambda d: ktok[d][:], 2), ("vtok", lambda d: vtok[d][:], 3),
                                         ("pv", lambda d: pa[d][:, :, 0, :], 0)):
                        for d in D2:
                            act.wait_ge(PE[d].sem, PE[d].at(it, name))
                            nc.scalar.copy(dst(d), bank(d, n)).then_inc(AC[d].sem, 1)
                    for j in range(LV - 1):
                        for d in D2:
                            act.wait_ge(PE[d].sem, PE[d].at(it, f"T{j}"))
                            nc.scalar.copy(T[d][:], bank(d, 3)).then_inc(AC[d].sem, 1)
                    for d in D2:
                        act.wait_ge(PE[d].sem, PE[d].at(it, "uw"))
                        nc.scalar.copy(uw[d][:].rearrange("p a x b -> p a (x b)"), banks(d, 0)).then_inc(AC[d].sem, 1)
                if it0 == 0:
                    for d in D2:
                        act.wait_ge(s_tr, d + 1)
                        nc.scalar.copy(uw[d][:, :, 0, :], bank(d, 0)).then_inc(s_sc, 1)
                    for d in D2:
                        act.wait_ge(s_tr, d + 3)
                        nc.scalar.copy(mraw[d][:], bank(d, 0)).then_inc(s_bk, 1)

        @block.vector
        def _(dve):
            for d in D2:
                DV[d].prime(nc.vector.nop())
            dve.wait_ge(s_init, 1)
            for it0, count, c0 in loops:
                with dve.Fori(0, count) as i:
                    it = i + it0
                    chunk = (dve.snap(i + c0), dve.snap(c0 + count - 1 - i))
                    col = [dve.snap(chunk[d] * C) for d in D2]
                    for name, out, items in (("ar", ar, ((0, r.kk), (1, r.r))), ("bk", bk, ((2, r.nb), (2, r.k)))):
                        for d in D2:
                            wait_apart(dve, AC[d].sem, AC[d].at(it, "ex"), s_init)
                            dve.wait_ge(PE[d].sem, PE[d].before(it, "ktok"))
                            for x, (n, src) in enumerate(items):
                                for h in range(2):
                                    s = slice(64 * h, 64 * h + 64)
                                    last = nc.vector.tensor_tensor(out[d][s, :, x, 64 * h:64 * h + 64], ex[d][s, n],
                                                                   src[s, :, bass.ds(col[d], C)], ALU.mult)
                            last.then_inc(DV[d].sem, 1)
                    for name, dst, n in (("lq", lq, 0), ("pq", pq, 2)):
                        for d in D2:
                            dve.wait_ge(PE[d].sem, PE[d].at(it, name))
                            mask = g.tri[:, d, :, :].rearrange("p x b -> p (x b)").unsqueeze(1)
                            nc.vector.tensor_tensor(dst[d], banks(d, n), mask.to_broadcast([P, HP, 2 * P]),
                                                    ALU.mult).then_inc(DV[d].sem, 1)
                    for j in range(LV):
                        for d in D2:
                            dve.wait_ge(PE[d].sem, PE[d].at(it, f"G{j}"))
                            nc.vector.tensor_tensor(G[d][:], bank(d, 1),
                                                    g.levels[:, j:j + 1, :].to_broadcast([P, HP, P]),
                                                    ALU.mult).then_inc(DV[d].sem, 1)
                        for d in D2:
                            dve.wait_ge(PE[d].sem, PE[d].at(it, f"TT{j}"))
                            old = ident.unsqueeze(1).to_broadcast([P, HP, P]) if j == 0 else TT[d][:]
                            nc.vector.tensor_tensor(TT[d][:], bank(d, 2), old, ALU.add).then_inc(DV[d].sem, 1)
                    for d in D2:
                        dve.wait_ge(PE[d].sem, PE[d].at(it, "ry"))
                        nc.vector.tensor_tensor(T[d][:], bank(d, 2), ar[d][:, :, 1, :], ALU.add).then_inc(DV[d].sem, 1)
                    for d in D2:
                        dve.wait_ge(PE[d].sem, PE[d].at(it, "psi"))
                        nc.vector.tensor_tensor(G[d][:], bank(d, 3), ident.unsqueeze(1).to_broadcast([P, HP, P]),
                                                ALU.add).then_inc(DV[d].sem, 1)
                    for d in D2:
                        dve.wait_ge(PE[d].sem, PE[d].at(it, "y"))
                        if d == 1:
                            dve.wait_ge(DV[0].sem, DV[0].at(it, "y"))
                        for h in range(2):
                            s = slice(64 * h, 64 * h + 64)
                            dst = y[s, :, bass.ds(col[d], C)]
                            last = nc.vector.tensor_tensor(dst, dst, bank(d, 0)[s, :, 64 * h:64 * h + 64], ALU.add)
                        last.then_inc(DV[d].sem, 1)
                    for d in D2:
                        dve.wait_ge(PE[d].sem, PE[d].at(it, "m"))
                        e = r.ends[:, d, 1, :, bass.ds(chunk[d], 1)].to_broadcast([P, HP, P])
                        nc.vector.tensor_tensor(mraw[d][:], bank(d, 1), e, ALU.mult).then_inc(DV[d].sem, 1)

        @block.tensor
        def _(pe):
            for d in D2:
                PE[d].prime(nc.tensor.nop())
            pe.wait_ge(s_init, 1)

            def each(name, it, d, out, lhsT, rhs, waits, first=True, last=True, transpose=False):
                for sm, value in waits:
                    pe.wait_ge(sm, value)
                for p in range(HP):
                    if transpose:
                        ins = nc.tensor.transpose(out[:, p], lhsT(p), ident)
                    else:
                        ins = nc.tensor.matmul(out[:, p], lhsT(p), rhs(p), start=True, stop=True)
                ins.then_inc(PE[d].sem, 1)

            for it0, count, c0 in loops:
                with pe.Fori(0, count) as i:
                    it = i + it0

                    def dv(d, name):
                        return DV[d].sem, DV[d].at(it, name)

                    def ac(d, name):
                        return AC[d].sem, AC[d].at(it, name)

                    for d in D2:
                        each("lq", it, d, banks(d, 0), lambda p: bk[d][:, p, 0, :],
                             lambda p: ar[d][:, p].rearrange("p x b -> p (x b)"),
                             [dv(d, "bk")])
                    for d in D2:
                        each("pq", it, d, banks(d, 2), lambda p: bk[d][:, p, 1, :],
                             lambda p: ar[d][:, p].rearrange("p x b -> p (x b)"),
                             [])
                    for name, n, src, waits in (
                            ("atok", 0, lambda d, p: ar[d][:, p, 0, :], lambda d: [dv(d, "lq")]),
                            ("btok", 1, lambda d, p: bk[d][:, p, 0, :], lambda d: []),
                            ("ktok", 2, lambda d, p: bk[d][:, p, 1, :], lambda d: [dv(d, "pq")]),
                            ("vtok", 3, lambda d, p: vs[d][:, p, :], lambda d: [ac(d, "vs")])):
                        for d in D2:
                            each(name, it, d, bank(d, n), lambda p: src(d, p), None, waits(d), transpose=True)
                    for d in D2:
                        each("pv", it, d, bank(d, 0), lambda p: pq[d][:, p, 0:P], lambda p: vtok[d][:, p],
                             [ac(d, "vtok")])
                    for j in range(LV):
                        for d in D2:
                            if j == 0:
                                each("G0", it, d, bank(d, 1), lambda p: lq[d][:, p, 0:P], None, [], transpose=True)
                            else:
                                each(f"G{j}", it, d, bank(d, 1), lambda p: lq[d][:, p, 0:P], lambda p: T[d][:, p],
                                     [ac(d, f"T{j - 1}")])
                        for d in D2:
                            if j == 0:
                                each("TT0", it, d, bank(d, 2), lambda p: G[d][:, p], None, [dv(d, "G0")],
                                     transpose=True)
                            else:
                                each(f"TT{j}", it, d, bank(d, 2), lambda p: G[d][:, p], lambda p: TT[d][:, p],
                                     [dv(d, f"G{j}")])
                        if j < LV - 1:
                            for d in D2:
                                each(f"T{j}", it, d, bank(d, 3), lambda p: TT[d][:, p], None, [dv(d, f"TT{j}")],
                                     transpose=True)
                    for d in D2:
                        each("uw", it, d, banks(d, 0), lambda p: TT[d][:, p],
                             lambda p: pa[d][:, p].rearrange("p x b -> p (x b)"),
                             [dv(d, f"TT{LV - 1}"), ac(d, "pv")])
                    for d in D2:
                        each("ry", it, d, bank(d, 2), lambda p: uw[d][:, p, 1, :], lambda p: lq[d][:, p, P:2 * P],
                             [ac(d, "uw")])
                    for d in D2:
                        each("psi", it, d, bank(d, 3), lambda p: uw[d][:, p, 1, :], lambda p: btok[d][:, p], [])
                    for d in D2:
                        pe.wait_ge(*dv(d, "ry"))
                        pe.wait_ge(PO[d].sem, PO[d].at(it, "m0"))
                        for p in range(HP):
                            out = bank(d, 0)[:, p]
                            nc.tensor.matmul(out, vtok[d][:, p], pq[d][:, p, P:2 * P], start=True, stop=False)
                            nc.tensor.matmul(out, uw[d][:, p, 0, :], lq[d][:, p, P:2 * P], start=False, stop=False)
                            ins = nc.tensor.matmul(out, m0[d][:, p], T[d][:, p], start=False, stop=True)
                        ins.then_inc(PE[d].sem, 1)
                    for d in D2:
                        pe.wait_ge(*dv(d, "psi"))
                        for p in range(HP):
                            out = bank(d, 1)[:, p]
                            nc.tensor.matmul(out, ktok[d][:, p], vtok[d][:, p], start=True, stop=False)
                            nc.tensor.matmul(out, btok[d][:, p], uw[d][:, p, 0, :], start=False, stop=False)
                            ins = nc.tensor.matmul(out, G[d][:, p], m0[d][:, p], start=False, stop=True)
                        ins.then_inc(PE[d].sem, 1)
                if it0 == 0:
                    for d in D2:
                        pe.wait_ge(DV[d].sem, DV[d].at(CTX_CH - 1, "m"))
                        for p in range(HP):
                            ins = nc.tensor.transpose(bank(d, 0)[:, p], mraw[d][:, p], ident)
                        ins.then_inc(s_tr, 1)
                    pe.wait_ge(s_ld, 64)
                    for d in D2:
                        for p in range(HP):
                            ins = nc.tensor.transpose(bank(d, 0)[:, p], uw[d][:, p, 0, :], ident)
                        ins.then_inc(s_tr, 1)


def stage_rwkv_output(nc, g, w, r):
    y = g.oT[:, 4:8, :]
    with ExitStack() as ctx:
        def sb(name, shape, dt=F32):
            return ctx.enter_context(nc.sbuf_tensor(name, shape, dt))

        def sem(name):
            return ctx.enter_context(nc.semaphore(name))

        g2 = sb("ro_g2", [P, RW])
        sq = sb("ro_sq", [P, 2, TOK])
        rk = sb("ro_rk", [P, 2, TOK])
        std = sb("ro_std", [P, 2, TOK])
        s_g2, s_mean, s_ctr, s_sq, s_var, s_vd, s_rt = (sem("ro_g2"), sem("ro_mean"), sem("ro_ctr"), sem("ro_sq_"),
                                                       sem("ro_var"), sem("ro_vd"), sem("ro_rt"))
        s_rk, s_bon, s_done = sem("ro_rk_"), sem("ro_bon"), sem("ro_done")

        def slot(n):
            return g.ps[:, 2 * n:2 * n + 2, 0:TOK // 2]
        MEAN, VAR, BONUS, GATE = range(4)
        block = ctx.enter_context(nc.Block())

        @block.sync
        def _(sp):
            sp.dma_start(g2[:], w["rwkv_g2"][0]).then_inc(s_g2, 16)

        @block.tensor
        def _(pe):
            def over_heads(n, src, s_out):
                for half in range(2):
                    last = nc.tensor.matmul(slot(n)[:, half], g.blocks[:, 6, :], src[:, half * 320:half * 320 + 320],
                                            start=True, stop=True)
                last.then_inc(s_out, 1)

            pe.wait_ge(s_g2, 16)
            for n in range(HP):
                if n:
                    pe.wait_ge(s_done, n)
                over_heads(MEAN, y[:, n, :], s_mean)
                pe.wait_ge(s_sq, n + 1)
                over_heads(VAR, sq[:, n % 2], s_var)
                pe.wait_ge(s_rk, n + 1)
                for half in range(2):
                    nc.tensor.matmul(slot(GATE)[:, half], g2[:, n * P:(n + 1) * P],
                                     r.zg[:, half * 320:half * 320 + 320], start=True, stop=True)
                over_heads(BONUS, rk[:, n % 2], s_bon)

        @block.scalar
        def _(act):
            for n in range(HP):
                act.wait_ge(s_ctr, n + 1)
                nc.scalar.activation(sq[:, n % 2], y[:, n, :], ACT.Square).then_inc(s_sq, 1)
                act.wait_ge(s_vd, n + 1)
                nc.scalar.activation(std[:, n % 2], std[:, n % 2], ACT.Sqrt).then_inc(s_rt, 1)

        @block.vector
        def _(dve):
            chain = Chain(dve, g.dve_steps)
            for n in range(HP):
                yn, b = y[:, n, :], n % 2
                chain.step(nc.vector.scalar_tensor_tensor(rk[:, b], r.r[:, n, :], r.prm[:, n, 3:4], r.k[:, n, :],
                                                          ALU.mult, ALU.mult))
                nc.vector.nop().then_inc(s_rk, 1)
                dve.wait_ge(s_mean, n + 1)
                nc.vector.scalar_tensor_tensor(halves(yn), slot(MEAN), -1.0 / RN, halves(yn), ALU.mult,
                                               ALU.add).then_inc(s_ctr, 1)
                dve.wait_ge(s_var, n + 1)
                nc.vector.tensor_scalar(halves(std[:, b]), slot(VAR), 1.0 / RN, RWKV_LN_EPS, ALU.mult,
                                        ALU.add).then_inc(s_vd, 1)
                dve.wait_ge(s_rt, n + 1)
                chain.step(nc.vector.reciprocal(std[:, b], std[:, b]))
                chain.step(nc.vector.tensor_tensor(yn, yn, std[:, b], ALU.mult))
                chain.step(nc.vector.tensor_scalar(yn, yn, r.prm[:, n, 4:5], r.prm[:, n, 5:6], ALU.mult, ALU.add))
                dve.wait_ge(s_bon, n + 1)
                chain.step(nc.vector.tensor_tensor(halves(r.v[:, n, :]), halves(r.v[:, n, :]), slot(BONUS), ALU.mult))
                chain.step(nc.vector.tensor_tensor(yn, yn, r.v[:, n, :], ALU.add))
                nc.vector.tensor_tensor(halves(yn), halves(yn), slot(GATE), ALU.mult).then_inc(s_done, 1)
                dve.wait_ge(s_done, n + 1)


def stage_rwkv(nc, g, w):
    with ExitStack() as ctx:
        def sb(name, shape, dt=F32):
            return ctx.enter_context(nc.sbuf_tensor(name, shape, dt))
        r = Shared()
        r.S = -math.exp(-0.5)
        r.r, r.k, r.v = sb("r_r", [P, HP, TOK]), sb("r_k", [P, HP, TOK]), sb("r_v", [P, HP, TOK])
        r.kk, r.nb = sb("r_kk", [P, HP, TOK]), sb("r_nb", [P, HP, TOK])
        r.dd = sb("r_dd", [P, 2, HP, NCH, C + 1])
        r.ends = sb("r_ends", [P, 2, 2, HP, NCH])
        r.zg = sb("r_zg", [P, TOK])
        r.prm = sb("r_prm", [P, HP, 8])
        stage_rwkv_inputs(nc, g, w, r)
        stage_rwkv_scan(nc, g, w, r)
        stage_rwkv_output(nc, g, w, r)


BLK = P
MORE = (TOK * TOP_K) // (BLK + 1)
MORE += MORE % 2
NBLK = NE + MORE + 2
ROWS = TOK * TOP_K
U_MAIN, U_MORE = 4, 2


def stage_project_and_route(nc, g, w, m):
    with ExitStack() as ctx:
        def sb(name, shape, dt=F32):
            return ctx.enter_context(nc.sbuf_tensor(name, shape, dt))

        def sem(name):
            return ctx.enter_context(nc.semaphore(name))

        wout = sb("pr_wout", [P, KD, D])
        mod = sb("pr_mod", [P, 3, 2, D])
        w13 = sb("pr_w13", [P, KD, 2, FF])
        w2 = sb("pr_w2", [P, 2, D])
        wr = sb("pr_wr", [P, KD, NE])
        br = sb("pr_br", [P, NE])
        tmp = sb("pr_tmp", [P, 2, D])
        h2 = sb("pr_h2", [P, 2, D])
        ss, rms, rstd = sb("pr_ss", [P, NT]), sb("pr_rms", [P, NT]), sb("pr_rstd", [P, NT])
        s1 = sb("pr_s1", [P, 2, 2, FF])
        act1 = sb("pr_act1", [P, 2, FF])
        aT = sb("pr_aT", [P, 2, 2, P])
        scores, sel, selm = (sb("pr_scores", [P, NT, NE]), sb("pr_sel", [P, NT, NE]), sb("pr_selm", [P, NT, NE]))
        top = sb("pr_top", [P, NT, NG, 8])
        gs, gv, gif = sb("pr_gs", [P, NT, NG]), sb("pr_gv", [P, NT, 8]), sb("pr_gif", [P, NT, 8])
        gi, ti = sb("pr_gi", [P, NT, 8], U32), sb("pr_ti", [P, NT, 8], U32)
        geq, gmask = sb("pr_geq", [P, NT, NG]), sb("pr_gmask", [P, NT, NG])
        tv, tif = sb("pr_tv", [P, NT, 8]), sb("pr_tif", [P, NT, 8])
        room = [wout[:].rearrange("p k d -> p (k d)")[:, n * TOP_K * NT * NE:(n + 1) * TOP_K * NT * NE]
                for n in range(3)]
        eq, pick = (v.rearrange("p (k c) -> p k c", k=TOP_K) for v in room[:2])
        emore = room[2][:, 0:MORE * NE].rearrange("p (o e) -> p o e", e=NE)
        M = sb("pr_M", [P, NT, NE])
        wsum = sb("pr_wsum", [P, NT])
        iotai, iota = sb("pr_iotai", [P, NE], I32), sb("pr_iota", [P, NE])
        iotam = sb("pr_iotam", [P, MORE])
        before = sb("pr_before", [P, P])
        rowid = sb("pr_rowid", [P, TOP_K, NT], I32)
        empty = sb("pr_empty", [P, NBLK], I32)
        rank, q, blk, inblk = (sb("pr_rank", [P, NT, NE]), sb("pr_q", [P, NT, NE]), sb("pr_blk", [P, NT, NE]),
                               sb("pr_inblk", [P, NT, NE]))
        cnt, more, upto = sb("pr_cnt", [P, NE]), sb("pr_more", [P, NE]), sb("pr_upto", [P, NE])
        eblk = sb("pr_eblk", [P, NE])
        trow, trowi = sb("pr_trow", [P, TOP_K, NT]), sb("pr_trowi", [P, TOP_K, NT], U32)
        emf, nmf = sb("pr_emf", [P, MORE]), sb("pr_nmf", [P, 1])

        s_wout, s_x, s_mod, s_sh, s_rt, s_const = (sem("pr_s_wout"), sem("pr_s_x"), sem("pr_s_mod"), sem("pr_s_sh"),
                                                   sem("pr_s_rt"), sem("pr_s_const"))
        s_o, s_x1, s_sq, s_ms, s_sqrt, s_h2, s_h2st = (sem("pr_s_o"), sem("pr_s_x1"), sem("pr_s_sq"), sem("pr_s_ms"),
                                                       sem("pr_s_sqrt"), sem("pr_s_h2"), [sem("pr_s_h2st0"), sem("pr_s_h2st1")])
        s_tr, s_h2T, s_log, s_sc = sem("pr_s_tr"), sem("pr_s_h2T"), sem("pr_s_log"), sem("pr_s_sc")
        s_h13, s_silu, s_mul, s_at, s_aT, s_y, s_ysh = (sem("pr_s_h13"), sem("pr_s_silu"), sem("pr_s_mul"),
                                                        sem("pr_s_at"), sem("pr_s_aT"), sem("pr_s_y"), sem("pr_s_ysh"))
        s_M, s_rank, s_rows, s_zero, s_tab, s_back = (sem("pr_s_M"), sem("pr_s_rank"), sem("pr_s_rows"),
                                                      sem("pr_s_zero"), sem("pr_s_tab"), sem("pr_s_back"))
        h2T, ysh = g.hT, g.oT[:].rearrange("p a b -> p (a b)").rearrange("p (t d) -> p t d", d=D)
        block = ctx.enter_context(nc.Block())

        @block.sync
        def _(sp):
            sp.dma_start(wout[:, :, 0:512],
                         w["w_out"][0, :, 0:512].rearrange("(k p) n -> p k n", p=P)).then_inc(s_wout, 16)
            sp.dma_start(wout[:, :, 512:D],
                         w["w_out"][0, :, 512:D].rearrange("(k p) n -> p k n", p=P)).then_inc(s_wout, 16)
            sp.dma_start(m.x[:, 0, :], w["x_prompt"][0]).then_inc(s_x, 16)
            sp.dma_start(m.x[:, 1:NT, :], w["x_sample"][0].rearrange("(t p) d -> p t d", p=P)).then_inc(s_x, 16)
            for n, part in enumerate((2, 3, 4)):
                for s in range(2):
                    sp.dma_start(mod[:, n, s], g.mod_dram[s:s + 1, part * D:(part + 1) * D].to_broadcast([P, D])
                                 ).then_inc(s_mod, 16)
            sp.dma_start(wr[:], w["router_w"][0].rearrange("(p k) e -> p k e", k=KD)).then_inc(s_rt, 16)
            sp.dma_start(br[:], w["router_b"].to_broadcast([P, NE])).then_inc(s_rt, 16)
            sp.dma_start(w13[:, :, 0, :], w["sh_w1"][0].rearrange("(p k) f -> p k f", k=KD)).then_inc(s_sh, 16)
            sp.dma_start(w13[:, :, 1, :], w["sh_w3"][0].rearrange("(p k) f -> p k f", k=KD)).then_inc(s_sh, 16)
            sp.dma_start(w2[:], w["sh_w2"][0].rearrange("(p j) d -> p j d", j=2)).then_inc(s_sh, 16)
            for t in range(NT):
                sp.wait_ge(s_h2, t + 1)
                sp.dma_start(m.h_dram[t * P:(t + 1) * P, :], h2[:, t % 2]).then_inc(s_h2st[t % 2], 16)
            for b in range(2):
                sp.wait_ge(s_h2st[b], 16 * ((NT + 1 - b) // 2))
            sp.wait_ge(s_tab, 16 * TOP_K * NT)
            sp.dma_start(m.rows[:], m.tab_dram.rearrange("(p b) o -> p (b o)", p=P)).then_inc(s_back, 16)

        @block.gpsimd
        def _(pool):
            chain = Chain(pool, g.pool_steps)
            chain.step(nc.gpsimd.memset(empty[:], ROWS + TOP_K - 1))
            pool.dma_start(m.tab_dram.rearrange("(p b) o -> p (b o)", p=P), empty[:]).then_inc(s_zero, 16)
            chain.step(nc.gpsimd.iota(iotai[:], pattern=[[1, NE]], base=0, channel_multiplier=0))
            chain.step(nc.gpsimd.iota(rowid[:], pattern=[[1, TOP_K], [P * TOP_K, NT]], base=0,
                                      channel_multiplier=TOP_K))
            chain.step(nc.gpsimd.affine_select(out=before[:], in_=g.ones[:], compare_op=ALU.is_ge, fill=0.0,
                                               base=-1, pattern=[[1, P]], channel_multiplier=-1))
            nc.gpsimd.nop().then_inc(s_const, 1)
            for t in range(NT):
                pool.wait_ge(s_silu, t + 1)
                if t >= 2:
                    pool.wait_ge(s_at, t - 1)
                def split(v):
                    return v.rearrange("p (a j) -> p a j", j=2)
                nc.gpsimd.tensor_tensor(act1[:, t % 2].rearrange("p (j a) -> p a j", j=2), split(s1[:, t % 2, 0]),
                                        split(s1[:, t % 2, 1]), ALU.mult).then_inc(s_mul, 1)
            pool.wait_ge(s_zero, 16)
            pool.wait_ge(s_rows, 1)
            for k in range(TOP_K):
                for t in range(NT):
                    nc.gpsimd.indirect_dma_start(
                        out=m.tab_dram, out_offset=bass.IndirectOffsetOnAxis(ap=trowi[:, k, t:t + 1], axis=0),
                        in_=rowid[:, k, t:t + 1], in_offset=None).then_inc(s_tab, 16)

        @block.tensor
        def _(pe):
            for t in range(NT):
                if t >= 2:
                    pe.wait_ge(s_x1, t - 1)
                for n in range(2):
                    if t == 0:
                        pe.wait_ge(s_wout, 32)
                    for k in range(KD):
                        last = nc.tensor.matmul(g.ps[:, 2 * (t % 2) + n, :], g.oT[:, k, t * P:(t + 1) * P],
                                                wout[:, k, n * 512:(n + 1) * 512], start=k == 0, stop=k == KD - 1)
                last.then_inc(s_o, 1)
            for t in range(NT):
                pe.wait_ge(s_h2, t + 1)
                if t >= 1:
                    pe.wait_ge(s_h2T, t)
                for k in range(KD):
                    last = nc.tensor.transpose(g.ps[:, 4 + k // 4, (k % 4) * P:(k % 4 + 1) * P],
                                               h2[:, t % 2, k * P:(k + 1) * P], g.blocks[:, 0, :])
                last.then_inc(s_tr, 1)
            pe.wait_ge(s_h2T, NT)
            pe.wait_ge(s_rt, 32)
            for t in range(NT):
                for k in range(KD):
                    last = nc.tensor.matmul(g.ps[:, 6, t * NE:(t + 1) * NE], h2T[:, k, t * P:(t + 1) * P],
                                            wr[:, k, :], start=k == 0, stop=k == KD - 1)
            last.then_inc(s_log, 1)
            pe.wait_ge(s_sh, 48)
            for t in range(NT):
                if t >= 1:
                    pe.wait_ge(s_silu, t)
                for k in range(KD):
                    last = nc.tensor.matmul(g.ps[:, 7, :], h2T[:, k, t * P:(t + 1) * P],
                                            w13[:, k].rearrange("p a f -> p (a f)"), start=k == 0, stop=k == KD - 1)
                last.then_inc(s_h13, 1)
                if t == 2:
                    pe.wait_ge(s_M, 1)
                    for u in range(NT + 1):
                        out = g.ps[:, 5, u * NE:(u + 1) * NE]
                        for v in range(min(u, NT - 1) + 1):
                            last = nc.tensor.matmul(out, before[:] if v == u else g.ones[:], M[:, v, :],
                                                    start=v == 0, stop=v == min(u, NT - 1))
                    last.then_inc(s_rank, 1)
                pe.wait_ge(s_mul, t + 1)
                pe.wait_ge(s_aT, t)
                if t == 0:
                    pe.wait_ge(s_sc, 1)
                for j in range(2):
                    last = nc.tensor.transpose(g.ps[:, 4, j * P:(j + 1) * P], act1[:, t % 2, j * P:(j + 1) * P],
                                               g.blocks[:, 0, :])
                last.then_inc(s_at, 1)
                pe.wait_ge(s_aT, t + 1)
                if t == 0:
                    pe.wait_ge(s_x1, NT)
                if t >= 2:
                    pe.wait_ge(s_ysh, t - 1)
                for n in range(2):
                    for j in range(2):
                        last = nc.tensor.matmul(g.ps[:, 2 * (t % 2) + n, :], aT[:, t % 2, j],
                                                w2[:, j, n * 512:(n + 1) * 512], start=j == 0, stop=j == 1)
                last.then_inc(s_y, 1)

        @block.scalar
        def _(act):
            for t in range(NT):
                act.wait_ge(s_x1, t + 1)
                if t:
                    act.wait_ge(s_sq, t)
                nc.scalar.activation(s1[:].rearrange("p a b f -> p (a b f)"), m.x[:, t, :], ACT.Square,
                                     accum_out=ss[:, t:t + 1]).then_inc(s_sq, 1)
            act.wait_ge(s_ms, 1)
            nc.scalar.activation(rms[:], rms[:], ACT.Sqrt).then_inc(s_sqrt, 1)
            for t in range(NT):
                act.wait_ge(s_tr, t + 1)
                nc.scalar.copy(h2T[:, :, t * P:(t + 1) * P],
                               g.ps[:, 4:6, :].rearrange("p a (b c) -> p (a b) c", b=4)).then_inc(s_h2T, 1)
            act.wait_ge(s_log, 1)
            nc.scalar.activation(scores[:].rearrange("p t e -> p (t e)"), g.ps[:, 6, 0:NT * NE],
                                 ACT.Sigmoid).then_inc(s_sc, 1)
            for t in range(NT):
                act.wait_ge(s_h13, t + 1)
                if t >= 2:
                    act.wait_ge(s_mul, t - 1)
                nc.scalar.activation(s1[:, t % 2, 0], g.ps[:, 7, 0:FF], ACT.Silu)
                nc.scalar.copy(s1[:, t % 2, 1], g.ps[:, 7, FF:2 * FF]).then_inc(s_silu, 1)
                act.wait_ge(s_at, t + 1)
                if t >= 2:
                    act.wait_ge(s_y, t - 1)
                nc.scalar.copy(aT[:, t % 2].rearrange("p j a -> p (j a)"), g.ps[:, 4, 0:2 * P]).then_inc(s_aT, 1)
                act.wait_ge(s_y, t + 1)
                nc.scalar.copy(ysh[:, t, :], g.ps[:, 2 * (t % 2):2 * (t % 2) + 2, :]
                               .rearrange("p a b -> p (a b)")).then_inc(s_ysh, 1)

        @block.vector
        def _(dve):
            chain = Chain(dve, g.dve_steps)
            dve.wait_ge(s_x, 32)
            dve.wait_ge(s_mod, 96)
            for t in range(NT):
                dve.wait_ge(s_o, t + 1)
                chain.step(nc.vector.tensor_tensor(tmp[:, t % 2], g.ps[:, 2 * (t % 2):2 * (t % 2) + 2, :]
                                                   .rearrange("p a b -> p (a b)"), mod[:, 0, min(t, 1)], ALU.mult))
                nc.vector.tensor_tensor(m.x[:, t, :], m.x[:, t, :], tmp[:, t % 2], ALU.add).then_inc(s_x1, 1)
            dve.wait_ge(s_sq, NT)
            nc.vector.tensor_scalar(rms[:], ss[:], 1.0 / D, EPS, ALU.mult, ALU.add).then_inc(s_ms, 1)
            dve.wait_ge(s_sqrt, 1)
            chain.step(nc.vector.reciprocal(rstd[:], rms[:]))

            def split(v):
                return v.rearrange("p (a k) -> p a k", k=KD)
            for t in range(NT):
                s = min(t, 1)
                chain.step(nc.vector.scalar_tensor_tensor(tmp[:, t % 2], m.x[:, t, :], rstd[:, t:t + 1], mod[:, 2, s],
                                                          ALU.mult, ALU.mult))
                if t >= 2:
                    dve.wait_ge(s_tr, t - 1)
                    dve.wait_ge(s_h2st[t % 2], 16 * (t // 2))
                nc.vector.tensor_tensor(h2[:, t % 2].rearrange("p (k a) -> p a k", k=KD), split(tmp[:, t % 2]),
                                        split(mod[:, 1, s]), ALU.add).then_inc(s_h2, 1)
            dve.wait_ge(s_const, 1)
            chain.step(nc.vector.tensor_copy(iota[:], iotai[:]))
            dve.wait_ge(s_sc, 1)
            dve.wait_ge(s_rt, 32)
            chain.step(nc.vector.tensor_tensor(sel[:], scores[:], br[:].unsqueeze(1).to_broadcast([P, NT, NE]), ALU.add))
            for t in range(NT):
                for n in range(NG):
                    last = nc.vector.max(top[:, t, n, :], sel[:, t, n * 8:(n + 1) * 8])
            chain.step(last)
            chain.step(nc.vector.tensor_tensor(gs[:], top[:, :, :, 0], top[:, :, :, 1], ALU.add))
            for t in range(NT):
                last = nc.vector.max(gv[:, t, :], gs[:, t, :])
            chain.step(last)
            for t in range(NT):
                last = nc.vector.max_index(gi[:, t, :], gv[:, t, :], gs[:, t, :])
            chain.step(last)
            chain.step(nc.vector.tensor_copy(gif[:], gi[:]))
            group = iota[:, 0:NG].unsqueeze(1).to_broadcast([P, NT, NG])
            chain.step(nc.vector.tensor_tensor(gmask[:], gif[:, :, 0:1].to_broadcast([P, NT, NG]), group, ALU.is_equal))
            for j in range(1, TOPG):
                chain.step(nc.vector.tensor_tensor(geq[:], gif[:, :, j:j + 1].to_broadcast([P, NT, NG]), group,
                                                   ALU.is_equal))
                chain.step(nc.vector.tensor_tensor(gmask[:], gmask[:], geq[:], ALU.add))
            def by_group(v):
                return v.rearrange("p t (g e) -> p (t g) e", g=NG)
            def over(v):
                return v.rearrange("p t g -> p (t g)").unsqueeze(2).to_broadcast([P, NT * NG, NE // NG])
            chain.step(nc.vector.tensor_tensor(by_group(selm[:]), by_group(sel[:]), over(gmask[:]), ALU.mult))
            chain.step(nc.vector.tensor_scalar(geq[:], gmask[:], 1e30, -1e30, ALU.mult, ALU.add))
            chain.step(nc.vector.tensor_tensor(by_group(selm[:]), by_group(selm[:]), over(geq[:]), ALU.add))
            for t in range(NT):
                last = nc.vector.max(tv[:, t, :], selm[:, t, :])
            chain.step(last)
            for t in range(NT):
                last = nc.vector.max_index(ti[:, t, :], tv[:, t, :], selm[:, t, :])
            chain.step(last)
            chain.step(nc.vector.tensor_copy(tif[:], ti[:]))
            for k in range(TOP_K):
                last = nc.vector.tensor_tensor(eq[:, k].rearrange("p (t e) -> p t e", e=NE),
                                               tif[:, :, k:k + 1].to_broadcast([P, NT, NE]),
                                               iota[:].unsqueeze(1).to_broadcast([P, NT, NE]), ALU.is_equal)
            chain.step(last)
            nc.vector.tensor_reduce(M[:].rearrange("p t e -> p (t e)"), eq.rearrange("p k c -> p c k"), AX,
                                    ALU.add).then_inc(s_M, 1)

            def choose(out, table):
                chain.step(nc.vector.tensor_tensor(pick, eq, table.rearrange("p t e -> p (t e)").unsqueeze(1)
                                                   .to_broadcast([P, TOP_K, NT * NE]), ALU.mult))
                chain.step(nc.vector.tensor_reduce(out, pick.rearrange("p k (t e) -> p (k t) e", e=NE), AX, ALU.add))

            choose(m.wts[:].rearrange("p k t -> p (k t)"), scores[:])
            chain.step(nc.vector.tensor_reduce(wsum[:], m.wts[:].rearrange("p k t -> p t k"), AX, ALU.add))
            chain.step(nc.vector.reciprocal(wsum[:], wsum[:]))
            chain.step(nc.vector.scalar_tensor_tensor(m.wts[:], m.wts[:], ROUTED_SCALE,
                                                      wsum[:].unsqueeze(1).to_broadcast([P, TOP_K, NT]),
                                                      ALU.mult, ALU.mult))
            dve.wait_ge(s_rank, 1)
            chain.step(nc.vector.tensor_copy(rank[:].rearrange("p t e -> p (t e)"), g.ps[:, 5, 0:NT * NE]))
            chain.step(nc.vector.tensor_copy(cnt[:], g.ps[:, 5, NT * NE:(NT + 1) * NE]))
            chain.step(nc.vector.tensor_scalar(q[:], rank[:], float(BLK), None, ALU.is_ge))
            chain.step(nc.vector.tensor_scalar(more[:], cnt[:], float(BLK + 1), None, ALU.is_ge))
            for j in range(2, TOK // BLK):
                chain.step(nc.vector.scalar_tensor_tensor(q[:], rank[:], float(BLK * j), q[:], ALU.is_ge, ALU.add))
                chain.step(nc.vector.scalar_tensor_tensor(more[:], cnt[:], float(BLK * j + 1), more[:], ALU.is_ge,
                                                          ALU.add))
            chain.step(nc.vector.scalar_tensor_tensor(inblk[:], q[:], -float(BLK), rank[:], ALU.mult, ALU.add))
            chain.step(nc.vector.tensor_tensor_scan(upto[:], g.ones[:, 0:NE], more[:], 0.0, ALU.mult, ALU.add))
            chain.step(nc.vector.tensor_tensor(eblk[:], upto[:], more[:], ALU.subtract))
            chain.step(nc.vector.scalar_tensor_tensor(eblk[:], eblk[:], float(NE - 1), iota[:], ALU.add, ALU.subtract))
            chain.step(nc.vector.tensor_scalar(blk[:], q[:], 1.0, None, ALU.min))
            chain.step(nc.vector.tensor_tensor(blk[:], blk[:], eblk[:].unsqueeze(1).to_broadcast([P, NT, NE]), ALU.mult))
            chain.step(nc.vector.tensor_tensor(blk[:], blk[:], q[:], ALU.add))
            chain.step(nc.vector.tensor_tensor(blk[:], blk[:], iota[:].unsqueeze(1).to_broadcast([P, NT, NE]), ALU.add))
            chain.step(nc.vector.scalar_tensor_tensor(q[:], inblk[:], float(NBLK), blk[:], ALU.mult, ALU.add))
            choose(trow[:].rearrange("p k t -> p (k t)"), q[:])
            chain.step(nc.vector.tensor_copy(trowi[:], trow[:]))
            nc.vector.nop().then_inc(s_rows, 1)
            chain.step(nc.vector.tensor_scalar(iotam[:], iota[:, 0:MORE], 1.0, None, ALU.mult))
            chain.step(nc.vector.tensor_tensor(emore, upto[:].unsqueeze(1).to_broadcast([P, MORE, NE]),
                                               iotam[:].unsqueeze(2).to_broadcast([P, MORE, NE]), ALU.is_le))
            chain.step(nc.vector.tensor_reduce(emf[:], emore, AX, ALU.add))
            chain.step(nc.vector.tensor_scalar(emf[:], emf[:], float(NE - 1), None, ALU.min))
            chain.step(nc.vector.tensor_copy(m.emore[:], emf[0:1, :]))
            chain.step(nc.vector.tensor_scalar(emf[:], iotam[:], 2.0, upto[:, NE - 1:NE], ALU.mult, ALU.is_lt))
            chain.step(nc.vector.tensor_reduce(nmf[:], emf[:], AX, ALU.add))
            chain.step(nc.vector.tensor_scalar(nmf[:], nmf[:], 1.0, None, ALU.max))
            chain.step(nc.vector.tensor_copy(m.pairs[:], nmf[0:1, :]))
            dve.wait_ge(s_back, 16)
            chain.step(nc.vector.tensor_scalar(m.toks[:], m.rows[:], int(math.log2(TOP_K)), None,
                                               ALU.logical_shift_right))


def stage_experts(nc, g, w, m):
    ALL = (NE, U_MAIN), (MORE, U_MORE)
    with ExitStack() as ctx:
        def sb(name, shape, dt=F32):
            return ctx.enter_context(nc.sbuf_tensor(name, shape, dt))

        def sem(name):
            return ctx.enter_context(nc.semaphore(name))

        B2 = range(2)
        w13 = [sb(f"ex_w13_{b}", [P, KD, 2, FF]) for b in B2]
        w2 = [sb(f"ex_w2_{b}", [P, 2, D]) for b in B2]
        ids = [sb(f"ex_ids{b}", [P, 1], I32) for b in B2]
        outs = [sb(f"ex_outs{b}", [P, 1], I32) for b in B2]
        xg = [sb(f"ex_xg{b}", [P, D]) for b in B2]
        xT = [sb(f"ex_xT{b}", [P, KD, P]) for b in B2]
        silu = [sb(f"ex_silu{b}", [P, FF]) for b in B2]
        hid = [sb(f"ex_hid{b}", [P, FF]) for b in B2]
        hT = [sb(f"ex_hT{b}", [P, 2, P]) for b in B2]
        yo = [sb(f"ex_y{b}", [P, D]) for b in B2]

        s_w13, s_w2, s_xg, s_st = ([sem(f"ex_s_{n}{b}") for b in B2] for n in ("w13", "w2", "xg", "st"))
        s_ids, s_outs, s_begun = sem("ex_s_ids"), sem("ex_s_outs"), sem("ex_s_begun")
        names = ("xt", "xT0", "xT1", "up", "silu", "hid", "ht", "hT", "down", "y0", "y1")
        s = {n: sem(f"ex_{n}") for n in names}
        owner = {"xt": "pe", "up": "pe", "ht": "pe", "down": "pe", "xT0": "act", "silu": "act", "y0": "act",
                 "xT1": "dve", "hid": "dve", "hT": "dve", "y1": "dve"}

        def prime(eng, who):
            for n in names:
                if owner[n] == who:
                    eng.nop().then_inc(s[n], 2)

        def done(eng, name, n):
            eng.wait_ge(s[name], n + 3)

        def freed(eng, name, n):
            eng.wait_ge(s[name], n + 1)

        def landed(eng, sems, b, half, count=16):
            eng.wait_ge(sems[b], half * count + count)

        def loops(eng):
            yield NE // U_MAIN, U_MAIN, 0
            yield eng.value_load(m.pairs[0:1, 0:1], min_val=1, max_val=MORE // 2), U_MORE, NE

        block = ctx.enter_context(nc.Block())

        @block.sync
        def _(sp):
            for bodies, U, n0 in loops(sp):
                with sp.Fori(0, bodies) as i:
                    for u in range(U):
                        n, b = i * U + (n0 + u), u % 2
                        if n0 == 0:
                            e = sp.snap(i * U + u)
                        else:
                            e = sp.value_load(m.emore[0:1, bass.ds(i * U + u, 1)], min_val=0, max_val=NE - 1)
                        src1 = w["exp_w1"][0, bass.ds(e, 1)].rearrange("o (p k) f -> p (o k) f", k=KD)
                        src3 = w["exp_w3"][0, bass.ds(e, 1)].rearrange("o (p k) f -> p (o k) f", k=KD)
                        src2 = w["exp_w2"][0, bass.ds(e, 1)].rearrange("o (p j) d -> p (o j) d", j=2)
                        freed(sp, "up", n)
                        sp.dma_start(w13[b][:, :, 0, :], src1).then_inc(s_w13[b], 16)
                        sp.dma_start(w13[b][:, :, 1, :], src3).then_inc(s_w13[b], 16)
                        freed(sp, "down", n)
                        sp.dma_start(w2[b][:], src2).then_inc(s_w2[b], 16)

        @block.gpsimd
        def _(pool):
            def gather(n, col, b, wait=True):
                if wait:
                    freed(pool, "xt", n)
                nc.gpsimd.tensor_copy(ids[b][:], m.toks[:, col]).then_inc(s_ids, 1)
                if wait:
                    wait_apart(pool, s_ids, n + 1, s_begun)
                else:
                    pool.wait_ge(s_ids, 1)
                nc.gpsimd.indirect_dma_start(out=xg[b][:], out_offset=None, in_=m.h_dram,
                                             in_offset=bass.IndirectOffsetOnAxis(ap=ids[b][:, 0:1], axis=0),
                                             bounds_check=TOK - 1, oob_is_err=False).then_inc(s_xg[b], 16)

            def scatter(n, b):
                done(pool, "y0", n)
                done(pool, "y1", n)
                nc.gpsimd.tensor_copy(outs[b][:], m.rows[:, bass.ds(pool.snap(n), 1)]).then_inc(s_outs, 1)
                wait_apart(pool, s_outs, n + 1, s_begun)
                nc.gpsimd.indirect_dma_start(out=m.y_dram,
                                             out_offset=bass.IndirectOffsetOnAxis(ap=outs[b][:, 0:1], axis=0),
                                             in_=yo[b][:], in_offset=None,
                                             bounds_check=ROWS - 1, oob_is_err=False).then_inc(s_st[b], 16)

            for b in B2:
                nc.gpsimd.memset(xg[b][:], 0.0).then_inc(s_begun, 1)
            pool.wait_ge(s_begun, 2)
            gather(0, slice(0, 1), 0, wait=False)
            for bodies, U, n0 in loops(pool):
                with pool.Fori(0, bodies) as i:
                    for u in range(U):
                        n = i * U + (n0 + u)
                        gather(n + 1, bass.ds(pool.snap(n + 1), 1), (u + 1) % 2)
                        if u:
                            scatter(n - 1, (u - 1) % 2)
                    scatter(n, (U - 1) % 2)
            for b in B2:
                pool.wait_ge(s_st[b], bodies * 16 + 16 * (NE // 2))

        @block.tensor
        def _(pe):
            prime(pe, "pe")

            def transposes(n, b, half):
                landed(pe, s_xg, b, half)
                done(pe, "xT0", n - 1)
                done(pe, "xT1", n - 1)
                for k in range(KD):
                    last = nc.tensor.transpose(g.ps[:, k // 4, (k % 4) * P:(k % 4 + 1) * P],
                                               xg[b][:, k * P:(k + 1) * P], g.blocks[:, 0, :])
                last.then_inc(s["xt"], 1)

            def down(n, b, half):
                done(pe, "hT", n)
                landed(pe, s_w2, b, half)
                done(pe, "y0", n - 1)
                done(pe, "y1", n - 1)
                for c in range(2):
                    for j in range(2):
                        last = nc.tensor.matmul(g.ps[:, 6 + c, :], hT[b][:, j], w2[b][:, j, c * 512:(c + 1) * 512],
                                                start=j == 0, stop=j == 1)
                last.then_inc(s["down"], 1)

            transposes(0, 0, 0)
            for bodies, U, n0 in loops(pe):
                with pe.Fori(0, bodies) as i:
                    for u in range(U):
                        n, b = i * U + (n0 + u), u % 2
                        half = i * (U // 2) + (n0 + u) // 2
                        done(pe, "xT0", n)
                        done(pe, "xT1", n)
                        landed(pe, s_w13, b, half, 32)
                        freed(pe, "hid", n)
                        for k in range(KD):
                            last = nc.tensor.matmul(g.ps[:, 2 + b, :], xT[b][:, k],
                                                    w13[b][:, k].rearrange("p a f -> p (a f)"),
                                                    start=k == 0, stop=k == KD - 1)
                        last.then_inc(s["up"], 1)
                        if u:
                            down(n - 1, 1 - b, i * (U // 2) + (n0 + u - 1) // 2)
                        transposes(n + 1, 1 - b, i * (U // 2) + (n0 + u + 1) // 2)
                        done(pe, "hid", n)
                        freed(pe, "hT", n)
                        for j in range(2):
                            last = nc.tensor.transpose(g.ps[:, 4 + b, j * P:(j + 1) * P],
                                                       hid[b][:, j * P:(j + 1) * P], g.blocks[:, 0, :])
                        last.then_inc(s["ht"], 1)
                    down(n, b, half)

        @block.scalar
        def _(act):
            prime(act, "act")

            def copy_xT(n, b):
                done(act, "xt", n)
                freed(act, "up", n)
                nc.scalar.copy(xT[b][:, 0:4].rearrange("p k a -> p (k a)"), g.ps[:, 0, :]).then_inc(s["xT0"], 1)

            def copy_y(n, b, half):
                done(act, "down", n)
                act.wait_ge(s_st[b], half * 16)
                nc.scalar.copy(yo[b][:, 0:512], g.ps[:, 6, :]).then_inc(s["y0"], 1)

            copy_xT(0, 0)
            for bodies, U, n0 in loops(act):
                with act.Fori(0, bodies) as i:
                    for u in range(U):
                        n, b = i * U + (n0 + u), u % 2
                        done(act, "up", n)
                        freed(act, "hid", n)
                        nc.scalar.activation(silu[b][:], g.ps[:, 2 + b, 0:FF], ACT.Silu).then_inc(s["silu"], 1)
                        if u:
                            copy_y(n - 1, 1 - b, i * (U // 2) + (n0 + u - 1) // 2)
                        copy_xT(n + 1, 1 - b)
                    copy_y(n, b, i * (U // 2) + (n0 + u) // 2)

        @block.vector
        def _(dve):
            prime(dve, "dve")

            def copy_xT(n, b):
                done(dve, "xt", n)
                freed(dve, "up", n)
                nc.vector.tensor_copy(xT[b][:, 4:8].rearrange("p k a -> p (k a)"), g.ps[:, 1, :]).then_inc(s["xT1"], 1)

            def copy_y(n, b, half):
                done(dve, "down", n)
                dve.wait_ge(s_st[b], half * 16)
                nc.vector.tensor_copy(yo[b][:, 512:D], g.ps[:, 7, :]).then_inc(s["y1"], 1)

            copy_xT(0, 0)
            for bodies, U, n0 in loops(dve):
                with dve.Fori(0, bodies) as i:
                    for u in range(U):
                        n, b = i * U + (n0 + u), u % 2
                        done(dve, "silu", n)
                        freed(dve, "ht", n)
                        nc.vector.tensor_tensor(hid[b][:].rearrange("p (j a) -> p a j", j=2),
                                                silu[b][:].rearrange("p (a j) -> p a j", j=2),
                                                g.ps[:, 2 + b, FF:2 * FF].rearrange("p (a j) -> p a j", j=2),
                                                ALU.mult).then_inc(s["hid"], 1)
                        if u:
                            copy_y(n - 1, 1 - b, i * (U // 2) + (n0 + u - 1) // 2)
                        copy_xT(n + 1, 1 - b)
                        done(dve, "ht", n)
                        freed(dve, "down", n)
                        nc.vector.tensor_copy(hT[b][:].rearrange("p j a -> p (j a)"),
                                              g.ps[:, 4 + b, 0:2 * P]).then_inc(s["hT"], 1)
                    copy_y(n, b, i * (U // 2) + (n0 + u) // 2)


def stage_combine(nc, g, w, m):
    with ExitStack() as ctx:
        def sb(name, shape, dt=F32):
            return ctx.enter_context(nc.sbuf_tensor(name, shape, dt))

        def sem(name):
            return ctx.enter_context(nc.semaphore(name))

        rows = sb("cb_rows", [P, 2, TOP_K, D])
        g2 = sb("cb_g2", [P, 2, D])
        nf = sb("cb_nf", [P, D])
        sq = sb("cb_sq", [P, D])
        ss, rms, rstd = sb("cb_ss", [P, NT]), sb("cb_rms", [P, NT]), sb("cb_rstd", [P, NT])
        s_row = [sem(f"cb_s_row{b}") for b in range(2)]
        s_acc, s_in, s_x, s_sq, s_ms, s_rt, s_out, s_st = (
            sem("cb_s_acc"), sem("cb_s_in"), sem("cb_s_x"), sem("cb_s_sq"), sem("cb_s_ms"), sem("cb_s_rt"),
            sem("cb_s_out"), sem("cb_s_st"))
        acc = g.oT[:].rearrange("p a b -> p (a b)").rearrange("p (t d) -> p t d", d=D)
        block = ctx.enter_context(nc.Block())

        @block.sync
        def _(sp):
            def load(t):
                if t >= 2:
                    sp.wait_ge(s_acc, TOP_K * (t - 1))
                sp.dma_start(rows[:, t % 2], m.y_dram[t * P * TOP_K:(t + 1) * P * TOP_K, :]
                             .rearrange("(p k) d -> p k d", k=TOP_K)).then_inc(s_row[t % 2], 16)

            load(0)
            load(1)
            for s in range(2):
                sp.dma_start(g2[:, s], g.mod_dram[s:s + 1, 5 * D:6 * D].to_broadcast([P, D])).then_inc(s_in, 16)
            sp.dma_start(nf[:], w["norm_f"].rearrange("(o d) -> o d", o=1).to_broadcast([P, D])).then_inc(s_in, 16)
            for t in range(NT):
                if t + 2 < NT:
                    load(t + 2)
                sp.wait_ge(s_out, t + 1)
                dst = w["y_prompt"][0] if t == 0 else w["y_sample"][0, (t - 1) * P:t * P, :]
                sp.dma_start(dst, m.x[:, t, :]).then_inc(s_st, 16)
            sp.wait_ge(s_st, 16 * NT)

        @block.vector
        def _(dve):
            chain = Chain(dve, g.dve_steps)
            dve.wait_ge(s_in, 48)

            def finish(t):
                dve.wait_ge(s_rt, t + 1)
                chain.step(nc.vector.reciprocal(rstd[:, t:t + 1], rms[:, t:t + 1]))
                nc.vector.scalar_tensor_tensor(m.x[:, t, :], m.x[:, t, :], rstd[:, t:t + 1], nf[:], ALU.mult,
                                               ALU.mult).then_inc(s_out, 1)
            for t in range(NT):
                for k in range(TOP_K):
                    n = t * TOP_K + k
                    if k == 0:
                        dve.wait_ge(s_row[t % 2], 16 * (t // 2 + 1))
                    else:
                        dve.wait_ge(s_acc, n)
                    nc.vector.scalar_tensor_tensor(acc[:, t, :], rows[:, t % 2, k], m.wts[:, k, t:t + 1], acc[:, t, :],
                                                   ALU.mult, ALU.add).then_inc(s_acc, 1)
                dve.wait_ge(s_acc, (t + 1) * TOP_K)
                chain.step(nc.vector.tensor_tensor(acc[:, t, :], acc[:, t, :], g2[:, min(t, 1)], ALU.mult))
                nc.vector.tensor_tensor(m.x[:, t, :], m.x[:, t, :], acc[:, t, :], ALU.add).then_inc(s_x, 1)
                dve.wait_ge(s_sq, t + 1)
                nc.vector.tensor_scalar(rms[:, t:t + 1], ss[:, t:t + 1], 1.0 / D, EPS, ALU.mult,
                                        ALU.add).then_inc(s_ms, 1)
                if t:
                    finish(t - 1)
            finish(NT - 1)

        @block.scalar
        def _(act):
            for t in range(NT):
                act.wait_ge(s_x, t + 1)
                if t:
                    act.wait_ge(s_sq, t)
                nc.scalar.activation(sq[:], m.x[:, t, :], ACT.Square, accum_out=ss[:, t:t + 1]).then_inc(s_sq, 1)
                act.wait_ge(s_ms, t + 1)
                nc.scalar.activation(rms[:, t:t + 1], rms[:, t:t + 1], ACT.Sqrt).then_inc(s_rt, 1)


def build(nc, w):
    with ExitStack() as ctx:
        def sb(name, shape, dt=F32):
            return ctx.enter_context(nc.sbuf_tensor(name, shape, dt))

        g, m = Shared(), Shared()
        g.dve_steps = Count(ctx.enter_context(nc.semaphore("dve_steps")))
        g.pool_steps = Count(ctx.enter_context(nc.semaphore("pool_steps")))
        g.act_steps = Count(ctx.enter_context(nc.semaphore("act_steps")))
        g.ps = ctx.enter_context(nc.psum_tensor("ps", [P, 8, 512], F32))
        g.blocks = sb("blocks", [P, 7, P])
        g.levels = sb("levels", [P, 6, P])
        g.tri = sb("tri", [P, 2, 2, P])
        g.ones = sb("ones", [P, P])
        g.hT = sb("hT", [P, KD, TOK])
        g.oT = sb("oT", [P, KD, TOK])
        g.mod_dram = nc.dram_tensor("mod_dram", [2, MOD], F32, kind="Internal").ap()
        m.h_dram = nc.dram_tensor("h_dram", [TOK, D], F32, kind="Internal").ap()
        m.tab_dram = nc.dram_tensor("tab_dram", [P * NBLK, 1], I32, kind="Internal").ap()
        m.y_dram = nc.dram_tensor("y_dram", [ROWS, D], F32, kind="Internal").ap()
        stage_modulation(nc, g, w)
        stage_gla(nc, g, w)
        stage_rwkv(nc, g, w)
        m.x = sb("x_res", [P, NT, D])
        m.rows = sb("rows", [P, NBLK], I32)
        m.toks = sb("toks", [P, NBLK], I32)
        m.wts = sb("wts", [P, TOP_K, NT])
        m.emore = sb("emore", [1, MORE], I32)
        m.pairs = sb("pairs", [1, 1], I32)
        stage_project_and_route(nc, g, w, m)
        stage_experts(nc, g, w, m)
        stage_combine(nc, g, w, m)


_INS = ['x_prompt', 'x_sample', 'c', 'state_gla', 'state_rwkv', 'c_ctx', 'ada_w', 'ada_b', 'norm1', 'norm2', 'norm_f',
        'w_in', 'w_out', 'gla_w_dec', 'gla_b_dec', 'gla_norm', 'rwkv_conv', 'rwkv_w2', 'rwkv_w0', 'rwkv_a2', 'rwkv_a0',
        'rwkv_g2', 'rwkv_k_k', 'rwkv_k_a', 'rwkv_r_k', 'rwkv_ln_g', 'rwkv_ln_b', 'router_w', 'router_b', 'exp_w1',
        'exp_w3', 'exp_w2', 'sh_w1', 'sh_w3', 'sh_w2']
_OUTS = [('y_prompt', (1, CTX, D)), ('y_sample', (1, LAT, D)), ('new_state_gla', (1, 1, 2, GLA_H, GLA_DK, GLA_DV)),
         ('new_state_rwkv', (1, 1, 2, RH, RN, RN))]


def kernel(**inputs):
    import numpy as _np
    import concourse.bacc as _bacc
    from concourse.bass_utils import run_bass_kernel_spmd as _run

    nc = _bacc.Bacc("TRN2", target_bir_lowering=False, num_devices=1)
    arrays, w = {}, {}
    for name in _INS:
        a = _np.ascontiguousarray(inputs[name])
        arrays[f"in_{name}_dram"] = a
        w[name] = nc.dram_tensor(f"in_{name}_dram", a.shape, F32, kind="ExternalInput").ap()
    for name, shape in _OUTS:
        w[name] = nc.dram_tensor(f"out_{name}_dram", shape, F32, kind="ExternalOutput").ap()
    build(nc, w)
    r = _run(nc, [arrays], core_ids=[0])
    return tuple(r.results[0][f"out_{name}_dram"] for name, _ in _OUTS)
```

```python
import math
from contextlib import ExitStack

import concourse.bass as bass
from concourse import mybir

ALU = mybir.AluOpType
ACT = mybir.ActivationFunctionType
AX = mybir.AxisListType.X
F32 = mybir.dt.float32
I32 = mybir.dt.int32
U32 = mybir.dt.uint32

P = 128
D = 1024
KD = D // P
CTX, LAT = 128, 512
TOK = CTX + LAT
NT = TOK // P
GRID_W, GRID_H = 64, LAT // 64
EPS = 1e-6
RWKV_LN_EPS = 64e-5
MOD = 6 * D
C = 64
NCH = TOK // C
CTX_CH, LAT_CH = CTX // C, LAT // C

GLA_H, GLA_DK, GLA_DV, GLA_RANK = 4, 64, 128, 16
GLA_QK, GLA_W = GLA_H * GLA_DK, GLA_H * GLA_DV
GLA_COLS = 2 * GLA_QK + 2 * GLA_W + 2 * GLA_RANK
RH, RN = 8, 64
RW = RH * RN
DECAY_RANK, AAA_RANK, GATE_RANK = 64, 64, 128
HP = RH // 2

NE, TOP_K, NG, TOPG = 64, 8, 8, 4
FF = D // 4
ROUTED_SCALE = 2.5


class Count:

    def __init__(self, sem):
        self.sem, self.n = sem, 0


class Chain:

    def __init__(self, eng, count):
        self.eng, self.count = eng, count

    def step(self, ins):
        self.count.n += 1
        ins.then_inc(self.count.sem, 1)
        self.eng.wait_ge(self.count.sem, self.count.n)


class Shared:
    pass


def build_constants(nc, g, pool, chain):
    chain.step(nc.gpsimd.memset(g.ones[:], 1.0))
    for n in range(7):
        size = 1 << n
        m = g.blocks[:, n, :]
        v = m.rearrange("p (a b) -> p a b", b=size)
        chain.step(nc.gpsimd.memset(m, 1.0))
        chain.step(nc.gpsimd.affine_select(out=v, in_=v, compare_op=ALU.is_ge, fill=0.0, base=0,
                                           pattern=[[-size, P // size], [0, size]], channel_multiplier=1))
        chain.step(nc.gpsimd.affine_select(out=v, in_=v, compare_op=ALU.is_ge, fill=0.0, base=size - 1,
                                           pattern=[[size, P // size], [0, size]], channel_multiplier=-1))
    for n in range(6):
        chain.step(nc.gpsimd.tensor_tensor(g.levels[:, n, :], g.blocks[:, n + 1, :], g.blocks[:, n, :],
                                           ALU.subtract))
    for d in range(2):
        for kind in range(2):
            sign = 1 if d == 0 else -1
            chain.step(nc.gpsimd.affine_select(out=g.tri[:, d, kind, :], in_=g.blocks[:, 6, :],
                                               compare_op=ALU.is_ge, fill=0.0, base=kind - 1,
                                               pattern=[[sign, P]], channel_multiplier=-sign))


def stage_modulation(nc, g, w):
    NB, NBUF = MOD // 512, 3
    with ExitStack() as ctx:
        def sb(name, shape, dt=F32):
            return ctx.enter_context(nc.sbuf_tensor(name, shape, dt))

        def sem(name):
            return ctx.enter_context(nc.semaphore(name))

        aw = sb("ada_w_sb", [P, NBUF, KD, 512])
        cT = sb("cT", [P, 2, KD])
        scT = sb("silu_cT", [P, KD, 2])
        modrow = sb("modrow", [2, MOD])
        adab = sb("adab", [2, MOD])
        nrm = sb("normrows", [2, 2, D])
        x = sb("x_sb", [P, NT, D])
        sq = sb("sq", [P, D])
        ss = sb("ss", [P, NT])
        rms = sb("rms", [P, NT])
        rstd = sb("rstd", [P, NT])
        wb = sb("wb", [P, 2, D])
        shb = sb("shb", [P, 2, D])
        hx = sb("hx", [P, 2, D])

        s_c, s_rows, s_x = sem("m_c"), sem("m_rows"), sem("m_x")
        s_aw = [sem(f"m_aw{n}") for n in range(NBUF)]
        s_silu, s_mm, s_ev = sem("m_silu"), sem("m_mm"), sem("m_ev")
        s_mod, s_st, s_bc = sem("m_mod"), sem("m_st"), sem("m_bc")
        s_sq, s_ms, s_rt, s_rstd = sem("m_sq"), sem("m_ms"), sem("m_rt"), sem("m_rstd")
        s_hx, s_tr, s_hT = sem("m_hx"), sem("m_tr"), sem("m_hT")
        s_const = sem("m_const")

        ada = w["ada_w"][0].rearrange("(p k) n -> p k n", k=KD)
        block = ctx.enter_context(nc.Block())

        @block.sync
        def _(sp):
            sp.dma_start(cT[:, 0, :], w["c_ctx"].rearrange("(p k) -> p k", k=KD)).then_inc(s_c, 16)
            sp.dma_start(cT[:, 1, :], w["c"][0].rearrange("(p k) -> p k", k=KD)).then_inc(s_c, 16)
            for n in range(NB):
                if n >= NBUF:
                    sp.wait_ge(s_mm, n - NBUF + 1)
                sp.dma_start(aw[:, n % NBUF], ada[:, :, n * 512:(n + 1) * 512]).then_inc(s_aw[n % NBUF], 16)
            sp.wait_ge(s_mod, 1)
            sp.dma_start(g.mod_dram, modrow[:, :]).then_inc(s_st, 16)
            sp.wait_ge(s_st, 16)
            for s in range(2):
                sp.dma_start(wb[:, s], g.mod_dram[s:s + 1, D:2 * D].to_broadcast([P, D])).then_inc(s_bc, 16)
                sp.dma_start(shb[:, s], g.mod_dram[s:s + 1, 0:D].to_broadcast([P, D])).then_inc(s_bc, 16)

        @block.gpsimd
        def _(pool):
            for s in range(2):
                pool.dma_start(adab[s:s + 1, :], w["ada_b"]).then_inc(s_rows, 16)
                pool.dma_start(nrm[s:s + 1, 0, :], w["norm1"]).then_inc(s_rows, 16)
                pool.dma_start(nrm[s:s + 1, 1, :], w["norm2"]).then_inc(s_rows, 16)
            build_constants(nc, g, pool, Chain(pool, g.pool_steps))
            nc.gpsimd.nop().then_inc(s_const, 1)

        @block.scalar
        def _(act):
            act.dma_start(x[:, 0, :], w["x_prompt"][0]).then_inc(s_x, 16)
            act.dma_start(x[:, 1:NT, :], w["x_sample"][0].rearrange("(t p) d -> p t d", p=P)).then_inc(s_x, 16)
            act.wait_ge(s_c, 32)
            nc.scalar.activation(scT[:].rearrange("p k s -> p s k"), cT[:], ACT.Silu).then_inc(s_silu, 1)
            act.wait_ge(s_x, 32)
            for t in range(NT):
                if t:
                    act.wait_ge(s_sq, t)
                nc.scalar.activation(sq[:], x[:, t, :], ACT.Square, accum_out=ss[:, t:t + 1]).then_inc(s_sq, 1)
            act.wait_ge(s_ms, 1)
            nc.scalar.activation(rms[:], rms[:], ACT.Sqrt).then_inc(s_rt, 1)
            for t in range(NT):
                for half in range(2):
                    n = 2 * t + half
                    act.wait_ge(s_tr, n + 1)
                    nc.scalar.copy(g.hT[:, 4 * half:4 * half + 4, t * P:(t + 1) * P],
                                   g.ps[:, 4 + n % 4, :].rearrange("p (k m) -> p k m", k=4)).then_inc(s_hT, 1)

        @block.vector
        def _(dve):
            chain = Chain(dve, g.dve_steps)
            dve.wait_ge(s_rows, 16 * 6)
            for n in range(NB):
                dve.wait_ge(s_mm, n + 1)
                nc.vector.tensor_tensor(modrow[:, n * 512:(n + 1) * 512], g.ps[0:2, n % 4, :],
                                        adab[:, n * 512:(n + 1) * 512], ALU.add).then_inc(s_ev, 1)
            dve.wait_ge(s_ev, NB)
            for n, part in enumerate((1, 4)):
                row = modrow[:, part * D:(part + 1) * D]
                chain.step(nc.vector.scalar_tensor_tensor(row, row, 1.0, nrm[:, n, :], ALU.add, ALU.mult))
            nc.vector.nop().then_inc(s_mod, 1)
            dve.wait_ge(s_sq, NT)
            nc.vector.tensor_scalar(rms[:], ss[:], 1.0 / D, EPS, ALU.mult, ALU.add).then_inc(s_ms, 1)
            dve.wait_ge(s_rt, 1)
            chain.step(nc.vector.reciprocal(rstd[:], rms[:]))
            dve.wait_ge(s_bc, 64)
            for t in range(NT):
                s = min(t, 1)
                if t >= 2:
                    dve.wait_ge(s_tr, 2 * (t - 1))
                chain.step(nc.vector.scalar_tensor_tensor(hx[:, t % 2], x[:, t, :], rstd[:, t:t + 1], wb[:, s],
                                                          ALU.mult, ALU.mult))
                nc.vector.tensor_tensor(hx[:, t % 2], hx[:, t % 2], shb[:, s], ALU.add).then_inc(s_hx, 1)

        @block.tensor
        def _(pe):
            pe.wait_ge(s_silu, 1)
            for n in range(NB):
                pe.wait_ge(s_aw[n % NBUF], 16 * (n // NBUF + 1))
                if n >= 4:
                    pe.wait_ge(s_ev, n - 3)
                for k in range(KD):
                    last = nc.tensor.matmul(g.ps[0:2, n % 4, :], scT[:, k, :], aw[:, n % NBUF, k, :],
                                            start=k == 0, stop=k == KD - 1)
                last.then_inc(s_mm, 1)
            pe.wait_ge(s_const, 1)
            for t in range(NT):
                pe.wait_ge(s_hx, t + 1)
                for half in range(2):
                    n = 2 * t + half
                    if n >= 4:
                        pe.wait_ge(s_hT, n - 3)
                    for k in range(4):
                        kk = 4 * half + k
                        last = nc.tensor.transpose(g.ps[:, 4 + n % 4, k * P:(k + 1) * P],
                                                   hx[:, t % 2, kk * P:(kk + 1) * P], g.blocks[:, 0, :])
                    last.then_inc(s_tr, 1)


class Steps:

    def __init__(self, sem, *names):
        self.sem, self.names, self.n = sem, names, len(names)

    def prime(self, ins):
        ins.then_inc(self.sem, self.n)

    def before(self, it, name):
        return it * self.n + self.names.index(name) + 1

    def at(self, it, name):
        return it * self.n + self.n + self.names.index(name) + 1


def wait_apart(eng, sem, value, ready):
    value = reg(eng, value)
    eng.wait_ge(ready, 1)
    eng.wait_ge(sem, value)


def reg(eng, value):
    return value if isinstance(value, int) else eng.snap(value)


def log_decay_to_steps(nc, chain, dd, cum, reset, lw, mid):
    chain.step(nc.vector.tensor_tensor_scan(cum, reset, lw, 0.0, ALU.mult, ALU.add))
    cumc = cum.rearrange("p (c t) -> p c t", t=C)
    middle = cumc[:, :, mid:mid + 1]
    chain.step(nc.vector.tensor_tensor(dd[:, :, 1:C + 1], cumc, middle.to_broadcast([P, NCH, C]), ALU.subtract))
    chain.step(nc.vector.tensor_scalar(dd[:, :, 0:1], middle, -1.0, None, ALU.mult))


def stage_gla(nc, g, w):
    PAIRS, S = GLA_H // 2, 1.0 / 16.0
    with ExitStack() as ctx:
        def sb(name, shape, dt=F32):
            return ctx.enter_context(nc.sbuf_tensor(name, shape, dt))

        def sem(name):
            return ctx.enter_context(nc.semaphore(name))

        win = sb("gla_w", [P, 2, KD, 512])
        wz = sb("gla_wz", [P, KD, 2 * GLA_RANK])
        wdec = sb("gla_wdec", [2 * GLA_RANK, 2, GLA_QK])
        bdec = sb("gla_bdec", [P, 2, PAIRS])
        ng = sb("gla_ng", [P, GLA_H])
        z = sb("gla_z", [2 * GLA_RANK, TOK])
        q = sb("gla_q", [P, PAIRS, TOK])
        k = sb("gla_k", [P, PAIRS, TOK])
        v = sb("gla_v", [P, GLA_H, TOK])
        gate = sb("gla_gate", [P, GLA_H, TOK])
        tmp = sb("gla_tmp", [P, 4, TOK])
        xmin = sb("gla_xmin", [P, 4, TOK])
        reset = sb("gla_reset", [P, TOK])
        dd = sb("gla_dd", [P, 2, PAIRS, NCH, C + 1])
        ends = sb("gla_ends", [P, 2, 2, PAIRS, NCH])
        qs = sb("gla_qs", [P, 2, PAIRS, P])
        ks = sb("gla_ks", [P, 2, PAIRS, P])
        vs = sb("gla_vs", [P, 2, GLA_H, C])
        ktok = sb("gla_ktok", [P, 2, PAIRS, P])
        vtok = sb("gla_vtok", [P, 2, PAIRS, P])
        att = sb("gla_att", [P, 2, PAIRS, P])
        m0 = sb("gla_m0", [P, 2, PAIRS, GLA_DV])
        mraw = sb("gla_mraw", [P, 2, PAIRS, GLA_DV])
        msum = sb("gla_msum", [P, 2, PAIRS, GLA_DV])
        o = g.oT[:, 0:GLA_H, :]

        tiles = [("z", 0)] + [("q", p) for p in range(2)] + [("k", p) for p in range(2)] + \
                [("dec", n) for n in range(4)] + [("v", h) for h in range(4)] + [("g", h) for h in range(4)]
        by_act = [t for t in tiles if t[0] in "qkvg" or t[0] == "dec"]
        by_dve = [t for t in tiles if t[0] in ("z", "dec")]
        s_w = [sem("gla_s_w0"), sem("gla_s_w1")]
        s_small, s_init, s_ps = sem("gla_s_small"), sem("gla_s_init"), sem("gla_s_ps")
        s_eva, s_evd, s_ln = sem("gla_s_eva"), sem("gla_s_evd"), sem("gla_s_ln")
        s_dd, s_ends = sem("gla_s_dd"), sem("gla_s_ends")
        s_st, s_ld, s_zero = sem("gla_s_st"), sem("gla_s_ld"), sem("gla_s_zero")
        s_osq, s_oms, s_ort, s_orms = sem("gla_s_osq"), sem("gla_s_oms"), sem("gla_s_ort"), sem("gla_s_orms")
        PE = Steps(sem("gla_pe"), "ktok", "vtok", "scores", "out", "state")
        DV = Steps(sem("gla_dv"), "ks", "qs", "att", "out_f", "out", "msum", "mraw")
        AC = Steps(sem("gla_ac"), "exp_k", "exp_q", "ktok", "vtok")
        PO = Steps(sem("gla_po"), "m0", "vs")
        loops = ((0, CTX_CH, 0), (CTX_CH, LAT_CH, CTX_CH))

        def evacuated(eng, m):
            name = tiles[m]
            if name in by_act:
                eng.wait_ge(s_eva, by_act.index(name) + 1)
            if name in by_dve:
                eng.wait_ge(s_evd, by_dve.index(name) + 1)

        def slot(m):
            return g.ps[:, 2 * (m % 4):2 * (m % 4) + 2, 0:TOK // 2]

        w_in = w["w_in"][0].rearrange("(k p) n -> p k n", p=P)
        block = ctx.enter_context(nc.Block())

        @block.sync
        def _(sp):
            sp.dma_start(wz[:], w_in[:, :, GLA_COLS - 2 * GLA_RANK:GLA_COLS]).then_inc(s_small, 16)
            for d in range(2):
                sp.dma_start(bdec[:, d, :], w["gla_b_dec"][0, d].rearrange("(p c) -> c p", c=P), allow_slow_non_contiguous=True).then_inc(s_small, 16)
            sp.dma_start(ng[:], w["gla_norm"][0].rearrange("(h c) -> c h", c=P), allow_slow_non_contiguous=True).then_inc(s_small, 16)
            sp.wait_ge(s_zero, 1)
            for d in range(2):
                sp.dma_start(wdec[GLA_RANK * d:GLA_RANK * (d + 1), d, :], w["gla_w_dec"][0, d]).then_inc(s_small, 16)
            for b in range(3):
                if b == 2:
                    sp.wait_ge(s_ps, tiles.index(("k", 1)) + 1)
                sp.dma_start(win[:, b % 2], w_in[:, :, 512 * b:512 * (b + 1)]).then_inc(s_w[b % 2], 16)
            sp.wait_ge(DV.sem, DV.at(CTX_CH - 1, "mraw"))
            for d in range(2):
                for p in range(PAIRS):
                    sp.dma_start(w["new_state_gla"][0, 0, d, 2 * p:2 * p + 2].rearrange("h k v -> (h k) v"),
                                 mraw[:, d, p, :]).then_inc(s_st, 16)
            sp.wait_ge(s_st, 16 * 4)
            for d in range(2):
                for p in range(PAIRS):
                    sp.dma_start(mraw[:, d, p, :],
                                 w["state_gla"][0, 0, d, 2 * p:2 * p + 2].rearrange("h k v -> (h k) v")).then_inc(s_ld, 16)

        @block.tensor
        def _(pe):
            for m, (kind, n) in enumerate(tiles):
                if m >= 4:
                    evacuated(pe, m - 4)
                if (kind, n) == ("z", 0):
                    pe.wait_ge(s_small, 16 * 6)
                if n == 0 and kind in "qvg":
                    b = "qvg".index(kind)
                    pe.wait_ge(s_w[b % 2], 16 * (b // 2 + 1))
                if kind == "dec":
                    if n == 0:
                        evacuated(pe, 0)
                    for half in range(2):
                        last = nc.tensor.matmul(slot(m)[:, half], wdec[:, n // 2, (n % 2) * P:(n % 2 + 1) * P],
                                                z[:, half * 320:half * 320 + 320], start=True, stop=True)
                else:
                    for half in range(2):
                        for kt in range(KD):
                            if kind == "z":
                                lhsT, out = wz[:, kt, :], slot(m)[0:2 * GLA_RANK, half]
                            else:
                                c0 = (n + (2 if kind == "k" else 0)) * P
                                b = {"q": 0, "k": 0, "v": 1, "g": 2}[kind]
                                lhsT, out = win[:, b % 2, kt, c0:c0 + P], slot(m)[:, half]
                            last = nc.tensor.matmul(out, lhsT, g.hT[:, kt, half * 320:half * 320 + 320],
                                                    start=kt == 0, stop=kt == KD - 1)
                last.then_inc(s_ps, 1)
            PE.prime(nc.tensor.nop())
            for m in range(len(tiles) - 4, len(tiles)):
                evacuated(pe, m)
            pe.wait_ge(s_ends, 1)
            for it0, count, _ in loops:
                with pe.Fori(0, count) as i:
                    it = i + it0
                    units = [(d, p) for d in range(2) for p in range(PAIRS)]
                    pe.wait_ge(DV.sem, DV.at(it, "ks"))
                    pe.wait_ge(AC.sem, AC.before(it, "ktok"))
                    for n, (d, p) in enumerate(units):
                        last = nc.tensor.transpose(g.ps[:, 0, n * P:(n + 1) * P], ks[:, d, p], g.blocks[:, 0, :])
                    last.then_inc(PE.sem, 1)
                    pe.wait_ge(PO.sem, PO.at(it, "vs"))
                    pe.wait_ge(AC.sem, AC.before(it, "vtok"))
                    for n, (d, p) in enumerate(units):
                        last = nc.tensor.transpose(g.ps[:, 1, n * P:(n + 1) * P], vs[:, d, 2 * p:2 * p + 2, :],
                                                   g.blocks[:, 0, :])
                    last.then_inc(PE.sem, 1)
                    pe.wait_ge(DV.sem, DV.at(it, "qs"))
                    pe.wait_ge(DV.sem, DV.before(it, "att"))
                    for n, (d, p) in enumerate(units):
                        last = nc.tensor.matmul(g.ps[:, 2, n * P:(n + 1) * P], ks[:, d, p], qs[:, d, p],
                                                start=True, stop=True)
                    last.then_inc(PE.sem, 1)
                    pe.wait_ge(AC.sem, AC.at(it, "vtok"))
                    pe.wait_ge(DV.sem, DV.at(it, "att"))
                    pe.wait_ge(PO.sem, PO.at(it, "m0"))
                    for n, (d, p) in enumerate(units):
                        nc.tensor.matmul(g.ps[:, 3, n * P:(n + 1) * P], vtok[:, d, p], att[:, d, p],
                                         start=True, stop=False)
                        last = nc.tensor.matmul(g.ps[:, 3, n * P:(n + 1) * P], m0[:, d, p], qs[:, d, p],
                                                start=False, stop=True)
                    last.then_inc(PE.sem, 1)
                    pe.wait_ge(AC.sem, AC.at(it, "ktok"))
                    for n, (d, p) in enumerate(units):
                        last = nc.tensor.matmul(g.ps[:, 4, n * P:(n + 1) * P], ktok[:, d, p], vtok[:, d, p],
                                                start=True, stop=True)
                    last.then_inc(PE.sem, 1)
            for h in range(GLA_H):
                pe.wait_ge(s_osq, h + 1)
                if h >= 2:
                    pe.wait_ge(s_oms, h - 1)
                for half in range(2):
                    last = nc.tensor.matmul(g.ps[:, 2 * (h % 2) + half, 0:320], g.ones[:],
                                            tmp[:, h, half * 320:half * 320 + 320], start=True, stop=True)
                last.then_inc(s_orms, 1)

        @block.scalar
        def _(act):
            chain = Chain(act, g.act_steps)
            act.wait_ge(s_small, 16 * 6)
            dests = {"q": q, "k": k, "v": v, "g": gate}
            for m, (kind, n) in enumerate(tiles):
                if kind == "z":
                    continue
                act.wait_ge(s_ps, m + 1)
                src = slot(m)
                if kind == "dec":
                    dst = tmp[:, n, :].rearrange("p (a b) -> p a b", a=2)
                    nc.scalar.activation(dst, src, ACT.Abs, bias=bdec[:, n // 2, n % 2:n % 2 + 1]).then_inc(s_eva, 1)
                    if n == 3:
                        act.wait_ge(s_eva, by_act.index(("dec", 3)) + 1)
                        chain.step(nc.scalar.activation(tmp[:], tmp[:], ACT.Exp, scale=-1.0))
                        nc.scalar.activation(tmp[:], tmp[:], ACT.Ln, bias=1.0).then_inc(s_ln, 1)
                else:
                    dst = dests[kind][:, n, :].rearrange("p (a b) -> p a b", a=2)
                    nc.scalar.activation(dst, src, ACT.Silu if kind == "g" else ACT.Copy,
                                         scale=GLA_DK ** -0.5 if kind == "q" else 1.0).then_inc(s_eva, 1)
            act.wait_ge(s_dd, 1)
            for d in range(2):
                for n in range(2):
                    off, sign = ((0, -1.0), (C, 1.0))[n ^ d]
                    last = nc.scalar.activation(ends[:, d, n], dd[:, d, :, :, off], ACT.Exp, scale=sign * S)
            last.then_inc(s_ends, 1)
            AC.prime(nc.scalar.nop())
            act.wait_ge(s_init, 1)
            for it0, count, c0 in loops:
                with act.Fori(0, count) as i:
                    it = i + it0
                    wait_apart(act, PE.sem, PE.before(it, "out"), s_dd)
                    chunk = (act.snap(i + c0), act.snap(c0 + count - 1 - i))
                    for which, dst, name in ((0, ks, "exp_k"), (1, qs, "exp_q")):
                        for d in range(2):
                            off = (1, 0)[d]
                            sign = (-1.0, 1.0)[which ^ d]
                            for h in range(2):
                                r = slice(64 * h, 64 * h + 64)
                                src = dd[r, d, :, bass.ds(chunk[d], 1), off:off + C]
                                last = nc.scalar.activation(dst[r, d, :, 64 * h:64 * h + 64],
                                                            src.rearrange("p a o t -> p a (o t)"), ACT.Exp,
                                                            scale=sign * S)
                        last.then_inc(AC.sem, 1)
                    act.wait_ge(PE.sem, PE.at(it, "ktok"))
                    nc.scalar.copy(ktok[:].rearrange("p d a b -> p (d a b)"), g.ps[:, 0, :]).then_inc(AC.sem, 1)
                    act.wait_ge(PE.sem, PE.at(it, "vtok"))
                    nc.scalar.copy(vtok[:].rearrange("p d a b -> p (d a b)"), g.ps[:, 1, :]).then_inc(AC.sem, 1)
            act.wait_ge(DV.sem, DV.at(NCH - 1, "out"))
            for h in range(GLA_H):
                nc.scalar.activation(tmp[:, h, :], o[:, h, :], ACT.Square).then_inc(s_osq, 1)
            for h in range(GLA_H):
                act.wait_ge(s_oms, h + 1)
                nc.scalar.activation(tmp[:, h, :], tmp[:, h, :], ACT.Sqrt).then_inc(s_ort, 1)

        @block.gpsimd
        def _(pool):
            chain = Chain(pool, g.pool_steps)
            chain.step(nc.gpsimd.memset(wdec[:], 0.0))
            nc.gpsimd.nop().then_inc(s_zero, 1)
            for t in (qs, ks):
                chain.step(nc.gpsimd.memset(t[:], 0.0))
            chain.step(nc.gpsimd.memset(mraw[:], 0.0))
            chain.step(nc.gpsimd.memset(o, 0.0))
            nc.gpsimd.nop().then_inc(s_init, 1)
            PO.prime(nc.gpsimd.nop())
            pool.wait_ge(s_ends, 1)
            pool.wait_ge(s_eva, len(by_act))
            for it0, count, c0 in loops:
                if it0:
                    pool.wait_ge(s_ld, 64)
                with pool.Fori(0, count) as i:
                    it = i + it0
                    chunk = (pool.snap(i + c0), pool.snap(c0 + count - 1 - i))
                    col = (pool.snap((i + c0) * C), pool.snap((c0 + count - 1 - i) * C))
                    wait_apart(pool, DV.sem, DV.before(it, "mraw"), s_ends)
                    for d in range(2):
                        e = ends[:, d, 0, :, bass.ds(chunk[d], 1)].to_broadcast([P, PAIRS, GLA_DV])
                        last = nc.gpsimd.tensor_tensor(m0[:, d], mraw[:, d], e, ALU.mult)
                    last.then_inc(PO.sem, 1)
                    wait_apart(pool, PE.sem, PE.before(it, "vtok"), s_ends)
                    for d in range(2):
                        last = nc.gpsimd.tensor_copy(vs[:, d], v[:, :, bass.ds(col[d], C)])
                    last.then_inc(PO.sem, 1)

        @block.vector
        def _(dve):
            chain = Chain(dve, g.dve_steps)
            chain.step(nc.vector.memset(reset[:], 1.0))
            chain.step(nc.vector.memset(reset[:].rearrange("p (c t) -> p c t", t=C)[:, :, 0:1], 0.0))
            dve.wait_ge(s_ps, 1)
            nc.vector.tensor_copy(z[:].rearrange("p (a b) -> p a b", a=2),
                                  slot(0)[0:2 * GLA_RANK]).then_inc(s_evd, 1)
            dve.wait_ge(s_small, 16 * 6)
            for n in range(4):
                m = tiles.index(("dec", n))
                dve.wait_ge(s_eva, by_act.index(("dec", n)) + 1)
                nc.vector.tensor_scalar(xmin[:, n].rearrange("p (a b) -> p a b", a=2), slot(m),
                                        bdec[:, n // 2, n % 2:n % 2 + 1], 0.0, ALU.add,
                                        ALU.min).then_inc(s_evd, 1)
            dve.wait_ge(s_evd, 5)
            dve.wait_ge(s_ln, 1)
            for n in range(4):
                chain.step(nc.vector.tensor_tensor(xmin[:, n], xmin[:, n], tmp[:, n, :], ALU.subtract))
                log_decay_to_steps(nc, chain, dd[:, n // 2, n % 2], tmp[:, n, :], reset[:], xmin[:, n], C // 2 - 1)
            nc.vector.nop().then_inc(s_dd, 1)
            DV.prime(nc.vector.nop())
            dve.wait_ge(s_init, 1)
            dve.wait_ge(s_eva, len(by_act))
            for it0, count, c0 in loops:
                with dve.Fori(0, count) as i:
                    it = i + it0
                    chunk = (dve.snap(i + c0), dve.snap(c0 + count - 1 - i))
                    col = (dve.snap((i + c0) * C), dve.snap((c0 + count - 1 - i) * C))
                    for buf, src, name in ((ks, k, "exp_k"), (qs, q, "exp_q")):
                        dve.wait_ge(AC.sem, AC.at(it, name))
                        for d in range(2):
                            for h in range(2):
                                r = slice(64 * h, 64 * h + 64)
                                dst = buf[r, d, :, 64 * h:64 * h + 64]
                                last = nc.vector.tensor_tensor(dst, dst, src[r, :, bass.ds(col[d], C)], ALU.mult)
                        last.then_inc(DV.sem, 1)
                    dve.wait_ge(PE.sem, PE.at(it, "scores"))
                    dve.wait_ge(PE.sem, PE.before(it, "out"))
                    nc.vector.tensor_tensor(att[:], g.ps[:, 2, :].rearrange("p (d a b) -> p d a b", d=2, a=2),
                                            g.tri[:, :, 1:2, :].to_broadcast([P, 2, PAIRS, P]),
                                            ALU.mult).then_inc(DV.sem, 1)
                    dve.wait_ge(PE.sem, PE.at(it, "out"))
                    for d in range(2):
                        dst = o[:, :, bass.ds(col[d], C)]
                        src = g.ps[:, 3, 256 * d:256 * d + 256].rearrange("p (h t) -> p h t", t=C)
                        if d == 1:
                            dve.wait_ge(DV.sem, DV.at(it, "out_f"))
                        nc.vector.tensor_tensor(dst, dst, src, ALU.add).then_inc(DV.sem, 1)
                    dve.wait_ge(PE.sem, PE.at(it, "state"))
                    nc.vector.tensor_tensor(msum[:], m0[:],
                                            g.ps[:, 4, :].rearrange("p (d a b) -> p d a b", d=2, a=2),
                                            ALU.add).then_inc(DV.sem, 1)
                    dve.wait_ge(DV.sem, DV.at(it, "msum"))
                    for d in range(2):
                        e = ends[:, d, 1, :, bass.ds(chunk[d], 1)].to_broadcast([P, PAIRS, GLA_DV])
                        last = nc.vector.tensor_tensor(mraw[:, d], msum[:, d], e, ALU.mult)
                    last.then_inc(DV.sem, 1)
            for h in range(GLA_H):
                dve.wait_ge(s_orms, h + 1)
                nc.vector.tensor_scalar(tmp[:, h, :].rearrange("p (a b) -> p a b", a=2),
                                        g.ps[:, 2 * (h % 2):2 * (h % 2) + 2, 0:320], 1.0 / GLA_DV, EPS,
                                        ALU.mult, ALU.add).then_inc(s_oms, 1)
                dve.wait_ge(s_ort, h + 1)
                chain.step(nc.vector.reciprocal(tmp[:, h, :], tmp[:, h, :]))
                chain.step(nc.vector.tensor_tensor(o[:, h, :], o[:, h, :], tmp[:, h, :], ALU.mult))
                chain.step(nc.vector.scalar_tensor_tensor(o[:, h, :], o[:, h, :], ng[:, h:h + 1], gate[:, h, :],
                                                          ALU.mult, ALU.mult))


def halves(t):
    return t.rearrange("p (a b) -> p a b", a=2)


def stage_rwkv_inputs(nc, g, w, r):
    with ExitStack() as ctx:
        def sb(name, shape, dt=F32):
            return ctx.enter_context(nc.sbuf_tensor(name, shape, dt))

        def sem(name):
            return ctx.enter_context(nc.semaphore(name))

        RCOLS = 3 * RW + 2 * DECAY_RANK + AAA_RANK + GATE_RANK
        ZCOLS = RCOLS - 3 * RW
        tiles = [(n, i, P, b, i * P, b * RW + i * P) for b, n in enumerate("rkv") for i in range(HP)]
        tiles = [("zw", 0, P, 3, 0, 3 * RW), ("za", 0, AAA_RANK, 3, P, 3 * RW + P),
                 ("zg", 0, P, 3, P + AAA_RANK, 3 * RW + P + AAA_RANK)] + tiles
        blocks = [3, 0, 1, 2]
        NPAD = 3
        win = sb("rw_w", [P, 2, KD, 512])
        convrow = sb("rw_convrow", [9, RCOLS])
        conv = sb("rw_conv", [P, len(tiles), 9])
        params = sb("rw_params", [8, RW])
        cpad = sb("rw_cpad", [P, NPAD, CTX + 2])
        lpad = sb("rw_lpad", [P, NPAD, GRID_H + 2, GRID_W + 2])
        zw = sb("rw_zw", [P, TOK])
        za = sb("rw_za", [AAA_RANK, TOK])
        w2 = sb("rw_w2", [P, RW])
        a2 = sb("rw_a2", [AAA_RANK, RW])
        omk = sb("rw_omk", [P, HP])
        reset = sb("rw_reset", [P, TOK])
        sig = sb("rw_sig", [P, 2, TOK])
        cum = sb("rw_cum", [P, TOK])
        a = sb("rw_a", [P, 2, TOK])
        sq = sb("rw_sq", [P, 2, TOK])

        s_w = [sem("rw_s_w0"), sem("rw_s_w1")]
        s_small, s_pad, s_ps, s_ev = sem("rw_s_small"), sem("rw_s_pad"), sem("rw_s_ps"), sem("rw_s_ev")
        s_trow, s_prm, s_conv = sem("rw_s_trow"), sem("rw_s_prm"), sem("rw_s_conv")
        s_z, s_pd, s_sig, s_dd = sem("rw_s_z"), sem("rw_s_pd"), sem("rw_s_sig"), sem("rw_s_dd")
        s_pa, s_a, s_sq, s_pk, s_kk, s_rt = (sem("rw_s_pa"), sem("rw_s_a"), sem("rw_s_sq"), sem("rw_s_pk"),
                                             sem("rw_s_kk"), sem("rw_s_rt"))
        s_kd = sem("rw_s_kd")
        w_in = w["w_in"][0].rearrange("(k p) n -> p k n", p=P)
        dests = {"r": r.r, "k": r.k, "v": r.v}

        def dest(m):
            name, i, width = tiles[m][:3]
            return {"zw": zw[:], "za": za[:], "zg": r.zg[:]}[name] if name[0] == "z" else dests[name][:, i, :]

        def slot(n):
            return g.ps[:, 2 * (n % 4):2 * (n % 4) + 2, 0:TOK // 2]

        block = ctx.enter_context(nc.Block())

        @block.sync
        def _(sp):
            sp.dma_start(convrow[:], w["rwkv_conv"][0].rearrange("a b c -> (a b) c")).then_inc(s_small, 16)
            for n, name in enumerate(("rwkv_a0", "rwkv_k_k", "rwkv_k_a", "rwkv_r_k", "rwkv_ln_g", "rwkv_ln_b")):
                sp.dma_start(params[n:n + 1, :], w[name]).then_inc(s_small, 16)
            sp.dma_start(params[6:8, :], w["rwkv_w0"][0]).then_inc(s_small, 16)
            for n, b in enumerate(blocks):
                if n >= 2:
                    sp.wait_ge(s_ps, 3 if n == 2 else 3 + HP)
                width = ZCOLS if b == 3 else 512
                c0 = GLA_COLS + 512 * b
                sp.dma_start(win[:, n % 2, :, 0:width], w_in[:, :, c0:c0 + width]).then_inc(s_w[n % 2], 16)
                if n == 0:
                    sp.dma_start(w2[:], w["rwkv_w2"][0].rearrange("d r n -> (d r) n")).then_inc(s_small, 16)
                    sp.dma_start(a2[:], w["rwkv_a2"][0]).then_inc(s_small, 16)

        @block.gpsimd
        def _(pool):
            chain = Chain(pool, g.pool_steps)
            chain.step(nc.gpsimd.memset(cpad[:], 0.0))
            chain.step(nc.gpsimd.memset(lpad[:], 0.0))
            nc.gpsimd.nop().then_inc(s_pad, 1)

        @block.tensor
        def _(pe):
            pe.wait_ge(s_small, 16 * 10)
            for m, (_, _, width, _, _, c) in enumerate(tiles):
                nc.tensor.transpose(g.ps[0:width, 6, 9 * m:9 * m + 9], convrow[:, c:c + width], g.blocks[0:9, 0, 0:9])
            for n in range(HP):
                last = nc.tensor.transpose(g.ps[:, 7, 8 * n:8 * n + 8], params[:, n * P:(n + 1) * P],
                                           g.blocks[0:8, 0, 0:8])
            last.then_inc(s_trow, 1)
            for m, (name, i, width, b, c, _) in enumerate(tiles):
                n = blocks.index(b)
                if i == 0:
                    pe.wait_ge(s_w[n % 2], 16 * (n // 2 + 1))
                if m == 3:
                    pe.wait_ge(s_prm, 1)
                if m >= 4:
                    pe.wait_ge(s_ev, m - 3)
                for half in range(2):
                    for kt in range(KD):
                        last = nc.tensor.matmul(slot(m)[0:width, half], win[:, n % 2, kt, c:c + width],
                                                g.hT[:, kt, half * 320:half * 320 + 320],
                                                start=kt == 0, stop=kt == KD - 1)
                last.then_inc(s_ps, 1)
            pe.wait_ge(s_ev, len(tiles))
            pe.wait_ge(s_conv, 2)
            pe.wait_ge(s_z, 1)
            for n in range(2 * HP):
                if n < HP:
                    if n >= 2:
                        pe.wait_ge(s_kd, n - 1)
                    for half in range(2):
                        last = nc.tensor.matmul(slot(n % 2)[:, half], a2[:, n * P:(n + 1) * P],
                                                za[:, half * 320:half * 320 + 320], start=True, stop=True)
                    last.then_inc(s_pa, 1)
                if n >= 2:
                    pe.wait_ge(s_sig, n - 1)
                rows = slice(64 * (n // HP), 64 * (n // HP) + 64)
                for half in range(2):
                    last = nc.tensor.matmul(slot(2 + n % 2)[:, half], w2[rows, (n % HP) * P:(n % HP + 1) * P],
                                            zw[rows, half * 320:half * 320 + 320], start=True, stop=True)
                last.then_inc(s_pd, 1)
                if n < HP:
                    pe.wait_ge(s_sq, n + 1)
                    pe.wait_ge(s_a, n + 1)
                    for half in range(2):
                        last = nc.tensor.matmul(slot(n % 2)[:, half], g.blocks[:, 6, :],
                                                sq[:, n % 2, half * 320:half * 320 + 320], start=True, stop=True)
                    last.then_inc(s_pk, 1)

        @block.scalar
        def _(act):
            act.wait_ge(s_pad, 1)
            for m, (name, i, width, _, _, _) in enumerate(tiles):
                act.wait_ge(s_ps, m + 1)
                if m >= NPAD:
                    act.wait_ge(s_conv, m - NPAD + 1)
                b, s = m % NPAD, slice(0, width)
                nc.scalar.copy(cpad[s, b, 1:CTX + 1], slot(m)[s, 0, 0:CTX])
                nc.scalar.copy(lpad[s, b, 1:4, 1:GRID_W + 1],
                               slot(m)[s, 0, CTX:320].rearrange("p (y x) -> p y x", x=GRID_W))
                nc.scalar.copy(lpad[s, b, 4:9, 1:GRID_W + 1],
                               slot(m)[s, 1].rearrange("p (y x) -> p y x", x=GRID_W)).then_inc(s_ev, 1)
            act.wait_ge(s_conv, 3)
            nc.scalar.activation(zw[:], zw[:], ACT.Tanh).then_inc(s_z, 1)
            nc.scalar.activation(r.zg[:], r.zg[:], ACT.Sigmoid).then_inc(s_z, 1)
            act.wait_ge(s_conv, len(tiles))
            for n in range(2 * HP):
                if n < HP:
                    act.wait_ge(s_pa, n + 1)
                    if n >= 2:
                        act.wait_ge(s_kk, n - 1)
                        act.wait_ge(s_pk, n - 1)
                    nc.scalar.activation(halves(a[:, n % 2]), slot(n % 2), ACT.Sigmoid,
                                         bias=r.prm[:, n, 0:1]).then_inc(s_a, 1)
                    nc.scalar.activation(sq[:, n % 2], r.k[:, n, :], ACT.Square,
                                         scale=r.prm[:, n, 1:2]).then_inc(s_sq, 1)
                act.wait_ge(s_pd, n + 1)
                if n >= 2:
                    act.wait_ge(s_dd, n - 1)
                nc.scalar.activation(halves(sig[:, n % 2]), slot(2 + n % 2), ACT.Sigmoid,
                                     bias=r.prm[:, n % HP, 6 + n // HP:7 + n // HP]).then_inc(s_sig, 1)
                if n < HP:
                    act.wait_ge(s_kd, n + 1)
                    nc.scalar.activation(r.kk[:, n, :], r.kk[:, n, :], ACT.Sqrt).then_inc(s_rt, 1)
            act.wait_ge(s_dd, 2 * HP)
            for d in range(2):
                for n in range(2):
                    off, sign = ((0, -1.0), (C, 1.0))[n ^ d]
                    nc.scalar.activation(r.ends[:, d, n], r.dd[:, d, :, :, off], ACT.Exp, scale=sign * r.S)

        @block.vector
        def _(dve):
            chain = Chain(dve, g.dve_steps)
            chain.step(nc.vector.memset(reset[:], 1.0))
            chain.step(nc.vector.memset(reset[:].rearrange("p (c t) -> p c t", t=C)[:, :, 0:1], 0.0))
            dve.wait_ge(s_trow, 1)
            for m, (_, _, width, _, _, _) in enumerate(tiles):
                last = nc.vector.tensor_copy(conv[0:width, m, :], g.ps[0:width, 6, 9 * m:9 * m + 9])
            chain.step(last)
            chain.step(nc.vector.tensor_copy(r.prm[:], g.ps[:, 7, 0:8 * HP].rearrange("p (a b) -> p a b", b=8)))
            nc.vector.nop().then_inc(s_prm, 1)
            chain.step(nc.vector.tensor_scalar(omk[:], r.prm[:, :, 2], -1.0, 1.0, ALU.mult, ALU.add))
            for m, (_, _, width, _, _, _) in enumerate(tiles):
                dve.wait_ge(s_ev, m + 1)
                s, b = slice(0, width), m % NPAD
                out = dest(m)[s]
                lat = out[:, CTX:TOK].rearrange("p (y x) -> p y x", x=GRID_W)
                for tap in range(9):
                    y, x = tap // 3, tap % 3
                    src, wt = lpad[s, b, y:y + GRID_H, x:x + GRID_W], conv[s, m, tap:tap + 1]
                    if tap == 0:
                        chain.step(nc.vector.tensor_scalar(lat, src, wt, None, ALU.mult))
                    else:
                        chain.step(nc.vector.scalar_tensor_tensor(lat, src, wt, lat, ALU.mult, ALU.add))
                    if y == 1:
                        src = cpad[s, b, x:x + CTX]
                        if x == 0:
                            chain.step(nc.vector.tensor_scalar(out[:, 0:CTX], src, wt, None, ALU.mult))
                        else:
                            chain.step(nc.vector.scalar_tensor_tensor(out[:, 0:CTX], src, wt, out[:, 0:CTX],
                                                                      ALU.mult, ALU.add))
                nc.vector.nop().then_inc(s_conv, 1)
            for n in range(2 * HP):
                if n < HP:
                    dve.wait_ge(s_pk, n + 1)
                    nc.vector.tensor_scalar(halves(r.kk[:, n, :]), slot(n % 2), 1e-24, None,
                                            ALU.max).then_inc(s_kd, 1)
                    dve.wait_ge(s_rt, n + 1)
                    chain.step(nc.vector.reciprocal(r.kk[:, n, :], r.kk[:, n, :]))
                    chain.step(nc.vector.scalar_tensor_tensor(r.kk[:, n, :], r.k[:, n, :], r.prm[:, n, 1:2],
                                                              r.kk[:, n, :], ALU.mult, ALU.mult))
                    dve.wait_ge(s_a, n + 1)
                    chain.step(nc.vector.scalar_tensor_tensor(r.nb[:, n, :], r.kk[:, n, :], -1.0, a[:, n % 2],
                                                              ALU.mult, ALU.mult))
                    chain.step(nc.vector.tensor_scalar(a[:, n % 2], a[:, n % 2], r.prm[:, n, 2:3],
                                                       omk[:, n:n + 1], ALU.mult, ALU.add))
                    nc.vector.tensor_tensor(r.k[:, n, :], r.k[:, n, :], a[:, n % 2], ALU.mult).then_inc(s_kk, 1)
                dve.wait_ge(s_sig, n + 1)
                log_decay_to_steps(nc, chain, r.dd[:, n // HP, n % HP], cum[:], reset[:], sig[:, n % 2], C // 2 - 1)
                nc.vector.nop().then_inc(s_dd, 1)


def stage_rwkv_scan(nc, g, w, r):
    LV = 6
    y = g.oT[:, 4:8, :]
    ITS = NCH
    with ExitStack() as ctx:
        def sb(name, shape, dt=F32):
            return ctx.enter_context(nc.sbuf_tensor(name, shape, dt))

        def sem(name):
            return ctx.enter_context(nc.semaphore(name))

        D2 = range(2)
        big = g.hT[:].rearrange("p a b -> p (a b)")

        def room(at, d, width):
            return big[:, at + d * HP * width:at + (d + 1) * HP * width].rearrange("p (a b) -> p a b", a=HP)

        lq, pq, m0 = ([room(at, d, P) for d in D2] for at in (0, 1024, 2048))
        lqc, pqc, m0c = ([room(at, d, C) for d in D2] for at in (3072, 3584, 4096))
        ex = [sb(f"ex{d}", [P, 3, HP, C]) for d in D2]
        arc = [sb(f"arc{d}", [P, HP, 2, C]) for d in D2]
        a_ = [sb(f"ab{d}", [P, HP, P]) for d in D2]
        bk = [sb(f"bk{d}", [P, HP, 2, P]) for d in D2]
        vs = [sb(f"vs{d}", [P, HP, P]) for d in D2]
        btok = [sb(f"btok{d}", [P, HP, P]) for d in D2]
        ktok = [sb(f"ktok{d}", [P, HP, P]) for d in D2]
        vtok = [sb(f"vtok{d}", [P, HP, P]) for d in D2]
        vtokc = [sb(f"vtokc{d}", [P, HP, C]) for d in D2]
        pac = [sb(f"pac{d}", [P, HP, 2, C]) for d in D2]
        uw = [sb(f"uw{d}", [P, HP, 2, P]) for d in D2]
        uc = [sb(f"uc{d}", [P, HP, C]) for d in D2]
        G = [sb(f"G{d}", [P, HP, P]) for d in D2]
        T = [sb(f"T{d}", [P, HP, P]) for d in D2]
        TT = [sb(f"TT{d}", [P, HP, P]) for d in D2]
        ryc = [sb(f"ryc{d}", [P, HP, C]) for d in D2]
        mc = [sb(f"mc{d}", [P, HP, C]) for d in D2]
        states = [sb(f"states{d}", [P, HP, P]) for d in D2]
        identc = sb("identc", [P, C])
        upto = sb("upto", [P, 2, C])

        levels = [f"{x}{j}" for j in range(1, LV) for x in ("G", "TT", "T")][:-1]
        PE = [Steps(sem(f"rs_pe{d}"), "lq", "pq", "atok", "btok", "ktok", "vtok", "T0", "pv", *levels,
                    "uw", "ry", "psi", "y", "m") for d in D2]
        DV = [Steps(sem(f"rs_dv{d}"), "lq", "TT0a", "TT0", "pq", *[x for x in levels if x[0] == "G" or x[:2] == "TT"],
                    "ry", "psi", "ar", "bk", "y", "m") for d in D2]
        AC = [Steps(sem(f"rs_ac{d}"), "atok", "btok", "ktok", "vtok", "T0", "pv",
                    *[f"T{j}" for j in range(1, LV - 1)], "ex", "uw", "vs") for d in D2]
        PO = [Steps(sem(f"rs_po{d}"), "m0c", "m0") for d in D2]
        s_init, s_st, s_ld, s_tr, s_sc, s_bk = (sem("rs_init"), sem("rs_st"), sem("rs_ld"), sem("rs_tr"),
                                               sem("rs_sc"), sem("rs_bk"))

        def chunks(it):
            if isinstance(it, int) and it < CTX_CH:
                return it, CTX_CH - 1 - it
            return it, NCH - 1 + CTX_CH - it

        def over(eng, body, between):
            for it in range(CTX_CH):
                body(it, chunks(it), chunks(it + 1))
            between()
            with eng.Fori(0, ITS - 1 - CTX_CH) as i:
                at, nxt = chunks(i + CTX_CH), chunks(i + (CTX_CH + 1))
                body(i + CTX_CH, [eng.snap(c) for c in at], [eng.snap(c) for c in nxt])
            body(ITS - 1, chunks(ITS - 1), None)

        def nothing():
            pass

        def bank(d, n):
            return g.ps[:, 4 * d + n, :].rearrange("p (a b) -> p a b", a=HP)

        def bankc(d, n):
            return g.ps[:, 4 * d + n, 0:HP * C].rearrange("p (a b) -> p a b", a=HP)

        def spread(stacked):
            return stacked.unsqueeze(2).to_broadcast([P, HP, 2, C])

        def mask(m):
            return m.rearrange("p (x b) -> p x b", x=2).unsqueeze(1).to_broadcast([P, HP, 2, C])

        def wide(t):
            return t.rearrange("p a (x b) -> p a x b", x=2)

        ident = g.blocks[:, 0, :]
        idents = ident.unsqueeze(1).to_broadcast([P, HP, P])
        block = ctx.enter_context(nc.Block())

        @block.sync
        def _(sp):
            def heads(t, d):
                return t[0, 0, d].rearrange("(p e) v k -> e v p k", e=2)
            sp.wait_ge(s_init, 1)
            for d in D2:
                for e in range(2):
                    s = slice(64 * e, 64 * e + 64)
                    sp.dma_start(states[d][s, :, 64 * e:64 * e + 64], heads(w["state_rwkv"], d)[e]).then_inc(s_ld, 16)
            sp.wait_ge(s_sc, 4)
            for d in D2:
                for e in range(2):
                    s = slice(64 * e, 64 * e + 64)
                    sp.dma_start(heads(w["new_state_rwkv"], d)[e], states[d][s, :, 64 * e:64 * e + 64]).then_inc(s_st, 16)
            sp.wait_ge(s_st, 64)

        @block.gpsimd
        def _(pool):
            chain = Chain(pool, g.pool_steps)
            for d in D2:
                for t in (a_[d], bk[d], vs[d], uw[d], states[d], mc[d]):
                    chain.step(nc.gpsimd.memset(t[:], 0.0))
            chain.step(nc.gpsimd.memset(y, 0.0))
            chain.step(nc.gpsimd.tensor_tensor(identc[:], ident[:, 0:C], ident[:, C:P], ALU.add))
            for d in D2:
                incl = g.tri[:, d, 1, :]
                chain.step(nc.gpsimd.tensor_tensor(upto[:, d, :], incl[:, 0:C], incl[:, C:P], ALU.add))
            nc.gpsimd.nop().then_inc(s_init, 1)
            for d in D2:
                PO[d].prime(nc.gpsimd.nop())

            def body(it, at, nxt):
                for d in D2:
                    wait_apart(pool, DV[d].sem, DV[d].before(it, "m"), s_init)
                    wait_apart(pool, PE[d].sem, PE[d].before(it, "m"), s_init)
                    e = r.ends[:, d, 0, :, bass.ds(at[d], 1)].to_broadcast([P, HP, C])
                    chain_m0(d, nc.gpsimd.tensor_tensor(m0c[d], mc[d][:], e, ALU.mult), it)
                    nc.gpsimd.tensor_tensor(wide(m0[d]), spread(m0c[d]), mask(g.blocks[:, 6, :]),
                                            ALU.mult).then_inc(PO[d].sem, 1)

            def chain_m0(d, ins, it):
                ins.then_inc(PO[d].sem, 1)
                wait_apart(pool, PO[d].sem, PO[d].at(it, "m0c"), s_init)

            over(pool, body, lambda: pool.wait_ge(s_bk, 2))

        @block.scalar
        def _(act):
            def decays(it, nxt):
                for d in D2:
                    if it is not None:
                        wait_apart(act, DV[d].sem, DV[d].before(it, "bk"), s_init)
                    excl, incl, sign = ((0, 1, 1.0), (1, 0, -1.0))[d]
                    for n, (off, sg) in enumerate(((excl, sign), (incl, sign), (incl, -sign))):
                        src = r.dd[:, d, :, bass.ds(nxt[d], 1), off:off + C]
                        last = nc.scalar.activation(ex[d][:, n], src.rearrange("p a o t -> p a (o t)"),
                                                    ACT.Exp, scale=sg * r.S)
                    last.then_inc(AC[d].sem, 1)

            def values(nxt):
                for d in D2:
                    col = reg(act, nxt[d] * C)
                    for h in range(2):
                        s = slice(64 * h, 64 * h + 64)
                        last = nc.scalar.copy(vs[d][s, :, 64 * h:64 * h + 64], r.v[s, :, bass.ds(col, C)])
                    last.then_inc(AC[d].sem, 1)

            def on_diagonal(dst, src, d):
                for h in range(2):
                    s = slice(64 * h, 64 * h + 64)
                    last = nc.scalar.copy(dst[s, :, 64 * h:64 * h + 64], src[s])
                return last

            for d in D2:
                act.nop().then_inc(AC[d].sem, AC[d].names.index("ex"))
            act.wait_ge(s_init, 1)
            decays(None, chunks(0))
            for d in D2:
                act.wait_ge(AC[d].sem, AC[d].before(0, "ex"))
                act.nop().then_inc(AC[d].sem, 1)
            values(chunks(0))

            def body(it, at, nxt):
                def copy(name, dst, n, src=bank):
                    for d in D2:
                        act.wait_ge(PE[d].sem, PE[d].at(it, name))
                        nc.scalar.copy(dst(d), src(d, n)).then_inc(AC[d].sem, 1)

                copy("atok", lambda d: pac[d][:, :, 1, :], 2, bankc)
                copy("btok", lambda d: btok[d][:], 3)
                copy("ktok", lambda d: ktok[d][:], 0)
                for d in D2:
                    act.wait_ge(PE[d].sem, PE[d].at(it, "vtok"))
                    nc.scalar.copy(vtok[d][:], bank(d, 1))
                    for h in range(2):
                        s = slice(64 * h, 64 * h + 64)
                        last = nc.scalar.copy(vtokc[d][s], bank(d, 1)[s, :, 64 * h:64 * h + 64])
                    last.then_inc(AC[d].sem, 1)
                copy("T0", lambda d: T[d][:], 3)
                copy("pv", lambda d: pac[d][:, :, 0, :], 2, bankc)
                for j in range(1, LV - 1):
                    copy(f"T{j}", lambda d: T[d][:], 3)
                if nxt:
                    decays(it, nxt)
                else:
                    for d in D2:
                        act.wait_ge(AC[d].sem, AC[d].at(it, f"T{LV - 2}"))
                        act.nop().then_inc(AC[d].sem, 1)
                for d in D2:
                    act.wait_ge(PE[d].sem, PE[d].at(it, "uw"))
                    out = bank(d, 0).rearrange("p a (x b) -> p a x b", x=2)
                    for h in range(2):
                        s = slice(64 * h, 64 * h + 64)
                        nc.scalar.copy(uw[d][s, :, :, 64 * h:64 * h + 64], out[s])
                    nc.scalar.copy(uc[d][:], out[:, :, 0, :]).then_inc(AC[d].sem, 1)
                if nxt:
                    values(nxt)

            def switch():
                for d in D2:
                    act.wait_ge(DV[d].sem, DV[d].at(CTX_CH - 1, "m"))
                    on_diagonal(uw[d][:, :, 0, :], mc[d][:], d).then_inc(s_sc, 1)
                for d in D2:
                    act.wait_ge(s_tr, d + 1)
                    nc.scalar.copy(states[d][:], bank(d, 0)).then_inc(s_sc, 1)
                    for h in range(2):
                        s = slice(64 * h, 64 * h + 64)
                        last = nc.scalar.copy(mc[d][s], bank(d, 1)[s, :, 64 * h:64 * h + 64])
                    last.then_inc(s_bk, 1)

            over(act, body, switch)

        @block.vector
        def _(dve):
            def inputs(it, nxt):
                col = [reg(dve, nxt[d] * C) for d in D2]
                for d in D2:
                    if it is None:
                        dve.wait_ge(AC[d].sem, AC[d].before(0, "ex"))
                    else:
                        wait_apart(dve, DV[d].sem, DV[d].at(it, "ry"), s_init)
                        wait_apart(dve, AC[d].sem, AC[d].at(it, "ex"), s_init)
                    at = bass.ds(col[d], C)
                    for x, src in enumerate((r.kk, r.r)):
                        nc.vector.tensor_tensor(arc[d][:, :, x, :], ex[d][:, x], src[:, :, at], ALU.mult)
                    for h in range(2):
                        s = slice(64 * h, 64 * h + 64)
                        last = nc.vector.tensor_tensor(a_[d][s, :, 64 * h:64 * h + 64], ex[d][s, 0],
                                                       r.kk[s, :, at], ALU.mult)
                    last.then_inc(DV[d].sem, 1)
                    for x, src in enumerate((r.nb, r.k)):
                        for h in range(2):
                            s = slice(64 * h, 64 * h + 64)
                            last = nc.vector.tensor_tensor(bk[d][s, :, x, 64 * h:64 * h + 64], ex[d][s, 2],
                                                           src[s, :, at], ALU.mult)
                    last.then_inc(DV[d].sem, 1)

            for d in D2:
                dve.nop().then_inc(DV[d].sem, DV[d].names.index("ar"))
            dve.wait_ge(s_init, 1)
            inputs(None, chunks(0))
            for d in D2:
                dve.wait_ge(DV[d].sem, DV[d].before(0, "bk"))
                dve.nop().then_inc(DV[d].sem, 2)

            def body(it, at, nxt):
                def masked(name, dst, dstc, n):
                    for d in D2:
                        dve.wait_ge(PE[d].sem, PE[d].at(it, name))
                        out = wide(bank(d, n))
                        nc.vector.tensor_tensor(wide(dst[d]), spread(out[:, :, 0, :]), mask(g.tri[:, d, 0, :]),
                                                ALU.mult)
                        nc.vector.tensor_tensor(dstc[d], out[:, :, 1, :],
                                                upto[:, d:d + 1, :].to_broadcast([P, HP, C]),
                                                ALU.mult).then_inc(DV[d].sem, 1)

                masked("lq", lq, lqc, 0)
                for d in D2:
                    wait_apart(dve, DV[d].sem, DV[d].at(it, "lq"), s_init)
                    nc.vector.tensor_tensor(TT[d][:], lq[d], g.levels[:, 0:1, :].to_broadcast([P, HP, P]),
                                            ALU.mult).then_inc(DV[d].sem, 1)
                for d in D2:
                    wait_apart(dve, DV[d].sem, DV[d].at(it, "TT0a"), s_init)
                    nc.vector.tensor_tensor(TT[d][:], TT[d][:], idents, ALU.add).then_inc(DV[d].sem, 1)
                masked("pq", pq, pqc, 1)
                for j in range(1, LV):
                    for d in D2:
                        dve.wait_ge(PE[d].sem, PE[d].at(it, f"G{j}"))
                        nc.vector.tensor_tensor(G[d][:], bank(d, 1),
                                                g.levels[:, j:j + 1, :].to_broadcast([P, HP, P]),
                                                ALU.mult).then_inc(DV[d].sem, 1)
                    for d in D2:
                        dve.wait_ge(PE[d].sem, PE[d].at(it, f"TT{j}"))
                        nc.vector.tensor_tensor(TT[d][:], bank(d, 2), TT[d][:], ALU.add).then_inc(DV[d].sem, 1)
                for d in D2:
                    dve.wait_ge(PE[d].sem, PE[d].at(it, "ry"))
                    nc.vector.tensor_tensor(ryc[d][:], bankc(d, 2), arc[d][:, :, 1, :],
                                            ALU.add).then_inc(DV[d].sem, 1)
                for d in D2:
                    dve.wait_ge(PE[d].sem, PE[d].at(it, "psi"))
                    nc.vector.tensor_tensor(G[d][:], bank(d, 3), idents, ALU.add).then_inc(DV[d].sem, 1)
                if nxt:
                    inputs(it, nxt)
                else:
                    for d in D2:
                        dve.wait_ge(DV[d].sem, DV[d].at(it, "psi"))
                        dve.nop().then_inc(DV[d].sem, 2)
                col = [reg(dve, at[d] * C) for d in D2]
                for d in D2:
                    wait_apart(dve, PE[d].sem, PE[d].at(it, "y"), s_init)
                    dst = y[:, :, bass.ds(col[d], C)]
                    nc.vector.tensor_tensor(dst, dst, bankc(d, 0), ALU.add).then_inc(DV[d].sem, 1)
                    if d == 0:
                        dve.wait_ge(DV[0].sem, DV[0].at(it, "y"))
                    dve.wait_ge(PE[d].sem, PE[d].at(it, "m"))
                    e = r.ends[:, d, 1, :, bass.ds(at[d], 1)].to_broadcast([P, HP, C])
                    nc.vector.tensor_tensor(mc[d][:], bankc(d, 1), e, ALU.mult).then_inc(DV[d].sem, 1)

            over(dve, body, nothing)

        @block.tensor
        def _(pe):
            for d in D2:
                PE[d].prime(nc.tensor.nop())
            pe.wait_ge(s_init, 1)

            def body(it, at, nxt):
                def dv(name):
                    return lambda d: (DV[d].sem, DV[d].at(it, name))

                def dv_before(name):
                    return lambda d: (DV[d].sem, DV[d].before(it, name))

                def ac(name):
                    return lambda d: (AC[d].sem, AC[d].at(it, name))

                def product(name, n, lhsT, rhs, *waits, cols=P):
                    for d in D2:
                        for wait in waits:
                            pe.wait_ge(*wait(d))
                        out = bankc(d, n) if cols == C else bank(d, n)
                        for p in range(HP):
                            if rhs:
                                ins = nc.tensor.matmul(out[:, p], lhsT(d, p), rhs(d, p), start=True, stop=True)
                            else:
                                ins = nc.tensor.transpose(out[:, p], lhsT(d, p), ident)
                        ins.then_inc(PE[d].sem, 1)

                def both(t):
                    return lambda d, p: t[d][:, p].rearrange("p x b -> p (x b)")

                def one(t, x=None):
                    return (lambda d, p: t[d][:, p]) if x is None else (lambda d, p: t[d][:, p, x, :])

                product("lq", 0, one(bk, 0), both(arc), dv_before("y"))
                product("pq", 1, one(bk, 1), both(arc), dv_before("m"))
                product("atok", 2, one(a_), lambda d, p: identc[:], cols=C)
                product("btok", 3, one(bk, 0), None)
                product("ktok", 0, one(bk, 1), None, dv("lq"))
                product("vtok", 1, one(vs), None, dv("pq"), lambda d: (AC[d].sem, AC[d].before(it, "vs")))
                product("T0", 3, one(TT), None, ac("btok"), dv("TT0"))
                product("pv", 2, one(pq), one(vtokc), ac("vtok"), cols=C)
                for j in range(1, LV):
                    product(f"G{j}", 1, one(lq), one(T), ac(f"T{j - 1}" if j > 1 else "pv"))
                    product(f"TT{j}", 2, one(G), one(TT), dv(f"G{j}"))
                    if j < LV - 1:
                        product(f"T{j}", 3, one(TT), None, dv(f"TT{j}"))
                product("uw", 0, one(TT), both(pac), dv(f"TT{LV - 1}"))
                product("ry", 2, one(uw, 1), one(lqc), ac("uw"), cols=C)
                product("psi", 3, one(uw, 1), one(btok))
                for d in D2:
                    pe.wait_ge(*dv("ry")(d))
                    pe.wait_ge(PO[d].sem, PO[d].at(it, "m0"))
                    for p in range(HP):
                        out = bankc(d, 0)[:, p]
                        nc.tensor.matmul(out, vtok[d][:, p], pqc[d][:, p], start=True, stop=False)
                        nc.tensor.matmul(out, uw[d][:, p, 0, :], lqc[d][:, p], start=False, stop=False)
                        ins = nc.tensor.matmul(out, m0[d][:, p], ryc[d][:, p], start=False, stop=True)
                    ins.then_inc(PE[d].sem, 1)
                for d in D2:
                    pe.wait_ge(*dv("psi")(d))
                    for p in range(HP):
                        out = bankc(d, 1)[:, p]
                        nc.tensor.matmul(out, ktok[d][:, p], vtokc[d][:, p], start=True, stop=False)
                        nc.tensor.matmul(out, btok[d][:, p], uc[d][:, p], start=False, stop=False)
                        ins = nc.tensor.matmul(out, G[d][:, p], m0c[d][:, p], start=False, stop=True)
                    ins.then_inc(PE[d].sem, 1)

            def switch():
                pe.wait_ge(s_ld, 64)
                for d in D2:
                    pe.wait_ge(s_sc, d + 1)
                    for p in range(HP):
                        nc.tensor.transpose(bank(d, 0)[:, p], uw[d][:, p, 0, :], ident)
                    for p in range(HP):
                        ins = nc.tensor.transpose(bank(d, 1)[:, p], states[d][:, p], ident)
                    ins.then_inc(s_tr, 1)
                pe.wait_ge(s_bk, 2)

            over(pe, body, switch)


def stage_rwkv_output(nc, g, w, r):
    y = g.oT[:, 4:8, :]
    with ExitStack() as ctx:
        def sb(name, shape, dt=F32):
            return ctx.enter_context(nc.sbuf_tensor(name, shape, dt))

        def sem(name):
            return ctx.enter_context(nc.semaphore(name))

        g2 = sb("ro_g2", [P, RW])
        sq = sb("ro_sq", [P, 2, TOK])
        rk = sb("ro_rk", [P, 2, TOK])
        std = sb("ro_std", [P, 2, TOK])
        s_g2, s_mean, s_ctr, s_sq, s_var, s_vd, s_rt = (sem("ro_g2"), sem("ro_mean"), sem("ro_ctr"), sem("ro_sq_"),
                                                       sem("ro_var"), sem("ro_vd"), sem("ro_rt"))
        s_rk, s_bon, s_done = sem("ro_rk_"), sem("ro_bon"), sem("ro_done")

        def slot(n):
            return g.ps[:, 2 * n:2 * n + 2, 0:TOK // 2]
        MEAN, VAR, BONUS, GATE = range(4)
        block = ctx.enter_context(nc.Block())

        @block.sync
        def _(sp):
            sp.dma_start(g2[:], w["rwkv_g2"][0]).then_inc(s_g2, 16)

        @block.tensor
        def _(pe):
            def over_heads(n, src, s_out):
                for half in range(2):
                    last = nc.tensor.matmul(slot(n)[:, half], g.blocks[:, 6, :], src[:, half * 320:half * 320 + 320],
                                            start=True, stop=True)
                last.then_inc(s_out, 1)

            pe.wait_ge(s_g2, 16)
            for n in range(HP):
                if n:
                    pe.wait_ge(s_done, n)
                over_heads(MEAN, y[:, n, :], s_mean)
                pe.wait_ge(s_sq, n + 1)
                over_heads(VAR, sq[:, n % 2], s_var)
                pe.wait_ge(s_rk, n + 1)
                for half in range(2):
                    nc.tensor.matmul(slot(GATE)[:, half], g2[:, n * P:(n + 1) * P],
                                     r.zg[:, half * 320:half * 320 + 320], start=True, stop=True)
                over_heads(BONUS, rk[:, n % 2], s_bon)

        @block.scalar
        def _(act):
            for n in range(HP):
                act.wait_ge(s_ctr, n + 1)
                nc.scalar.activation(sq[:, n % 2], y[:, n, :], ACT.Square).then_inc(s_sq, 1)
                act.wait_ge(s_vd, n + 1)
                nc.scalar.activation(std[:, n % 2], std[:, n % 2], ACT.Sqrt).then_inc(s_rt, 1)

        @block.vector
        def _(dve):
            chain = Chain(dve, g.dve_steps)
            for n in range(HP):
                yn, b = y[:, n, :], n % 2
                chain.step(nc.vector.scalar_tensor_tensor(rk[:, b], r.r[:, n, :], r.prm[:, n, 3:4], r.k[:, n, :],
                                                          ALU.mult, ALU.mult))
                nc.vector.nop().then_inc(s_rk, 1)
                dve.wait_ge(s_mean, n + 1)
                nc.vector.scalar_tensor_tensor(halves(yn), slot(MEAN), -1.0 / RN, halves(yn), ALU.mult,
                                               ALU.add).then_inc(s_ctr, 1)
                dve.wait_ge(s_var, n + 1)
                nc.vector.tensor_scalar(halves(std[:, b]), slot(VAR), 1.0 / RN, RWKV_LN_EPS, ALU.mult,
                                        ALU.add).then_inc(s_vd, 1)
                dve.wait_ge(s_rt, n + 1)
                chain.step(nc.vector.reciprocal(std[:, b], std[:, b]))
                chain.step(nc.vector.tensor_tensor(yn, yn, std[:, b], ALU.mult))
                chain.step(nc.vector.tensor_scalar(yn, yn, r.prm[:, n, 4:5], r.prm[:, n, 5:6], ALU.mult, ALU.add))
                dve.wait_ge(s_bon, n + 1)
                chain.step(nc.vector.tensor_tensor(halves(r.v[:, n, :]), halves(r.v[:, n, :]), slot(BONUS), ALU.mult))
                chain.step(nc.vector.tensor_tensor(yn, yn, r.v[:, n, :], ALU.add))
                nc.vector.tensor_tensor(halves(yn), halves(yn), slot(GATE), ALU.mult).then_inc(s_done, 1)
                dve.wait_ge(s_done, n + 1)


def stage_rwkv(nc, g, w):
    with ExitStack() as ctx:
        def sb(name, shape, dt=F32):
            return ctx.enter_context(nc.sbuf_tensor(name, shape, dt))
        r = Shared()
        r.S = -math.exp(-0.5)
        r.r, r.k, r.v = sb("r_r", [P, HP, TOK]), sb("r_k", [P, HP, TOK]), sb("r_v", [P, HP, TOK])
        r.kk, r.nb = sb("r_kk", [P, HP, TOK]), sb("r_nb", [P, HP, TOK])
        r.dd = sb("r_dd", [P, 2, HP, NCH, C + 1])
        r.ends = sb("r_ends", [P, 2, 2, HP, NCH])
        r.zg = sb("r_zg", [P, TOK])
        r.prm = sb("r_prm", [P, HP, 8])
        stage_rwkv_inputs(nc, g, w, r)
        stage_rwkv_scan(nc, g, w, r)
        stage_rwkv_output(nc, g, w, r)


BLK = P
MORE = (TOK * TOP_K) // (BLK + 1)
MORE += MORE % 2
NBLK = NE + MORE + 2
ROWS = TOK * TOP_K
U_MAIN, U_MORE = 4, 2


def stage_project_and_route(nc, g, w, m):
    with ExitStack() as ctx:
        def sb(name, shape, dt=F32):
            return ctx.enter_context(nc.sbuf_tensor(name, shape, dt))

        def sem(name):
            return ctx.enter_context(nc.semaphore(name))

        wout = sb("pr_wout", [P, KD, D])
        mod = sb("pr_mod", [P, 3, 2, D])
        w13 = sb("pr_w13", [P, KD, 2, FF])
        w2 = sb("pr_w2", [P, 2, D])
        wr = sb("pr_wr", [P, KD, NE])
        br = sb("pr_br", [P, NE])
        tmp = sb("pr_tmp", [P, 2, D])
        h2 = sb("pr_h2", [P, 2, D])
        ss, rms, rstd = sb("pr_ss", [P, NT]), sb("pr_rms", [P, NT]), sb("pr_rstd", [P, NT])
        s1 = sb("pr_s1", [P, 2, 2, FF])
        act1 = sb("pr_act1", [P, 2, FF])
        aT = sb("pr_aT", [P, 2, 2, P])
        scores, sel, selm = (sb("pr_scores", [P, NT, NE]), sb("pr_sel", [P, NT, NE]), sb("pr_selm", [P, NT, NE]))
        top = sb("pr_top", [P, NT, NG, 8])
        gs, gv, gif = sb("pr_gs", [P, NT, NG]), sb("pr_gv", [P, NT, 8]), sb("pr_gif", [P, NT, 8])
        gi, ti = sb("pr_gi", [P, NT, 8], U32), sb("pr_ti", [P, NT, 8], U32)
        geq, gmask = sb("pr_geq", [P, NT, NG]), sb("pr_gmask", [P, NT, NG])
        tv, tif = sb("pr_tv", [P, NT, 8]), sb("pr_tif", [P, NT, 8])
        room = [wout[:].rearrange("p k d -> p (k d)")[:, n * TOP_K * NT * NE:(n + 1) * TOP_K * NT * NE]
                for n in range(3)]
        eq, pick = (v.rearrange("p (k c) -> p k c", k=TOP_K) for v in room[:2])
        emore = room[2][:, 0:MORE * NE].rearrange("p (o e) -> p o e", e=NE)
        M = sb("pr_M", [P, NT, NE])
        wsum = sb("pr_wsum", [P, NT])
        iotai, iota = sb("pr_iotai", [P, NE], I32), sb("pr_iota", [P, NE])
        iotam = sb("pr_iotam", [P, MORE])
        before = sb("pr_before", [P, P])
        rowid = sb("pr_rowid", [P, TOP_K, NT], I32)
        empty = sb("pr_empty", [P, NBLK], I32)
        rank, q, blk, inblk = (sb("pr_rank", [P, NT, NE]), sb("pr_q", [P, NT, NE]), sb("pr_blk", [P, NT, NE]),
                               sb("pr_inblk", [P, NT, NE]))
        cnt, more, upto = sb("pr_cnt", [P, NE]), sb("pr_more", [P, NE]), sb("pr_upto", [P, NE])
        eblk = sb("pr_eblk", [P, NE])
        trow, trowi = sb("pr_trow", [P, TOP_K, NT]), sb("pr_trowi", [P, TOP_K, NT], U32)
        emf, nmf = sb("pr_emf", [P, MORE]), sb("pr_nmf", [P, 1])

        s_wout, s_x, s_mod, s_sh, s_rt, s_const = (sem("pr_s_wout"), sem("pr_s_x"), sem("pr_s_mod"), sem("pr_s_sh"),
                                                   sem("pr_s_rt"), sem("pr_s_const"))
        s_o, s_x1, s_sq, s_ms, s_sqrt, s_h2, s_h2st = (sem("pr_s_o"), sem("pr_s_x1"), sem("pr_s_sq"), sem("pr_s_ms"),
                                                       sem("pr_s_sqrt"), sem("pr_s_h2"), [sem("pr_s_h2st0"), sem("pr_s_h2st1")])
        s_tr, s_h2T, s_log, s_sc = sem("pr_s_tr"), sem("pr_s_h2T"), sem("pr_s_log"), sem("pr_s_sc")
        s_h13, s_silu, s_mul, s_at, s_aT, s_y, s_ysh = (sem("pr_s_h13"), sem("pr_s_silu"), sem("pr_s_mul"),
                                                        sem("pr_s_at"), sem("pr_s_aT"), sem("pr_s_y"), sem("pr_s_ysh"))
        s_M, s_rank, s_rows, s_zero, s_tab, s_back = (sem("pr_s_M"), sem("pr_s_rank"), sem("pr_s_rows"),
                                                      sem("pr_s_zero"), sem("pr_s_tab"), sem("pr_s_back"))
        h2T, ysh = g.hT, g.oT[:].rearrange("p a b -> p (a b)").rearrange("p (t d) -> p t d", d=D)
        block = ctx.enter_context(nc.Block())

        @block.sync
        def _(sp):
            sp.dma_start(wout[:, :, 0:512],
                         w["w_out"][0, :, 0:512].rearrange("(k p) n -> p k n", p=P)).then_inc(s_wout, 16)
            sp.dma_start(wout[:, :, 512:D],
                         w["w_out"][0, :, 512:D].rearrange("(k p) n -> p k n", p=P)).then_inc(s_wout, 16)
            sp.dma_start(m.x[:, 0, :], w["x_prompt"][0]).then_inc(s_x, 16)
            sp.dma_start(m.x[:, 1:NT, :], w["x_sample"][0].rearrange("(t p) d -> p t d", p=P)).then_inc(s_x, 16)
            for n, part in enumerate((2, 3, 4)):
                for s in range(2):
                    sp.dma_start(mod[:, n, s], g.mod_dram[s:s + 1, part * D:(part + 1) * D].to_broadcast([P, D])
                                 ).then_inc(s_mod, 16)
            sp.dma_start(wr[:], w["router_w"][0].rearrange("(p k) e -> p k e", k=KD)).then_inc(s_rt, 16)
            sp.dma_start(br[:], w["router_b"].to_broadcast([P, NE])).then_inc(s_rt, 16)
            sp.dma_start(w13[:, :, 0, :], w["sh_w1"][0].rearrange("(p k) f -> p k f", k=KD)).then_inc(s_sh, 16)
            sp.dma_start(w13[:, :, 1, :], w["sh_w3"][0].rearrange("(p k) f -> p k f", k=KD)).then_inc(s_sh, 16)
            sp.dma_start(w2[:], w["sh_w2"][0].rearrange("(p j) d -> p j d", j=2)).then_inc(s_sh, 16)
            for t in range(NT):
                sp.wait_ge(s_h2, t + 1)
                sp.dma_start(m.h_dram[t * P:(t + 1) * P, :], h2[:, t % 2]).then_inc(s_h2st[t % 2], 16)
            for b in range(2):
                sp.wait_ge(s_h2st[b], 16 * ((NT + 1 - b) // 2))
            sp.wait_ge(s_tab, 16 * TOP_K * NT)
            sp.dma_start(m.rows[:], m.tab_dram.rearrange("(p b) o -> p (b o)", p=P)).then_inc(s_back, 16)

        @block.gpsimd
        def _(pool):
            chain = Chain(pool, g.pool_steps)
            chain.step(nc.gpsimd.memset(empty[:], ROWS + TOP_K - 1))
            pool.dma_start(m.tab_dram.rearrange("(p b) o -> p (b o)", p=P), empty[:]).then_inc(s_zero, 16)
            chain.step(nc.gpsimd.iota(iotai[:], pattern=[[1, NE]], base=0, channel_multiplier=0))
            chain.step(nc.gpsimd.iota(rowid[:], pattern=[[1, TOP_K], [P * TOP_K, NT]], base=0,
                                      channel_multiplier=TOP_K))
            chain.step(nc.gpsimd.affine_select(out=before[:], in_=g.ones[:], compare_op=ALU.is_ge, fill=0.0,
                                               base=-1, pattern=[[1, P]], channel_multiplier=-1))
            nc.gpsimd.nop().then_inc(s_const, 1)
            for t in range(NT):
                pool.wait_ge(s_silu, t + 1)
                if t >= 2:
                    pool.wait_ge(s_at, t - 1)
                def split(v):
                    return v.rearrange("p (a j) -> p a j", j=2)
                nc.gpsimd.tensor_tensor(act1[:, t % 2].rearrange("p (j a) -> p a j", j=2), split(s1[:, t % 2, 0]),
                                        split(s1[:, t % 2, 1]), ALU.mult).then_inc(s_mul, 1)
            pool.wait_ge(s_zero, 16)
            pool.wait_ge(s_rows, 1)
            for k in range(TOP_K):
                for t in range(NT):
                    nc.gpsimd.indirect_dma_start(
                        out=m.tab_dram, out_offset=bass.IndirectOffsetOnAxis(ap=trowi[:, k, t:t + 1], axis=0),
                        in_=rowid[:, k, t:t + 1], in_offset=None).then_inc(s_tab, 16)

        @block.tensor
        def _(pe):
            for t in range(NT):
                if t >= 2:
                    pe.wait_ge(s_x1, t - 1)
                for n in range(2):
                    if t == 0:
                        pe.wait_ge(s_wout, 32)
                    for k in range(KD):
                        last = nc.tensor.matmul(g.ps[:, 2 * (t % 2) + n, :], g.oT[:, k, t * P:(t + 1) * P],
                                                wout[:, k, n * 512:(n + 1) * 512], start=k == 0, stop=k == KD - 1)
                last.then_inc(s_o, 1)
            for t in range(NT):
                pe.wait_ge(s_h2, t + 1)
                if t >= 1:
                    pe.wait_ge(s_h2T, t)
                for k in range(KD):
                    last = nc.tensor.transpose(g.ps[:, 4 + k // 4, (k % 4) * P:(k % 4 + 1) * P],
                                               h2[:, t % 2, k * P:(k + 1) * P], g.blocks[:, 0, :])
                last.then_inc(s_tr, 1)
            pe.wait_ge(s_h2T, NT)
            pe.wait_ge(s_rt, 32)
            for t in range(NT):
                for k in range(KD):
                    last = nc.tensor.matmul(g.ps[:, 6, t * NE:(t + 1) * NE], h2T[:, k, t * P:(t + 1) * P],
                                            wr[:, k, :], start=k == 0, stop=k == KD - 1)
            last.then_inc(s_log, 1)
            pe.wait_ge(s_sh, 48)
            for t in range(NT):
                if t >= 1:
                    pe.wait_ge(s_silu, t)
                for k in range(KD):
                    last = nc.tensor.matmul(g.ps[:, 7, :], h2T[:, k, t * P:(t + 1) * P],
                                            w13[:, k].rearrange("p a f -> p (a f)"), start=k == 0, stop=k == KD - 1)
                last.then_inc(s_h13, 1)
                if t == 2:
                    pe.wait_ge(s_M, 1)
                    for u in range(NT + 1):
                        out = g.ps[:, 5, u * NE:(u + 1) * NE]
                        for v in range(min(u, NT - 1) + 1):
                            last = nc.tensor.matmul(out, before[:] if v == u else g.ones[:], M[:, v, :],
                                                    start=v == 0, stop=v == min(u, NT - 1))
                    last.then_inc(s_rank, 1)
                pe.wait_ge(s_mul, t + 1)
                pe.wait_ge(s_aT, t)
                if t == 0:
                    pe.wait_ge(s_sc, 1)
                for j in range(2):
                    last = nc.tensor.transpose(g.ps[:, 4, j * P:(j + 1) * P], act1[:, t % 2, j * P:(j + 1) * P],
                                               g.blocks[:, 0, :])
                last.then_inc(s_at, 1)
                pe.wait_ge(s_aT, t + 1)
                if t == 0:
                    pe.wait_ge(s_x1, NT)
                if t >= 2:
                    pe.wait_ge(s_ysh, t - 1)
                for n in range(2):
                    for j in range(2):
                        last = nc.tensor.matmul(g.ps[:, 2 * (t % 2) + n, :], aT[:, t % 2, j],
                                                w2[:, j, n * 512:(n + 1) * 512], start=j == 0, stop=j == 1)
                last.then_inc(s_y, 1)

        @block.scalar
        def _(act):
            for t in range(NT):
                act.wait_ge(s_x1, t + 1)
                if t:
                    act.wait_ge(s_sq, t)
                nc.scalar.activation(s1[:].rearrange("p a b f -> p (a b f)"), m.x[:, t, :], ACT.Square,
                                     accum_out=ss[:, t:t + 1]).then_inc(s_sq, 1)
            act.wait_ge(s_ms, 1)
            nc.scalar.activation(rms[:], rms[:], ACT.Sqrt).then_inc(s_sqrt, 1)
            for t in range(NT):
                act.wait_ge(s_tr, t + 1)
                nc.scalar.copy(h2T[:, :, t * P:(t + 1) * P],
                               g.ps[:, 4:6, :].rearrange("p a (b c) -> p (a b) c", b=4)).then_inc(s_h2T, 1)
            act.wait_ge(s_log, 1)
            nc.scalar.activation(scores[:].rearrange("p t e -> p (t e)"), g.ps[:, 6, 0:NT * NE],
                                 ACT.Sigmoid).then_inc(s_sc, 1)
            for t in range(NT):
                act.wait_ge(s_h13, t + 1)
                if t >= 2:
                    act.wait_ge(s_mul, t - 1)
                nc.scalar.activation(s1[:, t % 2, 0], g.ps[:, 7, 0:FF], ACT.Silu)
                nc.scalar.copy(s1[:, t % 2, 1], g.ps[:, 7, FF:2 * FF]).then_inc(s_silu, 1)
                act.wait_ge(s_at, t + 1)
                if t >= 2:
                    act.wait_ge(s_y, t - 1)
                nc.scalar.copy(aT[:, t % 2].rearrange("p j a -> p (j a)"), g.ps[:, 4, 0:2 * P]).then_inc(s_aT, 1)
                act.wait_ge(s_y, t + 1)
                nc.scalar.copy(ysh[:, t, :], g.ps[:, 2 * (t % 2):2 * (t % 2) + 2, :]
                               .rearrange("p a b -> p (a b)")).then_inc(s_ysh, 1)

        @block.vector
        def _(dve):
            chain = Chain(dve, g.dve_steps)
            dve.wait_ge(s_x, 32)
            dve.wait_ge(s_mod, 96)
            for t in range(NT):
                dve.wait_ge(s_o, t + 1)
                chain.step(nc.vector.tensor_tensor(tmp[:, t % 2], g.ps[:, 2 * (t % 2):2 * (t % 2) + 2, :]
                                                   .rearrange("p a b -> p (a b)"), mod[:, 0, min(t, 1)], ALU.mult))
                nc.vector.tensor_tensor(m.x[:, t, :], m.x[:, t, :], tmp[:, t % 2], ALU.add).then_inc(s_x1, 1)
            dve.wait_ge(s_sq, NT)
            nc.vector.tensor_scalar(rms[:], ss[:], 1.0 / D, EPS, ALU.mult, ALU.add).then_inc(s_ms, 1)
            dve.wait_ge(s_sqrt, 1)
            chain.step(nc.vector.reciprocal(rstd[:], rms[:]))

            def split(v):
                return v.rearrange("p (a k) -> p a k", k=KD)
            for t in range(NT):
                s = min(t, 1)
                chain.step(nc.vector.scalar_tensor_tensor(tmp[:, t % 2], m.x[:, t, :], rstd[:, t:t + 1], mod[:, 2, s],
                                                          ALU.mult, ALU.mult))
                if t >= 2:
                    dve.wait_ge(s_tr, t - 1)
                    dve.wait_ge(s_h2st[t % 2], 16 * (t // 2))
                nc.vector.tensor_tensor(h2[:, t % 2].rearrange("p (k a) -> p a k", k=KD), split(tmp[:, t % 2]),
                                        split(mod[:, 1, s]), ALU.add).then_inc(s_h2, 1)
            dve.wait_ge(s_const, 1)
            chain.step(nc.vector.tensor_copy(iota[:], iotai[:]))
            dve.wait_ge(s_sc, 1)
            dve.wait_ge(s_rt, 32)
            chain.step(nc.vector.tensor_tensor(sel[:], scores[:], br[:].unsqueeze(1).to_broadcast([P, NT, NE]), ALU.add))
            for t in range(NT):
                for n in range(NG):
                    last = nc.vector.max(top[:, t, n, :], sel[:, t, n * 8:(n + 1) * 8])
            chain.step(last)
            chain.step(nc.vector.tensor_tensor(gs[:], top[:, :, :, 0], top[:, :, :, 1], ALU.add))
            for t in range(NT):
                last = nc.vector.max(gv[:, t, :], gs[:, t, :])
            chain.step(last)
            for t in range(NT):
                last = nc.vector.max_index(gi[:, t, :], gv[:, t, :], gs[:, t, :])
            chain.step(last)
            chain.step(nc.vector.tensor_copy(gif[:], gi[:]))
            group = iota[:, 0:NG].unsqueeze(1).to_broadcast([P, NT, NG])
            chain.step(nc.vector.tensor_tensor(gmask[:], gif[:, :, 0:1].to_broadcast([P, NT, NG]), group, ALU.is_equal))
            for j in range(1, TOPG):
                chain.step(nc.vector.tensor_tensor(geq[:], gif[:, :, j:j + 1].to_broadcast([P, NT, NG]), group,
                                                   ALU.is_equal))
                chain.step(nc.vector.tensor_tensor(gmask[:], gmask[:], geq[:], ALU.add))
            def by_group(v):
                return v.rearrange("p t (g e) -> p (t g) e", g=NG)
            def over(v):
                return v.rearrange("p t g -> p (t g)").unsqueeze(2).to_broadcast([P, NT * NG, NE // NG])
            chain.step(nc.vector.tensor_tensor(by_group(selm[:]), by_group(sel[:]), over(gmask[:]), ALU.mult))
            chain.step(nc.vector.tensor_scalar(geq[:], gmask[:], 1e30, -1e30, ALU.mult, ALU.add))
            chain.step(nc.vector.tensor_tensor(by_group(selm[:]), by_group(selm[:]), over(geq[:]), ALU.add))
            for t in range(NT):
                last = nc.vector.max(tv[:, t, :], selm[:, t, :])
            chain.step(last)
            for t in range(NT):
                last = nc.vector.max_index(ti[:, t, :], tv[:, t, :], selm[:, t, :])
            chain.step(last)
            chain.step(nc.vector.tensor_copy(tif[:], ti[:]))
            for k in range(TOP_K):
                last = nc.vector.tensor_tensor(eq[:, k].rearrange("p (t e) -> p t e", e=NE),
                                               tif[:, :, k:k + 1].to_broadcast([P, NT, NE]),
                                               iota[:].unsqueeze(1).to_broadcast([P, NT, NE]), ALU.is_equal)
            chain.step(last)
            nc.vector.tensor_reduce(M[:].rearrange("p t e -> p (t e)"), eq.rearrange("p k c -> p c k"), AX,
                                    ALU.add).then_inc(s_M, 1)

            def choose(out, table):
                chain.step(nc.vector.tensor_tensor(pick, eq, table.rearrange("p t e -> p (t e)").unsqueeze(1)
                                                   .to_broadcast([P, TOP_K, NT * NE]), ALU.mult))
                chain.step(nc.vector.tensor_reduce(out, pick.rearrange("p k (t e) -> p (k t) e", e=NE), AX, ALU.add))

            choose(m.wts[:].rearrange("p k t -> p (k t)"), scores[:])
            chain.step(nc.vector.tensor_reduce(wsum[:], m.wts[:].rearrange("p k t -> p t k"), AX, ALU.add))
            chain.step(nc.vector.reciprocal(wsum[:], wsum[:]))
            chain.step(nc.vector.scalar_tensor_tensor(m.wts[:], m.wts[:], ROUTED_SCALE,
                                                      wsum[:].unsqueeze(1).to_broadcast([P, TOP_K, NT]),
                                                      ALU.mult, ALU.mult))
            dve.wait_ge(s_rank, 1)
            chain.step(nc.vector.tensor_copy(rank[:].rearrange("p t e -> p (t e)"), g.ps[:, 5, 0:NT * NE]))
            chain.step(nc.vector.tensor_copy(cnt[:], g.ps[:, 5, NT * NE:(NT + 1) * NE]))
            chain.step(nc.vector.tensor_scalar(q[:], rank[:], float(BLK), None, ALU.is_ge))
            chain.step(nc.vector.tensor_scalar(more[:], cnt[:], float(BLK + 1), None, ALU.is_ge))
            for j in range(2, TOK // BLK):
                chain.step(nc.vector.scalar_tensor_tensor(q[:], rank[:], float(BLK * j), q[:], ALU.is_ge, ALU.add))
                chain.step(nc.vector.scalar_tensor_tensor(more[:], cnt[:], float(BLK * j + 1), more[:], ALU.is_ge,
                                                          ALU.add))
            chain.step(nc.vector.scalar_tensor_tensor(inblk[:], q[:], -float(BLK), rank[:], ALU.mult, ALU.add))
            chain.step(nc.vector.tensor_tensor_scan(upto[:], g.ones[:, 0:NE], more[:], 0.0, ALU.mult, ALU.add))
            chain.step(nc.vector.tensor_tensor(eblk[:], upto[:], more[:], ALU.subtract))
            chain.step(nc.vector.scalar_tensor_tensor(eblk[:], eblk[:], float(NE - 1), iota[:], ALU.add, ALU.subtract))
            chain.step(nc.vector.tensor_scalar(blk[:], q[:], 1.0, None, ALU.min))
            chain.step(nc.vector.tensor_tensor(blk[:], blk[:], eblk[:].unsqueeze(1).to_broadcast([P, NT, NE]), ALU.mult))
            chain.step(nc.vector.tensor_tensor(blk[:], blk[:], q[:], ALU.add))
            chain.step(nc.vector.tensor_tensor(blk[:], blk[:], iota[:].unsqueeze(1).to_broadcast([P, NT, NE]), ALU.add))
            chain.step(nc.vector.scalar_tensor_tensor(q[:], inblk[:], float(NBLK), blk[:], ALU.mult, ALU.add))
            choose(trow[:].rearrange("p k t -> p (k t)"), q[:])
            chain.step(nc.vector.tensor_copy(trowi[:], trow[:]))
            nc.vector.nop().then_inc(s_rows, 1)
            chain.step(nc.vector.tensor_scalar(iotam[:], iota[:, 0:MORE], 1.0, None, ALU.mult))
            chain.step(nc.vector.tensor_tensor(emore, upto[:].unsqueeze(1).to_broadcast([P, MORE, NE]),
                                               iotam[:].unsqueeze(2).to_broadcast([P, MORE, NE]), ALU.is_le))
            chain.step(nc.vector.tensor_reduce(emf[:], emore, AX, ALU.add))
            chain.step(nc.vector.tensor_scalar(emf[:], emf[:], float(NE - 1), None, ALU.min))
            chain.step(nc.vector.tensor_copy(m.emore[:], emf[0:1, :]))
            chain.step(nc.vector.tensor_scalar(emf[:], iotam[:], 2.0, upto[:, NE - 1:NE], ALU.mult, ALU.is_lt))
            chain.step(nc.vector.tensor_reduce(nmf[:], emf[:], AX, ALU.add))
            chain.step(nc.vector.tensor_scalar(nmf[:], nmf[:], 1.0, None, ALU.max))
            chain.step(nc.vector.tensor_copy(m.pairs[:], nmf[0:1, :]))
            dve.wait_ge(s_back, 16)
            chain.step(nc.vector.tensor_scalar(m.toks[:], m.rows[:], int(math.log2(TOP_K)), None,
                                               ALU.logical_shift_right))


def stage_experts(nc, g, w, m):
    ALL = (NE, U_MAIN), (MORE, U_MORE)
    with ExitStack() as ctx:
        def sb(name, shape, dt=F32):
            return ctx.enter_context(nc.sbuf_tensor(name, shape, dt))

        def sem(name):
            return ctx.enter_context(nc.semaphore(name))

        B2 = range(2)
        w13 = [sb(f"ex_w13_{b}", [P, KD, 2, FF]) for b in B2]
        w2 = [sb(f"ex_w2_{b}", [P, 2, D]) for b in B2]
        ids = [sb(f"ex_ids{b}", [P, 1], I32) for b in B2]
        outs = [sb(f"ex_outs{b}", [P, 1], I32) for b in B2]
        xg = [sb(f"ex_xg{b}", [P, D]) for b in B2]
        xT = [sb(f"ex_xT{b}", [P, KD, P]) for b in B2]
        silu = [sb(f"ex_silu{b}", [P, FF]) for b in B2]
        hid = [sb(f"ex_hid{b}", [P, FF]) for b in B2]
        hT = [sb(f"ex_hT{b}", [P, 2, P]) for b in B2]
        yo = [sb(f"ex_y{b}", [P, D]) for b in B2]

        s_w13, s_w2, s_xg, s_st = ([sem(f"ex_s_{n}{b}") for b in B2] for n in ("w13", "w2", "xg", "st"))
        s_ids, s_outs, s_begun = sem("ex_s_ids"), sem("ex_s_outs"), sem("ex_s_begun")
        names = ("xt", "xT0", "xT1", "up", "silu", "hid", "ht", "hT", "down", "y0", "y1")
        s = {n: sem(f"ex_{n}") for n in names}
        owner = {"xt": "pe", "up": "pe", "ht": "pe", "down": "pe", "xT0": "act", "silu": "act", "y0": "act",
                 "xT1": "dve", "hid": "dve", "hT": "dve", "y1": "dve"}

        def prime(eng, who):
            for n in names:
                if owner[n] == who:
                    eng.nop().then_inc(s[n], 2)

        def done(eng, name, n):
            eng.wait_ge(s[name], n + 3)

        def freed(eng, name, n):
            eng.wait_ge(s[name], n + 1)

        def landed(eng, sems, b, half, count=16):
            eng.wait_ge(sems[b], half * count + count)

        def loops(eng):
            yield NE // U_MAIN, U_MAIN, 0
            yield eng.value_load(m.pairs[0:1, 0:1], min_val=1, max_val=MORE // 2), U_MORE, NE

        block = ctx.enter_context(nc.Block())

        @block.sync
        def _(sp):
            def load_w2(n, b, src):
                freed(sp, "down", n)
                sp.dma_start(w2[b][:], src).then_inc(s_w2[b], 16)

            for bodies, U, n0 in loops(sp):
                with sp.Fori(0, bodies) as i:
                    for u in range(U):
                        n, b = i * U + (n0 + u), u % 2
                        if n0 == 0:
                            e = sp.snap(i * U + u)
                        else:
                            e = sp.value_load(m.emore[0:1, bass.ds(i * U + u, 1)], min_val=0, max_val=NE - 1)
                        src1 = w["exp_w1"][0, bass.ds(e, 1)].rearrange("o (p k) f -> p (o k) f", k=KD)
                        src3 = w["exp_w3"][0, bass.ds(e, 1)].rearrange("o (p k) f -> p (o k) f", k=KD)
                        src2 = w["exp_w2"][0, bass.ds(e, 1)].rearrange("o (p j) d -> p (o j) d", j=2)
                        freed(sp, "up", n)
                        sp.dma_start(w13[b][:, :, 0, :], src1).then_inc(s_w13[b], 16)
                        sp.dma_start(w13[b][:, :, 1, :], src3).then_inc(s_w13[b], 16)
                        if u:
                            load_w2(n - 1, 1 - b, src2_before)
                        src2_before = src2
                    load_w2(n, b, src2)

        @block.gpsimd
        def _(pool):
            def gather(n, col, b, wait=True):
                if wait:
                    freed(pool, "xt", n)
                nc.gpsimd.tensor_copy(ids[b][:], m.toks[:, col]).then_inc(s_ids, 1)
                if wait:
                    wait_apart(pool, s_ids, n + 1, s_begun)
                else:
                    pool.wait_ge(s_ids, n + 1)
                nc.gpsimd.indirect_dma_start(out=xg[b][:], out_offset=None, in_=m.h_dram,
                                             in_offset=bass.IndirectOffsetOnAxis(ap=ids[b][:, 0:1], axis=0),
                                             bounds_check=TOK - 1, oob_is_err=False).then_inc(s_xg[b], 16)

            def scatter(n, b):
                col = pool.snap(n)
                done(pool, "y0", n)
                done(pool, "y1", n)
                nc.gpsimd.tensor_copy(outs[b][:], m.rows[:, bass.ds(col, 1)]).then_inc(s_outs, 1)
                wait_apart(pool, s_outs, n + 3, s_begun)
                nc.gpsimd.indirect_dma_start(out=m.y_dram,
                                             out_offset=bass.IndirectOffsetOnAxis(ap=outs[b][:, 0:1], axis=0),
                                             in_=yo[b][:], in_offset=None,
                                             bounds_check=ROWS - 1, oob_is_err=False).then_inc(s_st[b], 16)

            for b in B2:
                nc.gpsimd.memset(xg[b][:], 0.0).then_inc(s_begun, 1)
            pool.wait_ge(s_begun, 2)
            pool.nop().then_inc(s_outs, 2)
            for b in B2:
                gather(b, slice(b, b + 1), b, wait=False)
            for bodies, U, n0 in loops(pool):
                with pool.Fori(0, bodies) as i:
                    for u in range(U):
                        n = i * U + (n0 + u)
                        gather(n + 2, bass.ds(pool.snap(n + 2), 1), u % 2)
                        if u:
                            scatter(n - 1, (u - 1) % 2)
                    scatter(n, (U - 1) % 2)
            for b in B2:
                pool.wait_ge(s_st[b], bodies * 16 + 16 * (NE // 2))

        @block.tensor
        def _(pe):
            prime(pe, "pe")

            def transposes(n, b, half):
                landed(pe, s_xg, b, half)
                done(pe, "xT0", n - 1)
                done(pe, "xT1", n - 1)
                for k in range(KD):
                    last = nc.tensor.transpose(g.ps[:, k // 4, (k % 4) * P:(k % 4 + 1) * P],
                                               xg[b][:, k * P:(k + 1) * P], g.blocks[:, 0, :])
                last.then_inc(s["xt"], 1)

            def down(n, b, half):
                done(pe, "hT", n)
                landed(pe, s_w2, b, half)
                done(pe, "y0", n - 1)
                done(pe, "y1", n - 1)
                for c in range(2):
                    for j in range(2):
                        last = nc.tensor.matmul(g.ps[:, 6 + c, :], hT[b][:, j], w2[b][:, j, c * 512:(c + 1) * 512],
                                                start=j == 0, stop=j == 1)
                last.then_inc(s["down"], 1)

            transposes(0, 0, 0)
            for bodies, U, n0 in loops(pe):
                with pe.Fori(0, bodies) as i:
                    for u in range(U):
                        n, b = i * U + (n0 + u), u % 2
                        half = i * (U // 2) + (n0 + u) // 2
                        done(pe, "xT0", n)
                        done(pe, "xT1", n)
                        landed(pe, s_w13, b, half, 32)
                        freed(pe, "hid", n)
                        for k in range(KD):
                            last = nc.tensor.matmul(g.ps[:, 2 + b, :], xT[b][:, k],
                                                    w13[b][:, k].rearrange("p a f -> p (a f)"),
                                                    start=k == 0, stop=k == KD - 1)
                        last.then_inc(s["up"], 1)
                        transposes(n + 1, 1 - b, i * (U // 2) + (n0 + u + 1) // 2)
                        if u:
                            down(n - 1, 1 - b, i * (U // 2) + (n0 + u - 1) // 2)
                        done(pe, "hid", n)
                        freed(pe, "hT", n)
                        for j in range(2):
                            last = nc.tensor.transpose(g.ps[:, 4 + b, j * P:(j + 1) * P],
                                                       hid[b][:, j * P:(j + 1) * P], g.blocks[:, 0, :])
                        last.then_inc(s["ht"], 1)
                    down(n, b, half)

        @block.scalar
        def _(act):
            prime(act, "act")

            def copy_xT(n, b):
                done(act, "xt", n)
                freed(act, "up", n)
                nc.scalar.copy(xT[b][:, 0:4].rearrange("p k a -> p (k a)"), g.ps[:, 0, :]).then_inc(s["xT0"], 1)

            def copy_y(n, b, half):
                done(act, "down", n)
                act.wait_ge(s_st[b], half * 16)
                nc.scalar.copy(yo[b][:, 0:512], g.ps[:, 6, :]).then_inc(s["y0"], 1)

            copy_xT(0, 0)
            for bodies, U, n0 in loops(act):
                with act.Fori(0, bodies) as i:
                    for u in range(U):
                        n, b = i * U + (n0 + u), u % 2
                        done(act, "up", n)
                        freed(act, "hid", n)
                        nc.scalar.activation(silu[b][:], g.ps[:, 2 + b, 0:FF], ACT.Silu).then_inc(s["silu"], 1)
                        copy_xT(n + 1, 1 - b)
                        if u:
                            copy_y(n - 1, 1 - b, i * (U // 2) + (n0 + u - 1) // 2)
                    copy_y(n, b, i * (U // 2) + (n0 + u) // 2)

        @block.vector
        def _(dve):
            prime(dve, "dve")

            def copy_xT(n, b):
                done(dve, "xt", n)
                freed(dve, "up", n)
                nc.vector.tensor_copy(xT[b][:, 4:8].rearrange("p k a -> p (k a)"), g.ps[:, 1, :]).then_inc(s["xT1"], 1)

            def copy_y(n, b, half):
                done(dve, "down", n)
                dve.wait_ge(s_st[b], half * 16)
                nc.vector.tensor_copy(yo[b][:, 512:D], g.ps[:, 7, :]).then_inc(s["y1"], 1)

            copy_xT(0, 0)
            for bodies, U, n0 in loops(dve):
                with dve.Fori(0, bodies) as i:
                    for u in range(U):
                        n, b = i * U + (n0 + u), u % 2
                        done(dve, "silu", n)
                        freed(dve, "ht", n)
                        nc.vector.tensor_tensor(hid[b][:].rearrange("p (j a) -> p a j", j=2),
                                                silu[b][:].rearrange("p (a j) -> p a j", j=2),
                                                g.ps[:, 2 + b, FF:2 * FF].rearrange("p (a j) -> p a j", j=2),
                                                ALU.mult).then_inc(s["hid"], 1)
                        copy_xT(n + 1, 1 - b)
                        if u:
                            copy_y(n - 1, 1 - b, i * (U // 2) + (n0 + u - 1) // 2)
                        done(dve, "ht", n)
                        freed(dve, "down", n)
                        nc.vector.tensor_copy(hT[b][:].rearrange("p j a -> p (j a)"),
                                              g.ps[:, 4 + b, 0:2 * P]).then_inc(s["hT"], 1)
                    copy_y(n, b, i * (U // 2) + (n0 + u) // 2)


def stage_combine(nc, g, w, m):
    with ExitStack() as ctx:
        def sb(name, shape, dt=F32):
            return ctx.enter_context(nc.sbuf_tensor(name, shape, dt))

        def sem(name):
            return ctx.enter_context(nc.semaphore(name))

        rows = sb("cb_rows", [P, 2, TOP_K, D])
        g2 = sb("cb_g2", [P, 2, D])
        nf = sb("cb_nf", [P, D])
        sq = sb("cb_sq", [P, D])
        ss, rms, rstd = sb("cb_ss", [P, NT]), sb("cb_rms", [P, NT]), sb("cb_rstd", [P, NT])
        s_row = [sem(f"cb_s_row{b}") for b in range(2)]
        s_acc, s_in, s_x, s_sq, s_ms, s_rt, s_out, s_st = (
            sem("cb_s_acc"), sem("cb_s_in"), sem("cb_s_x"), sem("cb_s_sq"), sem("cb_s_ms"), sem("cb_s_rt"),
            sem("cb_s_out"), sem("cb_s_st"))
        acc = g.oT[:].rearrange("p a b -> p (a b)").rearrange("p (t d) -> p t d", d=D)
        block = ctx.enter_context(nc.Block())

        @block.sync
        def _(sp):
            def load(t):
                if t >= 2:
                    sp.wait_ge(s_acc, TOP_K * (t - 1))
                sp.dma_start(rows[:, t % 2], m.y_dram[t * P * TOP_K:(t + 1) * P * TOP_K, :]
                             .rearrange("(p k) d -> p k d", k=TOP_K)).then_inc(s_row[t % 2], 16)

            load(0)
            load(1)
            for s in range(2):
                sp.dma_start(g2[:, s], g.mod_dram[s:s + 1, 5 * D:6 * D].to_broadcast([P, D])).then_inc(s_in, 16)
            sp.dma_start(nf[:], w["norm_f"].rearrange("(o d) -> o d", o=1).to_broadcast([P, D])).then_inc(s_in, 16)
            for t in range(NT):
                if t + 2 < NT:
                    load(t + 2)
                sp.wait_ge(s_out, t + 1)
                dst = w["y_prompt"][0] if t == 0 else w["y_sample"][0, (t - 1) * P:t * P, :]
                sp.dma_start(dst, m.x[:, t, :]).then_inc(s_st, 16)
            sp.wait_ge(s_st, 16 * NT)

        @block.vector
        def _(dve):
            chain = Chain(dve, g.dve_steps)
            dve.wait_ge(s_in, 48)

            def finish(t):
                dve.wait_ge(s_rt, t + 1)
                chain.step(nc.vector.reciprocal(rstd[:, t:t + 1], rms[:, t:t + 1]))
                nc.vector.scalar_tensor_tensor(m.x[:, t, :], m.x[:, t, :], rstd[:, t:t + 1], nf[:], ALU.mult,
                                               ALU.mult).then_inc(s_out, 1)
            for t in range(NT):
                for k in range(TOP_K):
                    n = t * TOP_K + k
                    if k == 0:
                        dve.wait_ge(s_row[t % 2], 16 * (t // 2 + 1))
                    else:
                        dve.wait_ge(s_acc, n)
                    nc.vector.scalar_tensor_tensor(acc[:, t, :], rows[:, t % 2, k], m.wts[:, k, t:t + 1], acc[:, t, :],
                                                   ALU.mult, ALU.add).then_inc(s_acc, 1)
                dve.wait_ge(s_acc, (t + 1) * TOP_K)
                chain.step(nc.vector.tensor_tensor(acc[:, t, :], acc[:, t, :], g2[:, min(t, 1)], ALU.mult))
                nc.vector.tensor_tensor(m.x[:, t, :], m.x[:, t, :], acc[:, t, :], ALU.add).then_inc(s_x, 1)
                dve.wait_ge(s_sq, t + 1)
                nc.vector.tensor_scalar(rms[:, t:t + 1], ss[:, t:t + 1], 1.0 / D, EPS, ALU.mult,
                                        ALU.add).then_inc(s_ms, 1)
                if t:
                    finish(t - 1)
            finish(NT - 1)

        @block.scalar
        def _(act):
            for t in range(NT):
                act.wait_ge(s_x, t + 1)
                if t:
                    act.wait_ge(s_sq, t)
                nc.scalar.activation(sq[:], m.x[:, t, :], ACT.Square, accum_out=ss[:, t:t + 1]).then_inc(s_sq, 1)
                act.wait_ge(s_ms, t + 1)
                nc.scalar.activation(rms[:, t:t + 1], rms[:, t:t + 1], ACT.Sqrt).then_inc(s_rt, 1)


def build(nc, w):
    with ExitStack() as ctx:
        def sb(name, shape, dt=F32):
            return ctx.enter_context(nc.sbuf_tensor(name, shape, dt))

        g, m = Shared(), Shared()
        g.dve_steps = Count(ctx.enter_context(nc.semaphore("dve_steps")))
        g.pool_steps = Count(ctx.enter_context(nc.semaphore("pool_steps")))
        g.act_steps = Count(ctx.enter_context(nc.semaphore("act_steps")))
        g.ps = ctx.enter_context(nc.psum_tensor("ps", [P, 8, 512], F32))
        g.blocks = sb("blocks", [P, 7, P])
        g.levels = sb("levels", [P, 6, P])
        g.tri = sb("tri", [P, 2, 2, P])
        g.ones = sb("ones", [P, P])
        g.hT = sb("hT", [P, KD, TOK])
        g.oT = sb("oT", [P, KD, TOK])
        g.mod_dram = nc.dram_tensor("mod_dram", [2, MOD], F32, kind="Internal").ap()
        m.h_dram = nc.dram_tensor("h_dram", [TOK, D], F32, kind="Internal").ap()
        m.tab_dram = nc.dram_tensor("tab_dram", [P * NBLK, 1], I32, kind="Internal").ap()
        m.y_dram = nc.dram_tensor("y_dram", [ROWS, D], F32, kind="Internal").ap()
        stage_modulation(nc, g, w)
        stage_gla(nc, g, w)
        stage_rwkv(nc, g, w)
        m.x = sb("x_res", [P, NT, D])
        m.rows = sb("rows", [P, NBLK], I32)
        m.toks = sb("toks", [P, NBLK], I32)
        m.wts = sb("wts", [P, TOP_K, NT])
        m.emore = sb("emore", [1, MORE], I32)
        m.pairs = sb("pairs", [1, 1], I32)
        stage_project_and_route(nc, g, w, m)
        stage_experts(nc, g, w, m)
        stage_combine(nc, g, w, m)


_INS = ['x_prompt', 'x_sample', 'c', 'state_gla', 'state_rwkv', 'c_ctx', 'ada_w', 'ada_b', 'norm1', 'norm2', 'norm_f',
        'w_in', 'w_out', 'gla_w_dec', 'gla_b_dec', 'gla_norm', 'rwkv_conv', 'rwkv_w2', 'rwkv_w0', 'rwkv_a2', 'rwkv_a0',
        'rwkv_g2', 'rwkv_k_k', 'rwkv_k_a', 'rwkv_r_k', 'rwkv_ln_g', 'rwkv_ln_b', 'router_w', 'router_b', 'exp_w1',
        'exp_w3', 'exp_w2', 'sh_w1', 'sh_w3', 'sh_w2']
_OUTS = [('y_prompt', (1, CTX, D)), ('y_sample', (1, LAT, D)), ('new_state_gla', (1, 1, 2, GLA_H, GLA_DK, GLA_DV)),
         ('new_state_rwkv', (1, 1, 2, RH, RN, RN))]


def kernel(**inputs):
    import numpy as _np
    import concourse.bacc as _bacc
    from concourse.bass_utils import run_bass_kernel_spmd as _run

    nc = _bacc.Bacc("TRN2", target_bir_lowering=False, num_devices=1)
    arrays, w = {}, {}
    for name in _INS:
        a = _np.ascontiguousarray(inputs[name])
        arrays[f"in_{name}_dram"] = a
        w[name] = nc.dram_tensor(f"in_{name}_dram", a.shape, F32, kind="ExternalInput").ap()
    for name, shape in _OUTS:
        w[name] = nc.dram_tensor(f"out_{name}_dram", shape, F32, kind="ExternalOutput").ap()
    build(nc, w)
    r = _run(nc, [arrays], core_ids=[0])
    return tuple(r.results[0][f"out_{name}_dram"] for name, _ in _OUTS)
```

```python
import math
from contextlib import ExitStack

import concourse.bass as bass
from concourse import mybir

ALU = mybir.AluOpType
ACT = mybir.ActivationFunctionType
AX = mybir.AxisListType.X
F32 = mybir.dt.float32
I32 = mybir.dt.int32
U32 = mybir.dt.uint32

P = 128
D = 1024
KD = D // P
CTX, LAT = 128, 512
TOK = CTX + LAT
NT = TOK // P
GRID_W, GRID_H = 64, LAT // 64
EPS = 1e-6
RWKV_LN_EPS = 64e-5
MOD = 6 * D
MOD_FIRST = 2 * D
C = 64
NCH = TOK // C
CTX_CH, LAT_CH = CTX // C, LAT // C

GLA_H, GLA_DK, GLA_DV, GLA_RANK = 4, 64, 128, 16
GLA_QK, GLA_W = GLA_H * GLA_DK, GLA_H * GLA_DV
GLA_COLS = 2 * GLA_QK + 2 * GLA_W + 2 * GLA_RANK
RH, RN = 8, 64
RW = RH * RN
DECAY_RANK, AAA_RANK, GATE_RANK = 64, 64, 128
ZCOLS = 2 * DECAY_RANK + AAA_RANK + GATE_RANK
HP = RH // 2

NE, TOP_K, NG, TOPG = 64, 8, 8, 4
FF = D // 4
ROUTED_SCALE = 2.5


class Count:

    def __init__(self, sem):
        self.sem, self.n = sem, 0


class Chain:

    def __init__(self, eng, count):
        self.eng, self.count = eng, count

    def step(self, ins):
        self.count.n += 1
        ins.then_inc(self.count.sem, 1)
        self.eng.wait_ge(self.count.sem, self.count.n)


class Shared:
    pass


def build_constants(nc, g, pool, chain):
    chain.step(nc.gpsimd.memset(g.ones[:], 1.0))
    for n in range(7):
        size = 1 << n
        m = g.blocks[:, n, :]
        v = m.rearrange("p (a b) -> p a b", b=size)
        chain.step(nc.gpsimd.memset(m, 1.0))
        chain.step(nc.gpsimd.affine_select(out=v, in_=v, compare_op=ALU.is_ge, fill=0.0, base=0,
                                           pattern=[[-size, P // size], [0, size]], channel_multiplier=1))
        chain.step(nc.gpsimd.affine_select(out=v, in_=v, compare_op=ALU.is_ge, fill=0.0, base=size - 1,
                                           pattern=[[size, P // size], [0, size]], channel_multiplier=-1))
    for n in range(6):
        chain.step(nc.gpsimd.tensor_tensor(g.levels[:, n, :], g.blocks[:, n + 1, :], g.blocks[:, n, :],
                                           ALU.subtract))
    for d in range(2):
        for kind in range(2):
            sign = 1 if d == 0 else -1
            chain.step(nc.gpsimd.affine_select(out=g.tri[:, d, kind, :], in_=g.blocks[:, 6, :],
                                               compare_op=ALU.is_ge, fill=0.0, base=kind - 1,
                                               pattern=[[sign, P]], channel_multiplier=-sign))


def stage_modulation(nc, g, w):
    NB, NBUF = MOD_FIRST // 512, 3
    with ExitStack() as ctx:
        def sb(name, shape, dt=F32):
            return ctx.enter_context(nc.sbuf_tensor(name, shape, dt))

        def sem(name):
            return ctx.enter_context(nc.semaphore(name))

        aw = sb("ada_w_sb", [P, NBUF, KD, 512])
        cT = sb("cT", [P, 2, KD])
        scT = g.scT
        modrow = sb("modrow", [2, MOD_FIRST])
        adab = sb("adab", [2, MOD_FIRST])
        nrm = sb("normrow", [2, D])
        x = sb("x_sb", [P, NT, D])
        sq = sb("sq", [P, D])
        ss = sb("ss", [P, NT])
        rms = sb("rms", [P, NT])
        rstd = sb("rstd", [P, NT])
        wb = sb("wb", [P, 2, D])
        shb = sb("shb", [P, 2, D])
        hx = sb("hx", [P, 2, D])

        s_c, s_rows, s_x = sem("m_c"), sem("m_rows"), sem("m_x")
        s_aw = [sem(f"m_aw{n}") for n in range(NBUF)]
        s_silu, s_mm, s_ev = sem("m_silu"), sem("m_mm"), sem("m_ev")
        s_mod, s_st, s_bc = sem("m_mod"), sem("m_st"), sem("m_bc")
        s_sq, s_ms, s_rt = sem("m_sq"), sem("m_ms"), sem("m_rt")
        s_hx, s_tr, s_hT = sem("m_hx"), sem("m_tr"), sem("m_hT")
        s_const = sem("m_const")

        ada = w["ada_w"][0].rearrange("(p k) n -> p k n", k=KD)
        block = ctx.enter_context(nc.Block())

        @block.sync
        def _(sp):
            sp.dma_start(cT[:, 0, :], w["c_ctx"].rearrange("(p k) -> p k", k=KD)).then_inc(s_c, 16)
            sp.dma_start(cT[:, 1, :], w["c"][0].rearrange("(p k) -> p k", k=KD)).then_inc(s_c, 16)
            for n in range(NB):
                if n >= NBUF:
                    sp.wait_ge(s_mm, n - NBUF + 1)
                sp.dma_start(aw[:, n % NBUF], ada[:, :, n * 512:(n + 1) * 512]).then_inc(s_aw[n % NBUF], 16)
            sp.wait_ge(s_mod, 1)
            sp.dma_start(g.mod_dram[:, 0:MOD_FIRST], modrow[:, :]).then_inc(s_st, 16)
            sp.wait_ge(s_st, 16)
            for s in range(2):
                sp.dma_start(wb[:, s], g.mod_dram[s:s + 1, D:2 * D].to_broadcast([P, D])).then_inc(s_bc, 16)
                sp.dma_start(shb[:, s], g.mod_dram[s:s + 1, 0:D].to_broadcast([P, D])).then_inc(s_bc, 16)

        @block.gpsimd
        def _(pool):
            for s in range(2):
                pool.dma_start(adab[s:s + 1, :], w["ada_b"][:, 0:MOD_FIRST]).then_inc(s_rows, 16)
                pool.dma_start(nrm[s:s + 1, :], w["norm1"]).then_inc(s_rows, 16)
            build_constants(nc, g, pool, Chain(pool, g.pool_steps))
            nc.gpsimd.nop().then_inc(s_const, 1)

        @block.scalar
        def _(act):
            act.dma_start(x[:, 0, :], w["x_prompt"][0]).then_inc(s_x, 16)
            act.dma_start(x[:, 1:NT, :], w["x_sample"][0].rearrange("(t p) d -> p t d", p=P)).then_inc(s_x, 16)
            act.wait_ge(s_c, 32)
            nc.scalar.activation(scT[:].rearrange("p k s -> p s k"), cT[:], ACT.Silu).then_inc(s_silu, 1)
            act.wait_ge(s_x, 32)
            for t in range(NT):
                if t:
                    act.wait_ge(s_sq, t)
                nc.scalar.activation(sq[:], x[:, t, :], ACT.Square, accum_out=ss[:, t:t + 1]).then_inc(s_sq, 1)
            act.wait_ge(s_ms, 1)
            nc.scalar.activation(rms[:], rms[:], ACT.Sqrt).then_inc(s_rt, 1)
            for t in range(NT):
                for half in range(2):
                    n = 2 * t + half
                    act.wait_ge(s_tr, n + 1)
                    nc.scalar.copy(g.hT[:, 4 * half:4 * half + 4, t * P:(t + 1) * P],
                                   g.ps[:, 4 + n % 4, :].rearrange("p (k m) -> p k m", k=4)).then_inc(s_hT, 1)

        @block.vector
        def _(dve):
            chain = Chain(dve, g.dve_steps)
            dve.wait_ge(s_rows, 16 * 4)
            for n in range(NB):
                dve.wait_ge(s_mm, n + 1)
                nc.vector.tensor_tensor(modrow[:, n * 512:(n + 1) * 512], g.ps[0:2, n % 4, :],
                                        adab[:, n * 512:(n + 1) * 512], ALU.add).then_inc(s_ev, 1)
            dve.wait_ge(s_ev, NB)
            row = modrow[:, D:2 * D]
            chain.step(nc.vector.scalar_tensor_tensor(row, row, 1.0, nrm[:], ALU.add, ALU.mult))
            nc.vector.nop().then_inc(s_mod, 1)
            dve.wait_ge(s_sq, NT)
            nc.vector.tensor_scalar(rms[:], ss[:], 1.0 / D, EPS, ALU.mult, ALU.add).then_inc(s_ms, 1)
            dve.wait_ge(s_rt, 1)
            chain.step(nc.vector.reciprocal(rstd[:], rms[:]))
            dve.wait_ge(s_bc, 64)
            for t in range(NT):
                s = min(t, 1)
                if t >= 2:
                    dve.wait_ge(s_tr, 2 * (t - 1))
                chain.step(nc.vector.scalar_tensor_tensor(hx[:, t % 2], x[:, t, :], rstd[:, t:t + 1], wb[:, s],
                                                          ALU.mult, ALU.mult))
                nc.vector.tensor_tensor(hx[:, t % 2], hx[:, t % 2], shb[:, s], ALU.add).then_inc(s_hx, 1)

        @block.tensor
        def _(pe):
            pe.wait_ge(s_silu, 1)
            for n in range(NB):
                pe.wait_ge(s_aw[n % NBUF], 16 * (n // NBUF + 1))
                if n >= 4:
                    pe.wait_ge(s_ev, n - 3)
                for k in range(KD):
                    last = nc.tensor.matmul(g.ps[0:2, n % 4, :], scT[:, k, :], aw[:, n % NBUF, k, :],
                                            start=k == 0, stop=k == KD - 1)
                last.then_inc(s_mm, 1)
            pe.wait_ge(s_const, 1)
            for t in range(NT):
                pe.wait_ge(s_hx, t + 1)
                for half in range(2):
                    n = 2 * t + half
                    if n >= 4:
                        pe.wait_ge(s_hT, n - 3)
                    for k in range(4):
                        kk = 4 * half + k
                        last = nc.tensor.transpose(g.ps[:, 4 + n % 4, k * P:(k + 1) * P],
                                                   hx[:, t % 2, kk * P:(kk + 1) * P], g.blocks[:, 0, :])
                    last.then_inc(s_tr, 1)


class Steps:

    def __init__(self, sem, *names):
        self.sem, self.names, self.n = sem, names, len(names)

    def prime(self, ins):
        ins.then_inc(self.sem, self.n)

    def before(self, it, name):
        return it * self.n + self.names.index(name) + 1

    def at(self, it, name):
        return it * self.n + self.n + self.names.index(name) + 1


def wait_apart(eng, sem, value, ready):
    value = reg(eng, value)
    eng.wait_ge(ready, 1)
    eng.wait_ge(sem, value)


def reg(eng, value):
    return value if isinstance(value, int) else eng.snap(value)


def log_decay_to_steps(nc, chain, dd, cum, reset, lw, mid):
    chain.step(nc.vector.tensor_tensor_scan(cum, reset, lw, 0.0, ALU.mult, ALU.add))
    cumc = cum.rearrange("p (c t) -> p c t", t=C)
    middle = cumc[:, :, mid:mid + 1]
    chain.step(nc.vector.tensor_tensor(dd[:, :, 1:C + 1], cumc, middle.to_broadcast([P, NCH, C]), ALU.subtract))
    chain.step(nc.vector.tensor_scalar(dd[:, :, 0:1], middle, -1.0, None, ALU.mult))


def stage_gla(nc, g, w):
    PAIRS, S = GLA_H // 2, 1.0 / 16.0
    with ExitStack() as ctx:
        def sb(name, shape, dt=F32):
            return ctx.enter_context(nc.sbuf_tensor(name, shape, dt))

        def sem(name):
            return ctx.enter_context(nc.semaphore(name))

        win = g.win
        wz = sb("gla_wz", [P, KD, 2 * GLA_RANK])
        wdec = sb("gla_wdec", [2 * GLA_RANK, 2, GLA_QK])
        bdec = sb("gla_bdec", [P, 2, PAIRS])
        ng = sb("gla_ng", [P, GLA_H])
        z = sb("gla_z", [2 * GLA_RANK, TOK])
        q = sb("gla_q", [P, PAIRS, TOK])
        k = sb("gla_k", [P, PAIRS, TOK])
        v = sb("gla_v", [P, GLA_H, TOK])
        gate = sb("gla_gate", [P, GLA_H, TOK])
        tmp = sb("gla_tmp", [P, 4, TOK])
        xmin = sb("gla_xmin", [P, 4, TOK])
        reset = sb("gla_reset", [P, TOK])
        dd = sb("gla_dd", [P, 2, PAIRS, NCH, C + 1])
        ends = sb("gla_ends", [P, 2, 2, PAIRS, NCH])
        qs = sb("gla_qs", [P, 2, PAIRS, P])
        ks = sb("gla_ks", [P, 2, PAIRS, P])
        vs = sb("gla_vs", [P, 2, GLA_H, C])
        ktok = sb("gla_ktok", [P, 2, PAIRS, P])
        vtok = sb("gla_vtok", [P, 2, PAIRS, P])
        att = sb("gla_att", [P, 2, PAIRS, P])
        m0 = sb("gla_m0", [P, 2, PAIRS, GLA_DV])
        mraw = sb("gla_mraw", [P, 2, PAIRS, GLA_DV])
        msum = sb("gla_msum", [P, 2, PAIRS, GLA_DV])
        o = g.oT[:, 0:GLA_H, :]

        tiles = [("z", 0)] + [("q", p) for p in range(2)] + [("k", p) for p in range(2)] + \
                [("dec", n) for n in range(4)] + [("v", h) for h in range(4)] + [("g", h) for h in range(4)]
        by_act = [t for t in tiles if t[0] in "qkvg" or t[0] == "dec"]
        by_dve = [t for t in tiles if t[0] in ("z", "dec")]
        s_w = g.s_win
        s_small, s_init, s_ps = sem("gla_s_small"), sem("gla_s_init"), sem("gla_s_ps")
        s_eva, s_evd, s_ln = sem("gla_s_eva"), sem("gla_s_evd"), sem("gla_s_ln")
        s_dd, s_ends = sem("gla_s_dd"), sem("gla_s_ends")
        s_st, s_ld, s_zero = sem("gla_s_st"), sem("gla_s_ld"), sem("gla_s_zero")
        s_osq, s_oms, s_ort, s_orms = sem("gla_s_osq"), sem("gla_s_oms"), sem("gla_s_ort"), sem("gla_s_orms")
        PE = Steps(sem("gla_pe"), "ktok", "vtok", "scores", "out", "state")
        DV = Steps(sem("gla_dv"), "ks", "qs", "att", "out_f", "out", "msum", "mraw")
        AC = Steps(sem("gla_ac"), "exp_k", "exp_q", "ktok", "vtok")
        PO = Steps(sem("gla_po"), "m0", "vs")
        loops = ((0, CTX_CH, 0), (CTX_CH, LAT_CH, CTX_CH))
        ada = w["ada_w"][0].rearrange("(p k) n -> p k n", k=KD)
        aw = [win[:, 1, 0:KD // 2], win[:, 1, KD // 2:KD]]
        adab, row = sb("gla_adab", [2, 512]), sb("gla_modrow", [2, 512])
        s_aw, s_row = [sem("gla_s_awa"), sem("gla_s_awb")], sem("gla_s_row")
        s_am = [sem("gla_s_ama"), sem("gla_s_amb")]
        s_av = sem("gla_s_av")

        def evacuated(eng, m):
            name = tiles[m]
            if name in by_act:
                eng.wait_ge(s_eva, by_act.index(name) + 1)
            if name in by_dve:
                eng.wait_ge(s_evd, by_dve.index(name) + 1)

        def slot(m):
            return g.ps[:, 2 * (m % 4):2 * (m % 4) + 2, 0:TOK // 2]

        w_in = w["w_in"][0].rearrange("(k p) n -> p k n", p=P)
        block = ctx.enter_context(nc.Block())

        @block.sync
        def _(sp):
            sp.dma_start(wz[:], w_in[:, :, GLA_COLS - 2 * GLA_RANK:GLA_COLS]).then_inc(s_small, 16)
            for d in range(2):
                sp.dma_start(bdec[:, d, :], w["gla_b_dec"][0, d].rearrange("(p c) -> c p", c=P), allow_slow_non_contiguous=True).then_inc(s_small, 16)
            sp.dma_start(ng[:], w["gla_norm"][0].rearrange("(h c) -> c h", c=P), allow_slow_non_contiguous=True).then_inc(s_small, 16)
            sp.wait_ge(s_zero, 1)
            for d in range(2):
                sp.dma_start(wdec[GLA_RANK * d:GLA_RANK * (d + 1), d, :], w["gla_w_dec"][0, d]).then_inc(s_small, 16)
            for b in range(3):
                if b == 2:
                    sp.wait_ge(s_ps, tiles.index(("k", 1)) + 1)
                sp.dma_start(win[:, b % 2], w_in[:, :, 512 * b:512 * (b + 1)]).then_inc(s_w[b % 2], 16)

            def cols(i):
                at = reg(sp, i * 512 + MOD_FIRST)
                return bass.ds(at, 512)

            sp.wait_ge(s_ps, tiles.index(("v", 3)) + 1)
            for half in range(2):
                sp.dma_start(aw[half], ada[:, half * 4:half * 4 + 4, cols(0)]).then_inc(s_aw[half], 16)
            sp.dma_start(adab[:], w["ada_b"][:, cols(0)].to_broadcast([2, 512])).then_inc(s_aw[1], 16)
            sp.wait_ge(s_ps, len(tiles))
            sp.dma_start(win[:, 0, :, 0:ZCOLS], w_in[:, :, GLA_COLS + 3 * RW:GLA_COLS + 3 * RW + ZCOLS]
                         ).then_inc(s_w[0], 16)
            sp.wait_ge(DV.sem, DV.at(CTX_CH - 1, "mraw"))
            for d in range(2):
                for p in range(PAIRS):
                    sp.dma_start(w["new_state_gla"][0, 0, d, 2 * p:2 * p + 2].rearrange("h k v -> (h k) v"),
                                 mraw[:, d, p, :]).then_inc(s_st, 16)
            sp.wait_ge(s_st, 16 * 4)
            for d in range(2):
                for p in range(PAIRS):
                    sp.dma_start(mraw[:, d, p, :],
                                 w["state_gla"][0, 0, d, 2 * p:2 * p + 2].rearrange("h k v -> (h k) v")).then_inc(s_ld, 16)
            with sp.Fori(0, LAT_CH - 1) as i:
                this, nxt = cols(i), cols(i + 1)
                for half in range(2):
                    wait_apart(sp, s_am[half], i + 2, s_ps)
                    sp.dma_start(aw[half], ada[:, half * 4:half * 4 + 4, nxt]).then_inc(s_aw[half], 16)
                wait_apart(sp, s_av, i + 2, s_ps)
                sp.dma_start(adab[:], w["ada_b"][:, nxt].to_broadcast([2, 512])).then_inc(s_aw[1], 16)
                sp.dma_start(g.mod_dram[:, this], row[:]).then_inc(s_row, 16)
            sp.wait_ge(s_av, LAT_CH + 1)
            sp.dma_start(g.mod_dram[:, cols(LAT_CH - 1)], row[:]).then_inc(s_row, 16)
            sp.wait_ge(s_row, 16 * (LAT_CH + 1))

        @block.tensor
        def _(pe):
            for m, (kind, n) in enumerate(tiles):
                if m >= 4:
                    evacuated(pe, m - 4)
                if (kind, n) == ("z", 0):
                    pe.wait_ge(s_small, 16 * 6)
                if n == 0 and kind in "qvg":
                    b = "qvg".index(kind)
                    pe.wait_ge(s_w[b % 2], 16 * (b // 2 + 1))
                if kind == "dec":
                    if n == 0:
                        evacuated(pe, 0)
                    for half in range(2):
                        last = nc.tensor.matmul(slot(m)[:, half], wdec[:, n // 2, (n % 2) * P:(n % 2 + 1) * P],
                                                z[:, half * 320:half * 320 + 320], start=True, stop=True)
                else:
                    for half in range(2):
                        for kt in range(KD):
                            if kind == "z":
                                lhsT, out = wz[:, kt, :], slot(m)[0:2 * GLA_RANK, half]
                            else:
                                c0 = (n + (2 if kind == "k" else 0)) * P
                                b = {"q": 0, "k": 0, "v": 1, "g": 2}[kind]
                                lhsT, out = win[:, b % 2, kt, c0:c0 + P], slot(m)[:, half]
                            last = nc.tensor.matmul(out, lhsT, g.hT[:, kt, half * 320:half * 320 + 320],
                                                    start=kt == 0, stop=kt == KD - 1)
                last.then_inc(s_ps, 1)
            PE.prime(nc.tensor.nop())
            for m in range(len(tiles) - 4, len(tiles)):
                evacuated(pe, m)
            pe.wait_ge(s_ends, 1)
            for half in range(2):
                nc.tensor.nop().then_inc(s_am[half], 1)
            for it0, count, _ in loops:
                with pe.Fori(0, count) as i:
                    it = i + it0
                    if it0:
                        pe.wait_ge(s_av, i + 1)
                        for k in range(KD):
                            half = k // (KD // 2)
                            if k % (KD // 2) == 0:
                                pe.wait_ge(s_aw[half], (i * 16 + 16) * (half + 1))
                            ins = nc.tensor.matmul(g.ps[0:2, 5, :], g.scT[:, k, :], aw[half][:, k % (KD // 2), :],
                                                   start=k == 0, stop=k == KD - 1)
                            if k % (KD // 2) == KD // 2 - 1:
                                ins.then_inc(s_am[half], 1)
                    units = [(d, p) for d in range(2) for p in range(PAIRS)]
                    pe.wait_ge(DV.sem, DV.at(it, "ks"))
                    pe.wait_ge(AC.sem, AC.before(it, "ktok"))
                    for n, (d, p) in enumerate(units):
                        last = nc.tensor.transpose(g.ps[:, 0, n * P:(n + 1) * P], ks[:, d, p], g.blocks[:, 0, :])
                    last.then_inc(PE.sem, 1)
                    pe.wait_ge(PO.sem, PO.at(it, "vs"))
                    pe.wait_ge(AC.sem, AC.before(it, "vtok"))
                    for n, (d, p) in enumerate(units):
                        last = nc.tensor.transpose(g.ps[:, 1, n * P:(n + 1) * P], vs[:, d, 2 * p:2 * p + 2, :],
                                                   g.blocks[:, 0, :])
                    last.then_inc(PE.sem, 1)
                    pe.wait_ge(DV.sem, DV.at(it, "qs"))
                    pe.wait_ge(DV.sem, DV.before(it, "att"))
                    for n, (d, p) in enumerate(units):
                        last = nc.tensor.matmul(g.ps[:, 2, n * P:(n + 1) * P], ks[:, d, p], qs[:, d, p],
                                                start=True, stop=True)
                    last.then_inc(PE.sem, 1)
                    pe.wait_ge(AC.sem, AC.at(it, "vtok"))
                    pe.wait_ge(DV.sem, DV.at(it, "att"))
                    pe.wait_ge(PO.sem, PO.at(it, "m0"))
                    for n, (d, p) in enumerate(units):
                        nc.tensor.matmul(g.ps[:, 3, n * P:(n + 1) * P], vtok[:, d, p], att[:, d, p],
                                         start=True, stop=False)
                        last = nc.tensor.matmul(g.ps[:, 3, n * P:(n + 1) * P], m0[:, d, p], qs[:, d, p],
                                                start=False, stop=True)
                    last.then_inc(PE.sem, 1)
                    pe.wait_ge(AC.sem, AC.at(it, "ktok"))
                    for n, (d, p) in enumerate(units):
                        last = nc.tensor.matmul(g.ps[:, 4, n * P:(n + 1) * P], ktok[:, d, p], vtok[:, d, p],
                                                start=True, stop=True)
                    last.then_inc(PE.sem, 1)
            for h in range(GLA_H):
                pe.wait_ge(s_osq, h + 1)
                if h == 0:
                    pe.wait_ge(DV.sem, DV.at(NCH - 1, "mraw"))
                for half in range(2):
                    last = nc.tensor.matmul(g.ps[:, 2 * h + half, 0:320], g.ones[:],
                                            tmp[:, h, half * 320:half * 320 + 320], start=True, stop=True)
                last.then_inc(s_orms, 1)

        @block.scalar
        def _(act):
            chain = Chain(act, g.act_steps)
            act.wait_ge(s_small, 16 * 6)
            dests = {"q": q, "k": k, "v": v, "g": gate}
            for m, (kind, n) in enumerate(tiles):
                if kind == "z":
                    continue
                act.wait_ge(s_ps, m + 1)
                src = slot(m)
                if kind == "dec":
                    dst = tmp[:, n, :].rearrange("p (a b) -> p a b", a=2)
                    nc.scalar.activation(dst, src, ACT.Abs, bias=bdec[:, n // 2, n % 2:n % 2 + 1]).then_inc(s_eva, 1)
                    if n == 3:
                        act.wait_ge(s_eva, by_act.index(("dec", 3)) + 1)
                        chain.step(nc.scalar.activation(tmp[:], tmp[:], ACT.Exp, scale=-1.0))
                        nc.scalar.activation(tmp[:], tmp[:], ACT.Ln, bias=1.0).then_inc(s_ln, 1)
                else:
                    dst = dests[kind][:, n, :].rearrange("p (a b) -> p a b", a=2)
                    nc.scalar.activation(dst, src, ACT.Silu if kind == "g" else ACT.Copy,
                                         scale=GLA_DK ** -0.5 if kind == "q" else 1.0).then_inc(s_eva, 1)
            act.wait_ge(s_dd, 1)
            for d in range(2):
                for n in range(2):
                    off, sign = ((0, -1.0), (C, 1.0))[n ^ d]
                    last = nc.scalar.activation(ends[:, d, n], dd[:, d, :, :, off], ACT.Exp, scale=sign * S)
            last.then_inc(s_ends, 1)
            AC.prime(nc.scalar.nop())
            act.wait_ge(s_init, 1)
            for it0, count, c0 in loops:
                with act.Fori(0, count) as i:
                    it = i + it0
                    wait_apart(act, PE.sem, PE.before(it, "out"), s_dd)
                    chunk = (act.snap(i + c0), act.snap(c0 + count - 1 - i))
                    for which, dst, name in ((0, ks, "exp_k"), (1, qs, "exp_q")):
                        for d in range(2):
                            off = (1, 0)[d]
                            sign = (-1.0, 1.0)[which ^ d]
                            for h in range(2):
                                r = slice(64 * h, 64 * h + 64)
                                src = dd[r, d, :, bass.ds(chunk[d], 1), off:off + C]
                                last = nc.scalar.activation(dst[r, d, :, 64 * h:64 * h + 64],
                                                            src.rearrange("p a o t -> p a (o t)"), ACT.Exp,
                                                            scale=sign * S)
                        last.then_inc(AC.sem, 1)
                    act.wait_ge(PE.sem, PE.at(it, "ktok"))
                    nc.scalar.copy(ktok[:].rearrange("p d a b -> p (d a b)"), g.ps[:, 0, :]).then_inc(AC.sem, 1)
                    act.wait_ge(PE.sem, PE.at(it, "vtok"))
                    nc.scalar.copy(vtok[:].rearrange("p d a b -> p (d a b)"), g.ps[:, 1, :]).then_inc(AC.sem, 1)
            act.wait_ge(DV.sem, DV.at(NCH - 1, "out"))
            for h in range(GLA_H):
                nc.scalar.activation(tmp[:, h, :], o[:, h, :], ACT.Square).then_inc(s_osq, 1)
            for h in range(GLA_H):
                act.wait_ge(s_oms, h + 1)
                chain.step(nc.scalar.activation(tmp[:, h, :], tmp[:, h, :], ACT.Ln))
            for h in range(GLA_H):
                nc.scalar.activation(tmp[:, h, :], tmp[:, h, :], ACT.Exp, scale=-0.5).then_inc(s_ort, 1)

        @block.gpsimd
        def _(pool):
            chain = Chain(pool, g.pool_steps)
            chain.step(nc.gpsimd.memset(wdec[:], 0.0))
            nc.gpsimd.nop().then_inc(s_zero, 1)
            for t in (qs, ks):
                chain.step(nc.gpsimd.memset(t[:], 0.0))
            chain.step(nc.gpsimd.memset(mraw[:], 0.0))
            chain.step(nc.gpsimd.memset(o, 0.0))
            nc.gpsimd.nop().then_inc(s_init, 1)
            PO.prime(nc.gpsimd.nop())
            pool.wait_ge(s_ends, 1)
            pool.wait_ge(s_eva, len(by_act))
            for it0, count, c0 in loops:
                if it0:
                    pool.wait_ge(s_ld, 64)
                with pool.Fori(0, count) as i:
                    it = i + it0
                    chunk = (pool.snap(i + c0), pool.snap(c0 + count - 1 - i))
                    col = (pool.snap((i + c0) * C), pool.snap((c0 + count - 1 - i) * C))
                    wait_apart(pool, DV.sem, DV.before(it, "mraw"), s_ends)
                    for d in range(2):
                        e = ends[:, d, 0, :, bass.ds(chunk[d], 1)].to_broadcast([P, PAIRS, GLA_DV])
                        last = nc.gpsimd.tensor_tensor(m0[:, d], mraw[:, d], e, ALU.mult)
                    last.then_inc(PO.sem, 1)
                    wait_apart(pool, PE.sem, PE.before(it, "vtok"), s_ends)
                    for d in range(2):
                        last = nc.gpsimd.tensor_copy(vs[:, d], v[:, :, bass.ds(col[d], C)])
                    last.then_inc(PO.sem, 1)

        @block.vector
        def _(dve):
            chain = Chain(dve, g.dve_steps)
            chain.step(nc.vector.memset(reset[:], 1.0))
            chain.step(nc.vector.memset(reset[:].rearrange("p (c t) -> p c t", t=C)[:, :, 0:1], 0.0))
            dve.wait_ge(s_ps, 1)
            nc.vector.tensor_copy(z[:].rearrange("p (a b) -> p a b", a=2),
                                  slot(0)[0:2 * GLA_RANK]).then_inc(s_evd, 1)
            dve.wait_ge(s_small, 16 * 6)
            for n in range(4):
                m = tiles.index(("dec", n))
                dve.wait_ge(s_eva, by_act.index(("dec", n)) + 1)
                nc.vector.tensor_scalar(xmin[:, n].rearrange("p (a b) -> p a b", a=2), slot(m),
                                        bdec[:, n // 2, n % 2:n % 2 + 1], 0.0, ALU.add,
                                        ALU.min).then_inc(s_evd, 1)
            dve.wait_ge(s_evd, 5)
            dve.wait_ge(s_ln, 1)
            for n in range(4):
                chain.step(nc.vector.tensor_tensor(xmin[:, n], xmin[:, n], tmp[:, n, :], ALU.subtract))
                log_decay_to_steps(nc, chain, dd[:, n // 2, n % 2], tmp[:, n, :], reset[:], xmin[:, n], C // 2 - 1)
            nc.vector.nop().then_inc(s_dd, 1)
            DV.prime(nc.vector.nop())
            nc.vector.nop().then_inc(s_av, 1)
            nc.vector.nop().then_inc(s_row, 16)
            dve.wait_ge(s_init, 1)
            dve.wait_ge(s_eva, len(by_act))
            for it0, count, c0 in loops:
                with dve.Fori(0, count) as i:
                    it = i + it0
                    chunk = (dve.snap(i + c0), dve.snap(c0 + count - 1 - i))
                    col = (dve.snap((i + c0) * C), dve.snap((c0 + count - 1 - i) * C))
                    for buf, src, name in ((ks, k, "exp_k"), (qs, q, "exp_q")):
                        dve.wait_ge(AC.sem, AC.at(it, name))
                        for d in range(2):
                            for h in range(2):
                                r = slice(64 * h, 64 * h + 64)
                                dst = buf[r, d, :, 64 * h:64 * h + 64]
                                last = nc.vector.tensor_tensor(dst, dst, src[r, :, bass.ds(col[d], C)], ALU.mult)
                        last.then_inc(DV.sem, 1)
                    dve.wait_ge(PE.sem, PE.at(it, "scores"))
                    dve.wait_ge(PE.sem, PE.before(it, "out"))
                    nc.vector.tensor_tensor(att[:], g.ps[:, 2, :].rearrange("p (d a b) -> p d a b", d=2, a=2),
                                            g.tri[:, :, 1:2, :].to_broadcast([P, 2, PAIRS, P]),
                                            ALU.mult).then_inc(DV.sem, 1)
                    if it0:
                        dve.wait_ge(s_am[1], i + 2)
                        dve.wait_ge(s_row, i * 16 + 16)
                        nc.vector.tensor_tensor(row[:], g.ps[0:2, 5, :], adab[:], ALU.add).then_inc(s_av, 1)
                    dve.wait_ge(PE.sem, PE.at(it, "out"))
                    for d in range(2):
                        dst = o[:, :, bass.ds(col[d], C)]
                        src = g.ps[:, 3, 256 * d:256 * d + 256].rearrange("p (h t) -> p h t", t=C)
                        if d == 1:
                            dve.wait_ge(DV.sem, DV.at(it, "out_f"))
                        nc.vector.tensor_tensor(dst, dst, src, ALU.add).then_inc(DV.sem, 1)
                    dve.wait_ge(PE.sem, PE.at(it, "state"))
                    nc.vector.tensor_tensor(msum[:], m0[:],
                                            g.ps[:, 4, :].rearrange("p (d a b) -> p d a b", d=2, a=2),
                                            ALU.add).then_inc(DV.sem, 1)
                    dve.wait_ge(DV.sem, DV.at(it, "msum"))
                    for d in range(2):
                        e = ends[:, d, 1, :, bass.ds(chunk[d], 1)].to_broadcast([P, PAIRS, GLA_DV])
                        last = nc.vector.tensor_tensor(mraw[:, d], msum[:, d], e, ALU.mult)
                    last.then_inc(DV.sem, 1)
            for h in range(GLA_H):
                dve.wait_ge(s_orms, h + 1)
                nc.vector.tensor_scalar(tmp[:, h, :].rearrange("p (a b) -> p a b", a=2),
                                        g.ps[:, 2 * h:2 * h + 2, 0:320], 1.0 / GLA_DV, EPS,
                                        ALU.mult, ALU.add).then_inc(s_oms, 1)
            for h in range(GLA_H):
                dve.wait_ge(s_ort, h + 1)
                chain.step(nc.vector.tensor_tensor(o[:, h, :], o[:, h, :], tmp[:, h, :], ALU.mult))
                chain.step(nc.vector.scalar_tensor_tensor(o[:, h, :], o[:, h, :], ng[:, h:h + 1], gate[:, h, :],
                                                          ALU.mult, ALU.mult))


def halves(t):
    return t.rearrange("p (a b) -> p a b", a=2)


def stage_rwkv_inputs(nc, g, w, r):
    with ExitStack() as ctx:
        def sb(name, shape, dt=F32):
            return ctx.enter_context(nc.sbuf_tensor(name, shape, dt))

        def sem(name):
            return ctx.enter_context(nc.semaphore(name))

        RCOLS = 3 * RW + ZCOLS
        tiles = [(n, i, P, b, i * P, b * RW + i * P) for b, n in enumerate("rkv") for i in range(HP)]
        tiles = [("zw", 0, P, 3, 0, 3 * RW), ("za", 0, AAA_RANK, 3, P, 3 * RW + P),
                 ("zg", 0, P, 3, P + AAA_RANK, 3 * RW + P + AAA_RANK)] + tiles
        blocks = [3, 0, 1, 2]
        NPAD = 3
        win = g.win
        convrow = sb("rw_convrow", [9, RCOLS])
        conv = sb("rw_conv", [P, len(tiles), 9])
        params = sb("rw_params", [8, RW])
        cpad = sb("rw_cpad", [P, NPAD, CTX + 2])
        lpad = sb("rw_lpad", [P, NPAD, GRID_H + 2, GRID_W + 2])
        zw = sb("rw_zw", [P, TOK])
        za = sb("rw_za", [AAA_RANK, TOK])
        w2 = sb("rw_w2", [P, RW])
        a2 = sb("rw_a2", [AAA_RANK, RW])
        omk = sb("rw_omk", [P, HP])
        reset = sb("rw_reset", [P, TOK])
        sig = sb("rw_sig", [P, 2, TOK])
        cum = sb("rw_cum", [P, TOK])
        a = sb("rw_a", [P, HP, TOK])
        sq = sb("rw_sq", [P, 2, TOK])

        s_w, loaded = g.s_win, (32, 16)
        s_small, s_pad, s_ps, s_ev = sem("rw_s_small"), sem("rw_s_pad"), sem("rw_s_ps"), sem("rw_s_ev")
        s_trow, s_prm, s_conv = sem("rw_s_trow"), sem("rw_s_prm"), sem("rw_s_conv")
        s_z, s_pd, s_sig, s_dd = sem("rw_s_z"), sem("rw_s_pd"), sem("rw_s_sig"), sem("rw_s_dd")
        s_pa, s_a, s_sq, s_pk, s_rt = (sem("rw_s_pa"), sem("rw_s_a"), sem("rw_s_sq"), sem("rw_s_pk"),
                                       sem("rw_s_rt"))
        s_kd = sem("rw_s_kd")
        w_in = w["w_in"][0].rearrange("(k p) n -> p k n", p=P)
        dests = {"r": r.r, "k": r.k, "v": r.v}

        def dest(m):
            name, i, width = tiles[m][:3]
            return {"zw": zw[:], "za": za[:], "zg": r.zg[:]}[name] if name[0] == "z" else dests[name][:, i, :]

        def slot(n):
            return g.ps[:, 2 * (n % 4):2 * (n % 4) + 2, 0:TOK // 2]

        block = ctx.enter_context(nc.Block())

        @block.sync
        def _(sp):
            sp.dma_start(convrow[:], w["rwkv_conv"][0].rearrange("a b c -> (a b) c")).then_inc(s_small, 16)
            for n, name in enumerate(("rwkv_a0", "rwkv_k_k", "rwkv_k_a", "rwkv_r_k", "rwkv_ln_g", "rwkv_ln_b")):
                sp.dma_start(params[n:n + 1, :], w[name]).then_inc(s_small, 16)
            sp.dma_start(params[6:8, :], w["rwkv_w0"][0]).then_inc(s_small, 16)
            sp.dma_start(w2[:], w["rwkv_w2"][0].rearrange("d r n -> (d r) n")).then_inc(s_small, 16)
            sp.dma_start(a2[:], w["rwkv_a2"][0]).then_inc(s_small, 16)
            sp.dma_start(win[:, 1], w_in[:, :, GLA_COLS:GLA_COLS + 512]).then_inc(s_w[1], 16)
            for n in (2, 3):
                sp.wait_ge(s_ps, 3 if n == 2 else 3 + HP)
                c0 = GLA_COLS + 512 * blocks[n]
                sp.dma_start(win[:, n % 2], w_in[:, :, c0:c0 + 512]).then_inc(s_w[n % 2], 16)

        @block.gpsimd
        def _(pool):
            chain = Chain(pool, g.pool_steps)
            chain.step(nc.gpsimd.memset(cpad[:], 0.0))
            chain.step(nc.gpsimd.memset(lpad[:], 0.0))
            nc.gpsimd.nop().then_inc(s_pad, 1)

        @block.tensor
        def _(pe):
            def vectors():
                pe.wait_ge(s_small, 16 * 10)
                for m, (_, _, width, _, _, c) in enumerate(tiles):
                    nc.tensor.transpose(g.ps[0:width, 6, 9 * m:9 * m + 9], convrow[:, c:c + width],
                                        g.blocks[0:9, 0, 0:9])
                for n in range(HP):
                    last = nc.tensor.transpose(g.ps[:, 7, 8 * n:8 * n + 8], params[:, n * P:(n + 1) * P],
                                               g.blocks[0:8, 0, 0:8])
                last.then_inc(s_trow, 1)

            for m, (name, i, width, b, c, _) in enumerate(tiles):
                n = blocks.index(b)
                if i == 0:
                    pe.wait_ge(s_w[n % 2], loaded[n % 2] + 16 * (n // 2 + 1))
                if m == 3:
                    pe.wait_ge(s_prm, 1)
                if m >= 4:
                    pe.wait_ge(s_ev, m - 3)
                for half in range(2):
                    for kt in range(KD):
                        last = nc.tensor.matmul(slot(m)[0:width, half], win[:, n % 2, kt, c:c + width],
                                                g.hT[:, kt, half * 320:half * 320 + 320],
                                                start=kt == 0, stop=kt == KD - 1)
                last.then_inc(s_ps, 1)
                if m == 0:
                    vectors()
            pe.wait_ge(s_ev, len(tiles))
            pe.wait_ge(s_conv, 2)
            pe.wait_ge(s_z, 1)
            for n in range(2 * HP):
                if n < HP:
                    if n >= 2:
                        pe.wait_ge(s_kd, n - 1)
                    for half in range(2):
                        last = nc.tensor.matmul(slot(n % 2)[:, half], a2[:, n * P:(n + 1) * P],
                                                za[:, half * 320:half * 320 + 320], start=True, stop=True)
                    last.then_inc(s_pa, 1)
                if n >= 2:
                    pe.wait_ge(s_sig, n - 1)
                rows = slice(64 * (n // HP), 64 * (n // HP) + 64)
                for half in range(2):
                    last = nc.tensor.matmul(slot(2 + n % 2)[:, half], w2[rows, (n % HP) * P:(n % HP + 1) * P],
                                            zw[rows, half * 320:half * 320 + 320], start=True, stop=True)
                last.then_inc(s_pd, 1)
                if n < HP:
                    pe.wait_ge(s_sq, n + 1)
                    pe.wait_ge(s_a, n + 1)
                    for half in range(2):
                        last = nc.tensor.matmul(slot(n % 2)[:, half], g.blocks[:, 6, :],
                                                sq[:, n % 2, half * 320:half * 320 + 320], start=True, stop=True)
                    last.then_inc(s_pk, 1)

        @block.scalar
        def _(act):
            chain = Chain(act, g.act_steps)
            act.wait_ge(s_pad, 1)
            for m, (name, i, width, _, _, _) in enumerate(tiles):
                act.wait_ge(s_ps, m + 1)
                if m >= NPAD:
                    act.wait_ge(s_conv, m - NPAD + 1)
                b, s = m % NPAD, slice(0, width)
                nc.scalar.copy(cpad[s, b, 1:CTX + 1], slot(m)[s, 0, 0:CTX])
                nc.scalar.copy(lpad[s, b, 1:4, 1:GRID_W + 1],
                               slot(m)[s, 0, CTX:320].rearrange("p (y x) -> p y x", x=GRID_W))
                nc.scalar.copy(lpad[s, b, 4:9, 1:GRID_W + 1],
                               slot(m)[s, 1].rearrange("p (y x) -> p y x", x=GRID_W)).then_inc(s_ev, 1)
            act.wait_ge(s_conv, 3)
            nc.scalar.activation(zw[:], zw[:], ACT.Tanh).then_inc(s_z, 1)
            nc.scalar.activation(r.zg[:], r.zg[:], ACT.Sigmoid).then_inc(s_z, 1)
            act.wait_ge(s_conv, len(tiles))
            for n in range(2 * HP):
                if n < HP:
                    act.wait_ge(s_pa, n + 1)
                    if n >= 2:
                        act.wait_ge(s_pk, n - 1)
                    nc.scalar.activation(halves(a[:, n]), slot(n % 2), ACT.Sigmoid,
                                         bias=r.prm[:, n, 0:1]).then_inc(s_a, 1)
                    nc.scalar.activation(sq[:, n % 2], r.k[:, n, :], ACT.Square,
                                         scale=r.prm[:, n, 1:2]).then_inc(s_sq, 1)
                act.wait_ge(s_pd, n + 1)
                if n >= 2:
                    act.wait_ge(s_dd, n - 1)
                nc.scalar.activation(halves(sig[:, n % 2]), slot(2 + n % 2), ACT.Sigmoid,
                                     bias=r.prm[:, n % HP, 6 + n // HP:7 + n // HP]).then_inc(s_sig, 1)
            act.wait_ge(s_kd, HP)
            chain.step(nc.scalar.activation(r.kk[:], r.kk[:], ACT.Ln))
            for n in range(HP):
                nc.scalar.activation(r.kk[:, n, :], r.kk[:, n, :], ACT.Exp, scale=-0.5).then_inc(s_rt, 1)
            act.wait_ge(s_dd, 2 * HP)
            for d in range(2):
                for n in range(2):
                    off, sign = ((0, -1.0), (C, 1.0))[n ^ d]
                    nc.scalar.activation(r.ends[:, d, n], r.dd[:, d, :, :, off], ACT.Exp, scale=sign * r.S)

        @block.vector
        def _(dve):
            chain = Chain(dve, g.dve_steps)
            chain.step(nc.vector.memset(reset[:], 1.0))
            chain.step(nc.vector.memset(reset[:].rearrange("p (c t) -> p c t", t=C)[:, :, 0:1], 0.0))
            dve.wait_ge(s_trow, 1)
            for m, (_, _, width, _, _, _) in enumerate(tiles):
                last = nc.vector.tensor_copy(conv[0:width, m, :], g.ps[0:width, 6, 9 * m:9 * m + 9])
            chain.step(last)
            chain.step(nc.vector.tensor_copy(r.prm[:], g.ps[:, 7, 0:8 * HP].rearrange("p (a b) -> p a b", b=8)))
            nc.vector.nop().then_inc(s_prm, 1)
            chain.step(nc.vector.tensor_scalar(omk[:], r.prm[:, :, 2], -1.0, 1.0, ALU.mult, ALU.add))
            for m, (_, _, width, _, _, _) in enumerate(tiles):
                dve.wait_ge(s_ev, m + 1)
                s, b = slice(0, width), m % NPAD
                out = dest(m)[s]
                lat = out[:, CTX:TOK].rearrange("p (y x) -> p y x", x=GRID_W)
                for tap in range(9):
                    y, x = tap // 3, tap % 3
                    src, wt = lpad[s, b, y:y + GRID_H, x:x + GRID_W], conv[s, m, tap:tap + 1]
                    if tap == 0:
                        chain.step(nc.vector.tensor_scalar(lat, src, wt, None, ALU.mult))
                    else:
                        chain.step(nc.vector.scalar_tensor_tensor(lat, src, wt, lat, ALU.mult, ALU.add))
                    if y == 1:
                        src = cpad[s, b, x:x + CTX]
                        if x == 0:
                            chain.step(nc.vector.tensor_scalar(out[:, 0:CTX], src, wt, None, ALU.mult))
                        else:
                            chain.step(nc.vector.scalar_tensor_tensor(out[:, 0:CTX], src, wt, out[:, 0:CTX],
                                                                      ALU.mult, ALU.add))
                nc.vector.nop().then_inc(s_conv, 1)
            for n in range(2 * HP):
                if n < HP:
                    dve.wait_ge(s_pk, n + 1)
                    nc.vector.tensor_scalar(halves(r.kk[:, n, :]), slot(n % 2), 1e-24, None,
                                            ALU.max).then_inc(s_kd, 1)
                    chain.step(nc.vector.tensor_scalar(r.nb[:, n, :], r.k[:, n, :], r.prm[:, n, 1:2], None, ALU.mult))
                    dve.wait_ge(s_a, n + 1)
                    chain.step(nc.vector.tensor_scalar(cum[:], a[:, n], r.prm[:, n, 2:3], omk[:, n:n + 1],
                                                       ALU.mult, ALU.add))
                    dve.wait_ge(s_sq, n + 1)
                    chain.step(nc.vector.tensor_tensor(r.k[:, n, :], r.k[:, n, :], cum[:], ALU.mult))
                dve.wait_ge(s_sig, n + 1)
                log_decay_to_steps(nc, chain, r.dd[:, n // HP, n % HP], cum[:], reset[:], sig[:, n % 2], C // 2 - 1)
                nc.vector.nop().then_inc(s_dd, 1)
            for n in range(HP):
                dve.wait_ge(s_rt, n + 1)
                chain.step(nc.vector.tensor_tensor(r.kk[:, n, :], r.nb[:, n, :], r.kk[:, n, :], ALU.mult))
                chain.step(nc.vector.scalar_tensor_tensor(r.nb[:, n, :], r.kk[:, n, :], -1.0, a[:, n],
                                                          ALU.mult, ALU.mult))


def stage_rwkv_scan(nc, g, w, r):
    LV = 6
    y = g.oT[:, 4:8, :]
    with ExitStack() as ctx:
        def sb(name, shape, dt=F32):
            return ctx.enter_context(nc.sbuf_tensor(name, shape, dt))

        def sem(name):
            return ctx.enter_context(nc.semaphore(name))

        D2 = range(2)
        big = g.hT[:].rearrange("p a b -> p (a b)")

        def room(at, d, width):
            return big[:, at + d * HP * width:at + (d + 1) * HP * width].rearrange("p (a b) -> p a b", a=HP)

        lq, pq, m0 = ([room(at, d, P) for d in D2] for at in (0, 1024, 2048))
        lb, pk = ([room(at, d, P).rearrange("p a (x b) -> p a x b", x=2) for d in D2] for at in (3072, 4096))
        ex = [sb(f"ex{d}", [P, 3, HP, C]) for d in D2]
        winroom = g.win[:].rearrange("p a b c -> p (a b c)")

        def wroom(n, d):
            return winroom[:, 1024 * n + 512 * d:1024 * n + 512 * (d + 1)]

        T, a_, vs, mr, vtok = ([wroom(n, d).rearrange("p (a b) -> p a b", a=HP) for d in D2] for n in range(5))
        rp = [wroom(5, d).rearrange("p (a x b) -> p a x b", a=HP, x=2) for d in D2]
        arc = [sb(f"arc{d}", [P, HP, 3, C]) for d in D2]
        bk = [winroom[:, 1024 * (6 + d):1024 * (7 + d)].rearrange("p (a x b) -> p a x b", a=HP, x=2) for d in D2]
        vtokc = [sb(f"vtokc{d}", [P, HP, C]) for d in D2]
        pac = [sb(f"pac{d}", [P, HP, 2, C]) for d in D2]
        uw = [sb(f"uw{d}", [P, HP, 2, P]) for d in D2]
        G = [sb(f"G{d}", [P, HP, P]) for d in D2]
        TT = [sb(f"TT{d}", [P, HP, P]) for d in D2]
        between = sb("between", [P, 2, HP, NCH])
        states = [sb(f"states{d}", [P, HP, P]) for d in D2]
        upto = sb("upto", [P, 2, C])

        aside = {0: "atok", 1: "ktok", 2: "btok", 3: "mtok", 4: "pv"}
        levels = [x for j in range(1, LV) for x in (f"G{j}", f"TT{j}", f"T{j}", aside.get(j)) if x][:-1]
        PE = [Steps(sem(f"rs_pe{d}"), "lq", "pq", "vtok", "T0", "atok", *levels,
                    "uw", "rp", "ym") for d in D2]
        inputs_at = {1: "A", 2: "K", 3: "B", LV - 2: "m0"}
        DV = [Steps(sem(f"rs_dv{d}"), "lqs", "TT0a", "TT0", "lq", "pq",
                    *[x for j in range(1, LV) for x in (f"G{j}", f"TT{j}", inputs_at.get(j)) if x],
                    "rp", "ar", "y", "mr") for d in D2]
        AC = [Steps(sem(f"rs_ac{d}"), "vtok", "T0", "atok", "ex", "T1", "ktok", "T2", "btok",
                    *[f"T{j}" for j in range(3, LV - 1)], "pv", "w", "u", "vs") for d in D2]
        s_zero = sem("rs_zero")
        s_init, s_st, s_ld, s_tr, s_sc, s_bk = (sem("rs_init"), sem("rs_st"), sem("rs_ld"), sem("rs_tr"),
                                               sem("rs_sc"), sem("rs_bk"))

        def chunks(it):
            if isinstance(it, int) and it < CTX_CH:
                return it, CTX_CH - 1 - it
            return it, NCH - 1 + CTX_CH - it

        def over(eng, body, between):
            for it in range(CTX_CH):
                body(it, chunks(it), chunks(it + 1))
            between()
            with eng.Fori(0, NCH - 1 - CTX_CH) as i:
                at, nxt = chunks(i + CTX_CH), chunks(i + (CTX_CH + 1))
                body(i + CTX_CH, [eng.snap(c) for c in at], [eng.snap(c) for c in nxt])
            body(NCH - 1, chunks(NCH - 1), None)

        def bank(d, n):
            return g.ps[:, 4 * d + n, :].rearrange("p (a b) -> p a b", a=HP)

        def bankc(d, n):
            return g.ps[:, 4 * d + n, 0:HP * C].rearrange("p (a b) -> p a b", a=HP)

        def spread(stacked):
            return stacked.unsqueeze(2).to_broadcast([P, HP, 2, C])

        def mask(m):
            return m.rearrange("p (x b) -> p x b", x=2).unsqueeze(1).to_broadcast([P, HP, 2, C])

        def wide(t):
            return t.rearrange("p a (x b) -> p a x b", x=2)

        ident = g.blocks[:, 0, :]
        idents = ident.unsqueeze(1).to_broadcast([P, HP, P])
        block = ctx.enter_context(nc.Block())

        @block.sync
        def _(sp):
            def heads(t, d):
                return t[0, 0, d].rearrange("(p e) v k -> e v p k", e=2)
            sp.wait_ge(s_init, 2)
            for d in D2:
                for e in range(2):
                    s = slice(64 * e, 64 * e + 64)
                    sp.dma_start(states[d][s, :, 64 * e:64 * e + 64], heads(w["state_rwkv"], d)[e]).then_inc(s_ld, 16)
            sp.wait_ge(s_bk, 4)
            for d in D2:
                for e in range(2):
                    s = slice(64 * e, 64 * e + 64)
                    sp.dma_start(heads(w["new_state_rwkv"], d)[e], states[d][s, :, 64 * e:64 * e + 64]).then_inc(s_st, 16)
            sp.wait_ge(s_st, 64)

        @block.gpsimd
        def _(pool):
            chain = Chain(pool, g.pool_steps)
            for d in D2:
                chain.step(nc.gpsimd.memset(a_[d], 0.0))
            for d in D2:
                incl = g.tri[:, d, 1, :]
                chain.step(nc.gpsimd.tensor_tensor(upto[:, d, :], incl[:, 0:C], incl[:, C:P], ALU.add))
                chain.step(nc.gpsimd.tensor_tensor(arc[d][:, :, 2, :], idents[:, :, 0:C], idents[:, :, C:P], ALU.add))
            nc.gpsimd.nop().then_inc(s_init, 1)
            chain.step(nc.gpsimd.tensor_copy(between[:], r.ends[:, :, 0]))
            for d, to, of in ((0, slice(1, 2), slice(0, 1)), (0, slice(3, NCH), slice(2, NCH - 1)),
                              (1, slice(0, 1), slice(1, 2)), (1, slice(2, NCH - 1), slice(3, NCH))):
                v = between[:, d, :, to]
                chain.step(nc.gpsimd.tensor_tensor(v, v, r.ends[:, d, 1, :, of], ALU.mult))
            for d in D2:
                for t in (mr[d], uw[d][:], states[d][:]):
                    chain.step(nc.gpsimd.memset(t, 0.0))
            chain.step(nc.gpsimd.memset(y, 0.0))
            nc.gpsimd.nop().then_inc(s_init, 1)

        @block.scalar
        def _(act):
            def decays(it, nxt):
                for d in D2:
                    if it is not None:
                        wait_apart(act, DV[d].sem, DV[d].before(it, "ar"), s_init)
                    excl, incl, sign = ((0, 1, 1.0), (1, 0, -1.0))[d]
                    for n, (off, sg) in enumerate(((excl, sign), (incl, sign), (incl, -sign))):
                        src = r.dd[:, d, :, bass.ds(nxt[d], 1), off:off + C]
                        last = nc.scalar.activation(ex[d][:, n], src.rearrange("p a o t -> p a (o t)"),
                                                    ACT.Exp, scale=sg * r.S)
                    last.then_inc(AC[d].sem, 1)

            def values(nxt):
                for d in D2:
                    col = reg(act, nxt[d] * C)
                    for h in range(2):
                        s = slice(64 * h, 64 * h + 64)
                        last = nc.scalar.copy(vs[d][s, :, 64 * h:64 * h + 64], r.v[s, :, bass.ds(col, C)])
                    last.then_inc(AC[d].sem, 1)

            def stacked(dst, src):
                for h in range(2):
                    s = slice(64 * h, 64 * h + 64)
                    last = nc.scalar.copy(dst[s], src[s, :, 64 * h:64 * h + 64])
                return last

            def on_diagonal(dst, src, d):
                for h in range(2):
                    s = slice(64 * h, 64 * h + 64)
                    last = nc.scalar.copy(dst[s, :, 64 * h:64 * h + 64], src[s])
                return last

            for d in D2:
                act.nop().then_inc(AC[d].sem, AC[d].names.index("ex"))
            act.wait_ge(s_init, 1)
            decays(None, chunks(0))
            act.wait_ge(s_zero, 1)
            for d in D2:
                act.wait_ge(AC[d].sem, AC[d].before(0, "ex"))
                act.nop().then_inc(AC[d].sem, AC[d].names.index("vs") - AC[d].names.index("ex") - 1)
            values(chunks(0))

            def body(it, at, nxt):
                def copy(name, dst, n, src=bank):
                    for d in D2:
                        act.wait_ge(PE[d].sem, PE[d].at(it, name))
                        nc.scalar.copy(dst(d), src(d, n)).then_inc(AC[d].sem, 1)

                for d in D2:
                    act.wait_ge(PE[d].sem, PE[d].at(it, "vtok"))
                    nc.scalar.copy(vtok[d], bank(d, 2))
                    stacked(vtokc[d][:], bank(d, 2)).then_inc(AC[d].sem, 1)
                copy("T0", lambda d: T[d][:], 3)
                for d in D2:
                    act.wait_ge(PE[d].sem, PE[d].at(it, "atok"))
                    stacked(pac[d][:, :, 1, :], bank(d, 0)).then_inc(AC[d].sem, 1)
                if nxt:
                    decays(it, nxt)
                else:
                    for d in D2:
                        act.wait_ge(AC[d].sem, AC[d].at(it, "atok"))
                        act.nop().then_inc(AC[d].sem, 1)
                copy("T1", lambda d: T[d][:], 3)
                for d in D2:
                    act.wait_ge(PE[d].sem, PE[d].at(it, "ktok"))
                    stacked(pk[d][:, :, 1, :], bank(d, 0)).then_inc(AC[d].sem, 1)
                copy("T2", lambda d: T[d][:], 3)
                for d in D2:
                    act.wait_ge(PE[d].sem, PE[d].at(it, "btok"))
                    stacked(lb[d][:, :, 1, :], bank(d, 0)).then_inc(AC[d].sem, 1)
                for j in range(3, LV - 1):
                    copy(f"T{j}", lambda d: T[d][:], 3)
                copy("pv", lambda d: pac[d][:, :, 0, :], 0, bankc)
                act.wait_ge(s_init, 2)
                for d in D2:
                    act.wait_ge(PE[d].sem, PE[d].at(it, "uw"))
                    out = bank(d, 0).rearrange("p a (x b) -> p a x b", x=2)
                    on_diagonal(uw[d][:, :, 1, :], out[:, :, 1, :], d).then_inc(AC[d].sem, 1)
                for d in D2:
                    out = bank(d, 0).rearrange("p a (x b) -> p a x b", x=2)
                    on_diagonal(uw[d][:, :, 0, :], out[:, :, 0, :], d).then_inc(AC[d].sem, 1)
                if nxt:
                    values(nxt)

            def switch():
                for d in D2:
                    act.wait_ge(s_tr, d + 1)
                    if d == 0:
                        act.wait_ge(s_ld, 64)
                    nc.scalar.copy(mr[d], states[d][:]).then_inc(s_bk, 1)
                for d in D2:
                    act.wait_ge(s_tr, d + 3)
                    act.wait_ge(s_bk, 2)
                    nc.scalar.copy(states[d][:], bank(d, 1)).then_inc(s_bk, 1)

            over(act, body, switch)

        @block.vector
        def _(dve):
            def on_diagonal(name, d, at):
                dst, n, src = {"A": (a_[d], 0, r.kk), "K": (bk[d][:, :, 1, :], 2, r.k),
                               "B": (bk[d][:, :, 0, :], 2, r.nb)}[name]
                for h in range(2):
                    s = slice(64 * h, 64 * h + 64)
                    last = nc.vector.tensor_tensor(dst[s, :, 64 * h:64 * h + 64], ex[d][s, n], src[s, :, at], ALU.mult)
                return last

            def stacked_inputs(d, at):
                for x, src in enumerate((r.kk, r.r)):
                    last = nc.vector.tensor_tensor(arc[d][:, :, x, :], ex[d][:, x], src[:, :, at], ALU.mult)
                return last

            def inputs(it, nxt, name):
                for d in D2:
                    if nxt is None:
                        before = DV[d].names[DV[d].names.index(name) - 1]
                        dve.wait_ge(DV[d].sem, DV[d].at(it, before))
                        dve.nop().then_inc(DV[d].sem, 1)
                        continue
                    at = bass.ds(reg(dve, nxt[d] * C), C)
                    if name == "ar":
                        wait_apart(dve, DV[d].sem, DV[d].at(it, "rp"), s_init)
                        stacked_inputs(d, at).then_inc(DV[d].sem, 1)
                    else:
                        wait_apart(dve, AC[d].sem, AC[d].at(it, "ex"), s_init)
                        on_diagonal(name, d, at).then_inc(DV[d].sem, 1)

            for d in D2:
                dve.nop().then_inc(DV[d].sem, DV[d].names.index("ar"))
            chain = Chain(dve, g.dve_steps)
            for d in D2:
                for t in (vs[d], bk[d]):
                    chain.step(nc.vector.memset(t, 0.0))
            nc.vector.nop().then_inc(s_zero, 1)
            dve.wait_ge(s_init, 1)
            for d in D2:
                dve.wait_ge(AC[d].sem, AC[d].before(0, "ex"))
                at = bass.ds(chunks(0)[d] * C, C)
                for name in "BKA":
                    on_diagonal(name, d, at)
                stacked_inputs(d, at).then_inc(DV[d].sem, 1)
                dve.wait_ge(DV[d].sem, DV[d].before(0, "ar"))
                dve.nop().then_inc(DV[d].sem, 2)

            def body(it, at, nxt):
                def strict(dst, d, n):
                    return nc.vector.tensor_tensor(wide(dst[d]), spread(wide(bank(d, n))[:, :, 0, :]),
                                                   mask(g.tri[:, d, 0, :]), ALU.mult)

                def inclusive(dst, d, n):
                    return nc.vector.tensor_tensor(dst[d][:, :, 0, :], wide(bank(d, n))[:, :, 1, :],
                                                   upto[:, d:d + 1, :].to_broadcast([P, HP, C]), ALU.mult)

                for d in D2:
                    dve.wait_ge(PE[d].sem, PE[d].at(it, "lq"))
                    strict(lq, d, 0).then_inc(DV[d].sem, 1)
                    wait_apart(dve, DV[d].sem, DV[d].at(it, "lqs"), s_init)
                    nc.vector.tensor_tensor(TT[d][:], lq[d], g.levels[:, 0:1, :].to_broadcast([P, HP, P]),
                                            ALU.mult).then_inc(DV[d].sem, 1)
                    wait_apart(dve, DV[d].sem, DV[d].at(it, "TT0a"), s_init)
                    nc.vector.tensor_tensor(TT[d][:], TT[d][:], idents, ALU.add).then_inc(DV[d].sem, 1)
                for d in D2:
                    inclusive(lb, d, 0).then_inc(DV[d].sem, 1)
                for d in D2:
                    dve.wait_ge(PE[d].sem, PE[d].at(it, "pq"))
                    strict(pq, d, 1)
                    inclusive(pk, d, 1).then_inc(DV[d].sem, 1)
                for j in range(1, LV):
                    for d in D2:
                        dve.wait_ge(PE[d].sem, PE[d].at(it, f"G{j}"))
                        nc.vector.tensor_tensor(G[d][:], bank(d, 1),
                                                g.levels[:, j:j + 1, :].to_broadcast([P, HP, P]),
                                                ALU.mult).then_inc(DV[d].sem, 1)
                    for d in D2:
                        dve.wait_ge(PE[d].sem, PE[d].at(it, f"TT{j}"))
                        nc.vector.tensor_tensor(TT[d][:], bank(d, 2), TT[d][:], ALU.add).then_inc(DV[d].sem, 1)
                    if j != LV - 2 and j in inputs_at:
                        inputs(it, nxt, inputs_at[j])
                    if j == LV - 2:
                        dve.wait_ge(s_init, 2)
                        for d in D2:
                            wait_apart(dve, PE[d].sem, PE[d].at(it, "mtok"), s_init)
                            e = between[:, d, :, bass.ds(at[d], 1)].to_broadcast([P, HP, P])
                            nc.vector.tensor_tensor(m0[d], bank(d, 0), e, ALU.mult).then_inc(DV[d].sem, 1)
                for d in D2:
                    dve.wait_ge(PE[d].sem, PE[d].at(it, "rp"))
                    nc.vector.tensor_tensor(rp[d], wide(bank(d, 2)), arc[d][:, :, 1:3, :],
                                            ALU.add).then_inc(DV[d].sem, 1)
                inputs(it, nxt, "ar")
                col = [reg(dve, at[d] * C) for d in D2]
                dve.wait_ge(s_init, 2)
                for d in D2:
                    wait_apart(dve, PE[d].sem, PE[d].at(it, "ym"), s_init)
                    dst, out = y[:, :, bass.ds(col[d], C)], wide(bank(d, 3))
                    nc.vector.tensor_tensor(dst, dst, out[:, :, 0, :], ALU.add).then_inc(DV[d].sem, 1)
                    if d == 0:
                        dve.wait_ge(DV[0].sem, DV[0].at(it, "y"))
                    nc.vector.tensor_tensor(wide(mr[d]), spread(out[:, :, 1, :]), mask(g.blocks[:, 6, :]),
                                            ALU.mult).then_inc(DV[d].sem, 1)

            def switch():
                for d in D2:
                    dve.wait_ge(s_tr, d + 1)
                    last = (CTX_CH - 1, 0)[d]
                    e = r.ends[:, d, 1, :, last:last + 1].to_broadcast([P, HP, P])
                    nc.vector.tensor_tensor(uw[d][:, :, 1, :], bank(d, 0), e, ALU.mult).then_inc(s_sc, 1)

            over(dve, body, switch)

        @block.tensor
        def _(pe):
            for d in D2:
                PE[d].prime(nc.tensor.nop())
            pe.wait_ge(s_init, 1)

            def body(it, at, nxt):
                def dv(name):
                    return lambda d: (DV[d].sem, DV[d].at(it, name))

                def dv_before(name):
                    return lambda d: (DV[d].sem, DV[d].before(it, name))

                def ac(name):
                    return lambda d: (AC[d].sem, AC[d].at(it, name))

                def product(name, n, lhsT, rhs, *waits, cols=P):
                    for d in D2:
                        for wait in waits:
                            pe.wait_ge(*wait(d))
                        out = bankc(d, n) if cols == C else bank(d, n)
                        for p in range(HP):
                            if rhs:
                                ins = nc.tensor.matmul(out[:, p], lhsT(d, p), rhs(d, p), start=True, stop=True)
                            else:
                                ins = nc.tensor.transpose(out[:, p], lhsT(d, p), ident)
                        ins.then_inc(PE[d].sem, 1)

                def both(t):
                    return lambda d, p: t[d][:, p, 0:2].rearrange("p x b -> p (x b)")

                def one(t, x=None):
                    return (lambda d, p: t[d][:, p]) if x is None else (lambda d, p: t[d][:, p, x, :])

                product("lq", 0, one(bk, 0), both(arc), dv_before("ar"))
                product("pq", 1, one(bk, 1), both(arc))
                product("vtok", 2, one(vs), None, lambda d: (AC[d].sem, AC[d].before(it, "vs")))
                product("T0", 3, one(TT), None, dv_before("mr"), dv("TT0"))
                product("atok", 0, one(a_), None, dv("lq"))
                for j in range(1, LV):
                    product(f"G{j}", 1, one(lq), one(T), ac(f"T{j - 1}"), *([dv("pq")] if j == 1 else []))
                    product(f"TT{j}", 2, one(G), one(TT), dv(f"G{j}"))
                    if j < LV - 1:
                        product(f"T{j}", 3, one(TT), None, dv(f"TT{j}"))
                    if aside.get(j) == "mtok":
                        product("mtok", 0, one(mr), None, ac("btok"), lambda d: (s_init, 2))
                    elif aside.get(j) == "pv":
                        product("pv", 0, one(pq), one(vtokc), dv("m0"), cols=C)
                    elif j in aside:
                        product(aside[j], 0, one(bk, aside[j] == "ktok"), None, ac(aside[j - 1]))
                product("uw", 0, one(TT), both(pac), ac("pv"), dv(f"TT{LV - 1}"))
                product("rp", 2, one(uw, 1), both(lb), ac("w"))
                for d in D2:
                    pe.wait_ge(*ac("u")(d))
                    pe.wait_ge(*dv("rp")(d))
                    for p in range(HP):
                        out = bank(d, 3)[:, p]
                        nc.tensor.matmul(out, vtok[d][:, p], both(pk)(d, p), start=True, stop=False)
                        nc.tensor.matmul(out, uw[d][:, p, 0, :], both(lb)(d, p), start=False, stop=False)
                        ins = nc.tensor.matmul(out, m0[d][:, p], both(rp)(d, p), start=False, stop=True)
                    ins.then_inc(PE[d].sem, 1)

            def switch():
                for d in D2:
                    pe.wait_ge(DV[d].sem, DV[d].at(CTX_CH - 1, "mr"))
                    for p in range(HP):
                        ins = nc.tensor.transpose(bank(d, 0)[:, p], mr[d][:, p], ident)
                    ins.then_inc(s_tr, 1)
                for d in D2:
                    pe.wait_ge(s_sc, d + 1)
                    for p in range(HP):
                        ins = nc.tensor.transpose(bank(d, 1)[:, p], uw[d][:, p, 1, :], ident)
                    ins.then_inc(s_tr, 1)
                pe.wait_ge(s_bk, 4)

            over(pe, body, switch)


def stage_rwkv_output(nc, g, w, r):
    y = g.oT[:, 4:8, :]
    with ExitStack() as ctx:
        def sb(name, shape, dt=F32):
            return ctx.enter_context(nc.sbuf_tensor(name, shape, dt))

        def sem(name):
            return ctx.enter_context(nc.semaphore(name))

        g2 = sb("ro_g2", [P, RW])
        sq = sb("ro_sq", [P, 2, TOK])
        rk = sb("ro_rk", [P, HP, TOK])
        std = sb("ro_std", [P, HP, TOK])
        s_g2, s_mean, s_ctr, s_sq, s_var, s_vd, s_rt = (sem("ro_g2"), sem("ro_mean"), sem("ro_ctr"), sem("ro_sq_"),
                                                       sem("ro_var"), sem("ro_vd"), sem("ro_rt"))
        s_bon, s_v, s_gate = sem("ro_bon"), sem("ro_v"), sem("ro_gate")

        def slot(n):
            return g.ps[:, 2 * n:2 * n + 2, 0:TOK // 2]

        block = ctx.enter_context(nc.Block())

        @block.sync
        def _(sp):
            sp.dma_start(g2[:], w["rwkv_g2"][0]).then_inc(s_g2, 16)
            for n in range(2):
                sp.dma_start(g.win[:, n], w["w_out"][0, :, n * 512:(n + 1) * 512].rearrange("(k p) n -> p k n", p=P)
                             ).then_inc(g.s_wout, 16)

        @block.tensor
        def _(pe):
            def over_heads(n, src, s_out):
                for half in range(2):
                    last = nc.tensor.matmul(slot(n)[:, half], g.blocks[:, 6, :], src[:, half * 320:half * 320 + 320],
                                            start=True, stop=True)
                last.then_inc(s_out, 1)

            for n in range(HP + 1):
                if n < HP:
                    if n >= 2:
                        pe.wait_ge(s_ctr, n - 1)
                    over_heads(n % 2, y[:, n, :], s_mean)
                if n:
                    pe.wait_ge(s_sq, n)
                    if n >= 3:
                        pe.wait_ge(s_vd, n - 2)
                    over_heads(2 + (n - 1) % 2, sq[:, (n - 1) % 2], s_var)
            pe.wait_ge(s_ctr, HP)
            for n in range(HP):
                if n == 2:
                    pe.wait_ge(s_vd, HP)
                over_heads(n, rk[:, n], s_bon)
            pe.wait_ge(s_g2, 16)
            for n in range(HP):
                pe.wait_ge(s_v, n + 1)
                for half in range(2):
                    last = nc.tensor.matmul(slot(n)[:, half], g2[:, n * P:(n + 1) * P],
                                            r.zg[:, half * 320:half * 320 + 320], start=True, stop=True)
                last.then_inc(s_gate, 1)

        @block.scalar
        def _(act):
            chain = Chain(act, g.act_steps)
            for n in range(HP):
                act.wait_ge(s_ctr, n + 1)
                if n >= 2:
                    act.wait_ge(s_var, n - 1)
                nc.scalar.activation(sq[:, n % 2], y[:, n, :], ACT.Square).then_inc(s_sq, 1)
            act.wait_ge(s_vd, HP)
            chain.step(nc.scalar.activation(std[:], std[:], ACT.Ln))
            for n in range(HP):
                nc.scalar.activation(std[:, n], std[:, n], ACT.Exp, scale=-0.5).then_inc(s_rt, 1)

        @block.vector
        def _(dve):
            chain = Chain(dve, g.dve_steps)
            for n in range(HP + 1):
                if n < HP:
                    chain.step(nc.vector.scalar_tensor_tensor(rk[:, n], r.r[:, n, :], r.prm[:, n, 3:4], r.k[:, n, :],
                                                              ALU.mult, ALU.mult))
                    dve.wait_ge(s_mean, n + 1)
                    nc.vector.scalar_tensor_tensor(halves(y[:, n, :]), slot(n % 2), -1.0 / RN, halves(y[:, n, :]),
                                                   ALU.mult, ALU.add).then_inc(s_ctr, 1)
                if n:
                    dve.wait_ge(s_var, n)
                    nc.vector.tensor_scalar(halves(std[:, n - 1]), slot(2 + (n - 1) % 2), 1.0 / RN, RWKV_LN_EPS,
                                            ALU.mult, ALU.add).then_inc(s_vd, 1)
            for n in range(HP):
                dve.wait_ge(s_bon, n + 1)
                nc.vector.tensor_tensor(halves(r.v[:, n, :]), halves(r.v[:, n, :]), slot(n), ALU.mult).then_inc(s_v, 1)
            dve.wait_ge(s_v, HP)
            for n in range(HP):
                yn = y[:, n, :]
                dve.wait_ge(s_rt, n + 1)
                chain.step(nc.vector.tensor_tensor(yn, yn, std[:, n], ALU.mult))
                chain.step(nc.vector.tensor_scalar(yn, yn, r.prm[:, n, 4:5], r.prm[:, n, 5:6], ALU.mult, ALU.add))
                chain.step(nc.vector.tensor_tensor(yn, yn, r.v[:, n, :], ALU.add))
                dve.wait_ge(s_gate, n + 1)
                chain.step(nc.vector.tensor_tensor(halves(yn), halves(yn), slot(n), ALU.mult))


def stage_rwkv(nc, g, w):
    with ExitStack() as ctx:
        def sb(name, shape, dt=F32):
            return ctx.enter_context(nc.sbuf_tensor(name, shape, dt))
        r = Shared()
        r.S = -math.exp(-0.5)
        r.r, r.k, r.v = sb("r_r", [P, HP, TOK]), sb("r_k", [P, HP, TOK]), sb("r_v", [P, HP, TOK])
        r.kk, r.nb = sb("r_kk", [P, HP, TOK]), sb("r_nb", [P, HP, TOK])
        r.dd = sb("r_dd", [P, 2, HP, NCH, C + 1])
        r.ends = sb("r_ends", [P, 2, 2, HP, NCH])
        r.zg = sb("r_zg", [P, TOK])
        r.prm = sb("r_prm", [P, HP, 8])
        stage_rwkv_inputs(nc, g, w, r)
        stage_rwkv_scan(nc, g, w, r)
        stage_rwkv_output(nc, g, w, r)


BLK = P
MORE = (TOK * TOP_K) // (BLK + 1)
MORE += MORE % 2
NBLK = NE + MORE + 2
ROWS = TOK * TOP_K
U_MAIN, U_MORE = 8, 2


def stage_project_and_route(nc, g, w, m):
    with ExitStack() as ctx:
        def sb(name, shape, dt=F32):
            return ctx.enter_context(nc.sbuf_tensor(name, shape, dt))

        def sem(name):
            return ctx.enter_context(nc.semaphore(name))

        wout = [g.win[:, n] for n in range(2)]
        mod = sb("pr_mod", [P, 3, 2, D])
        w13 = sb("pr_w13", [P, KD, 2, FF])
        w2 = sb("pr_w2", [P, 2, D])
        wr = sb("pr_wr", [P, KD, NE])
        br = sb("pr_br", [P, NE])
        work = sb("pr_work", [P, 4, D])
        tmp, h2 = work[:, 0:2], work[:, 2:4]
        ss, rms, rstd = sb("pr_ss", [P, NT]), sb("pr_rms", [P, NT]), sb("pr_rstd", [P, NT])
        s1 = sb("pr_s1", [P, 2, 2, FF])
        act1 = sb("pr_act1", [P, 2, FF])
        aT = sb("pr_aT", [P, 2, 2, P])
        scores, sel, selm = (sb("pr_scores", [P, NT, NE]), sb("pr_sel", [P, NT, NE]), sb("pr_selm", [P, NT, NE]))
        top = sb("pr_top", [P, NT, NG, 8])
        gs, gv, gif = sb("pr_gs", [P, NT, NG]), sb("pr_gv", [P, NT, 8]), sb("pr_gif", [P, NT, 8])
        gi, ti = sb("pr_gi", [P, NT, 8], U32), sb("pr_ti", [P, NT, 8], U32)
        geq, gmask = sb("pr_geq", [P, NT, NG]), sb("pr_gmask", [P, NT, NG])
        tv, tif = sb("pr_tv", [P, NT, 8]), sb("pr_tif", [P, NT, 8])
        room = [mod[:].rearrange("p a b d -> p (a b d)")[:, n * TOP_K * NT * NE:(n + 1) * TOP_K * NT * NE]
                for n in range(2)]
        eq, pick = (v.rearrange("p (k c) -> p k c", k=TOP_K) for v in room[:2])
        emore = work[:].rearrange("p a d -> p (a d)")[:, 0:MORE * NE].rearrange("p (o e) -> p o e", e=NE)
        M = sb("pr_M", [P, NT, NE])
        wsum = sb("pr_wsum", [P, NT])
        iotai, iotaf = sb("pr_iotai", [P, P], I32), sb("pr_iota", [P, P])
        iota = iotaf[:, 0:NE]
        iotam = sb("pr_iotam", [P, MORE])
        before = sb("pr_before", [P, P])
        rowid, rowf = sb("pr_rowid", [P, TOP_K, NT], I32), sb("pr_rowf", [P, TOP_K, NT])
        at_place = [room[n][:, 0:TOP_K * P].rearrange("p (k c) -> p k c", k=TOP_K) for n in range(2)]
        at_block = [room[n][:, TOP_K * P:TOP_K * (P + NBLK)].rearrange("p (k c) -> p k c", k=TOP_K)
                    for n in range(2)]
        gap = sb("pr_gap", [P, NBLK])
        spare = mod[:].rearrange("p a b d -> p (a b d)")[:, 2 * TOP_K * NT * NE:]
        rank, q, blk = (spare[:, n * NT * NE:(n + 1) * NT * NE].rearrange("p (t e) -> p t e", e=NE) for n in range(3))
        inblk = sb("pr_inblk", [P, NT, NE])
        cnt, more, upto = sb("pr_cnt", [P, NE]), sb("pr_more", [P, NE]), sb("pr_upto", [P, NE])
        eblk = sb("pr_eblk", [P, NE])
        place, pblk = sb("pr_place", [P, TOP_K, NT]), sb("pr_pblk", [P, TOP_K, NT])
        emf, nmf = sb("pr_emf", [P, MORE]), sb("pr_nmf", [P, 1])

        s_wout = g.s_wout
        s_x, s_mod, s_sh, s_rt, s_const = (sem("pr_s_x"), sem("pr_s_mod"), sem("pr_s_sh"), sem("pr_s_rt"),
                                           sem("pr_s_const"))
        s_o, s_x1, s_sq, s_ms, s_sqrt, s_h2, s_h2st = (sem("pr_s_o"), sem("pr_s_x1"), sem("pr_s_sq"), sem("pr_s_ms"),
                                                       sem("pr_s_sqrt"), sem("pr_s_h2"), [sem("pr_s_h2st0"), sem("pr_s_h2st1")])
        s_tr, s_h2T, s_log, s_sc = sem("pr_s_tr"), sem("pr_s_h2T"), sem("pr_s_log"), sem("pr_s_sc")
        s_h13, s_silu, s_mul, s_at, s_aT, s_y, s_ysh = (sem("pr_s_h13"), sem("pr_s_silu"), sem("pr_s_mul"),
                                                        sem("pr_s_at"), sem("pr_s_aT"), sem("pr_s_y"), sem("pr_s_ysh"))
        s_M, s_rank, s_ones, s_tab = sem("pr_s_M"), sem("pr_s_rank"), sem("pr_s_ones"), sem("pr_s_tab")
        h2T, ysh = g.hT, g.oT[:].rearrange("p a b -> p (a b)").rearrange("p (t d) -> p t d", d=D)
        block = ctx.enter_context(nc.Block())

        @block.sync
        def _(sp):
            sp.dma_start(m.x[:, 0, :], w["x_prompt"][0]).then_inc(s_x, 16)
            sp.dma_start(m.x[:, 1:NT, :], w["x_sample"][0].rearrange("(t p) d -> p t d", p=P)).then_inc(s_x, 16)
            for n, part in enumerate((2, 3, 4)):
                for s in range(2):
                    sp.dma_start(mod[:, n, s], g.mod_dram[s:s + 1, part * D:(part + 1) * D].to_broadcast([P, D])
                                 ).then_inc(s_mod, 16)
            sp.dma_start(h2[:, 1], w["norm2"].to_broadcast([P, D])).then_inc(s_mod, 16)
            sp.dma_start(wr[:], w["router_w"][0].rearrange("(p k) e -> p k e", k=KD)).then_inc(s_rt, 16)
            sp.dma_start(br[:], w["router_b"].to_broadcast([P, NE])).then_inc(s_rt, 16)
            sp.dma_start(w13[:, :, 0, :], w["sh_w1"][0].rearrange("(p k) f -> p k f", k=KD)).then_inc(s_sh, 16)
            sp.dma_start(w13[:, :, 1, :], w["sh_w3"][0].rearrange("(p k) f -> p k f", k=KD)).then_inc(s_sh, 16)
            sp.dma_start(w2[:], w["sh_w2"][0].rearrange("(p j) d -> p j d", j=2)).then_inc(s_sh, 16)
            for t in range(NT):
                sp.wait_ge(s_h2, t + 1)
                sp.dma_start(m.h_dram[t * P:(t + 1) * P, :], h2[:, t % 2]).then_inc(s_h2st[t % 2], 16)
            sp.wait_ge(s_o, NT)
            for b in range(2):
                load_w13(sp, w, m, b, b)
                load_w2(sp, w, m, b, b)
            for b in range(2):
                sp.wait_ge(s_h2st[b], 16 * ((NT + 1 - b) // 2))

        @block.gpsimd
        def _(pool):
            chain = Chain(pool, g.pool_steps)
            chain.step(nc.gpsimd.iota(iotai[:], pattern=[[1, P]], base=0, channel_multiplier=0))
            chain.step(nc.gpsimd.iota(rowid[:], pattern=[[1, TOP_K], [P * TOP_K, NT]], base=1,
                                      channel_multiplier=TOP_K))
            chain.step(nc.gpsimd.affine_select(out=before[:], in_=g.ones[:], compare_op=ALU.is_ge, fill=0.0,
                                               base=-1, pattern=[[1, P]], channel_multiplier=-1))
            nc.gpsimd.nop().then_inc(s_const, 1)
            for t in range(NT):
                pool.wait_ge(s_silu, t + 1)
                if t >= 2:
                    pool.wait_ge(s_at, t - 1)
                def split(v):
                    return v.rearrange("p (a j) -> p a j", j=2)
                nc.gpsimd.tensor_tensor(act1[:, t % 2].rearrange("p (j a) -> p a j", j=2), split(s1[:, t % 2, 0]),
                                        split(s1[:, t % 2, 1]), ALU.mult).then_inc(s_mul, 1)

        @block.tensor
        def _(pe):
            def transposes(t):
                pe.wait_ge(s_h2, t + 1)
                if t >= 1:
                    pe.wait_ge(s_h2T, t)
                for k in range(KD):
                    last = nc.tensor.transpose(g.ps[:, 4 + k // 4, (k % 4) * P:(k % 4 + 1) * P],
                                               h2[:, t % 2, k * P:(k + 1) * P], g.blocks[:, 0, :])
                last.then_inc(s_tr, 1)

            for t in range(NT):
                if t >= 2:
                    pe.wait_ge(s_x1, t - 1)
                for n in range(2):
                    if t == 0:
                        pe.wait_ge(s_wout, 32)
                    for k in range(KD):
                        last = nc.tensor.matmul(g.ps[:, 2 * (t % 2) + n, :], g.oT[:, k, t * P:(t + 1) * P],
                                                wout[n][:, k], start=k == 0, stop=k == KD - 1)
                last.then_inc(s_o, 1)
                if t:
                    transposes(t - 1)
            pe.wait_ge(s_rt, 32)
            for t in range(NT):
                if t == NT - 1:
                    transposes(t)
                pe.wait_ge(s_h2T, t + 1)
                for k in range(KD):
                    last = nc.tensor.matmul(g.ps[:, 6, t * NE:(t + 1) * NE], h2T[:, k, t * P:(t + 1) * P],
                                            wr[:, k, :], start=k == 0, stop=k == KD - 1)
            last.then_inc(s_log, 1)
            pe.wait_ge(s_sh, 48)
            def up(t):
                if t == 1:
                    pe.wait_ge(s_sc, 1)
                if t >= 2:
                    pe.wait_ge(s_silu, t - 1)
                for k in range(KD):
                    last = nc.tensor.matmul(g.ps[:, 7 - t % 2, :], h2T[:, k, t * P:(t + 1) * P],
                                            w13[:, k].rearrange("p a f -> p (a f)"), start=k == 0, stop=k == KD - 1)
                last.then_inc(s_h13, 1)

            up(0)
            for t in range(NT):
                if t + 1 < NT:
                    up(t + 1)
                if t == 0:
                    pe.wait_ge(s_M, 1)
                    for u in range(NT + 1):
                        out = g.ps[:, 5, u * NE:(u + 1) * NE]
                        for v in range(min(u, NT - 1) + 1):
                            last = nc.tensor.matmul(out, before[:] if v == u else g.ones[:], M[:, v, :],
                                                    start=v == 0, stop=v == min(u, NT - 1))
                    last.then_inc(s_rank, 1)
                pe.wait_ge(s_mul, t + 1)
                pe.wait_ge(s_aT, t)
                if t == 0:
                    pe.wait_ge(s_sc, 1)
                for j in range(2):
                    last = nc.tensor.transpose(g.ps[:, 4, j * P:(j + 1) * P], act1[:, t % 2, j * P:(j + 1) * P],
                                               g.blocks[:, 0, :])
                last.then_inc(s_at, 1)
                pe.wait_ge(s_aT, t + 1)
                if t == 0:
                    pe.wait_ge(s_x1, NT)
                if t >= 2:
                    pe.wait_ge(s_ysh, t - 1)
                for n in range(2):
                    for j in range(2):
                        last = nc.tensor.matmul(g.ps[:, 2 * (t % 2) + n, :], aT[:, t % 2, j],
                                                w2[:, j, n * 512:(n + 1) * 512], start=j == 0, stop=j == 1)
                last.then_inc(s_y, 1)
            for t in range(NT):
                pe.wait_ge(s_ones, 2 * t + 2)
                for k in range(TOP_K):
                    last = nc.tensor.matmul(g.ps[:, 6, 0:NBLK], at_place[t % 2][:, k], at_block[t % 2][:, k],
                                            start=t == 0 and k == 0, stop=t == NT - 1 and k == TOP_K - 1)
                last.then_inc(s_tab, 1)

        @block.scalar
        def _(act):
            for t in range(NT):
                act.wait_ge(s_x1, t + 1)
                if t:
                    act.wait_ge(s_sq, t)
                nc.scalar.activation(s1[:].rearrange("p a b f -> p (a b f)"), m.x[:, t, :], ACT.Square,
                                     accum_out=ss[:, t:t + 1]).then_inc(s_sq, 1)
                act.wait_ge(s_ms, t + 1)
                nc.scalar.activation(rms[:, t:t + 1], rms[:, t:t + 1], ACT.Sqrt).then_inc(s_sqrt, 1)
                act.wait_ge(s_tr, t + 1)
                nc.scalar.copy(h2T[:, :, t * P:(t + 1) * P],
                               g.ps[:, 4:6, :].rearrange("p a (b c) -> p (a b) c", b=4)).then_inc(s_h2T, 1)
            act.wait_ge(s_log, 1)
            nc.scalar.activation(scores[:].rearrange("p t e -> p (t e)"), g.ps[:, 6, 0:NT * NE],
                                 ACT.Sigmoid).then_inc(s_sc, 1)
            for t in range(NT):
                act.wait_ge(s_h13, t + 1)
                if t >= 2:
                    act.wait_ge(s_mul, t - 1)
                nc.scalar.activation(s1[:, t % 2, 0], g.ps[:, 7 - t % 2, 0:FF], ACT.Silu)
                nc.scalar.copy(s1[:, t % 2, 1], g.ps[:, 7 - t % 2, FF:2 * FF]).then_inc(s_silu, 1)
                act.wait_ge(s_at, t + 1)
                if t >= 2:
                    act.wait_ge(s_y, t - 1)
                nc.scalar.copy(aT[:, t % 2].rearrange("p j a -> p (j a)"), g.ps[:, 4, 0:2 * P]).then_inc(s_aT, 1)
                act.wait_ge(s_y, t + 1)
                nc.scalar.copy(ysh[:, t, :], g.ps[:, 2 * (t % 2):2 * (t % 2) + 2, :]
                               .rearrange("p a b -> p (a b)")).then_inc(s_ysh, 1)

        @block.vector
        def _(dve):
            chain = Chain(dve, g.dve_steps)
            dve.wait_ge(s_x, 32)
            def split(v):
                return v.rearrange("p (a k) -> p a k", k=KD)

            dve.wait_ge(s_mod, 112)
            for s in range(2):
                chain.step(nc.vector.scalar_tensor_tensor(mod[:, 2, s], mod[:, 2, s], 1.0, h2[:, 1], ALU.add,
                                                          ALU.mult))
            for t in range(NT):
                dve.wait_ge(s_o, t + 1)
                chain.step(nc.vector.tensor_tensor(tmp[:, t % 2], g.ps[:, 2 * (t % 2):2 * (t % 2) + 2, :]
                                                   .rearrange("p a b -> p (a b)"), mod[:, 0, min(t, 1)], ALU.mult))
                nc.vector.tensor_tensor(m.x[:, t, :], m.x[:, t, :], tmp[:, t % 2], ALU.add).then_inc(s_x1, 1)
                one, s = slice(t, t + 1), min(t, 1)
                dve.wait_ge(s_sq, t + 1)
                nc.vector.tensor_scalar(rms[:, one], ss[:, one], 1.0 / D, EPS, ALU.mult, ALU.add).then_inc(s_ms, 1)
                dve.wait_ge(s_sqrt, t + 1)
                chain.step(nc.vector.reciprocal(rstd[:, one], rms[:, one]))
                chain.step(nc.vector.scalar_tensor_tensor(tmp[:, t % 2], m.x[:, t, :], rstd[:, t:t + 1], mod[:, 2, s],
                                                          ALU.mult, ALU.mult))
                if t >= 2:
                    dve.wait_ge(s_tr, t - 1)
                    dve.wait_ge(s_h2st[t % 2], 16 * (t // 2))
                nc.vector.tensor_tensor(h2[:, t % 2].rearrange("p (k a) -> p a k", k=KD), split(tmp[:, t % 2]),
                                        split(mod[:, 1, s]), ALU.add).then_inc(s_h2, 1)
            dve.wait_ge(s_const, 1)
            chain.step(nc.vector.tensor_copy(iotaf[:], iotai[:]))
            chain.step(nc.vector.tensor_copy(rowf[:], rowid[:]))
            dve.wait_ge(s_sc, 1)
            dve.wait_ge(s_rt, 32)
            chain.step(nc.vector.tensor_tensor(sel[:], scores[:], br[:].unsqueeze(1).to_broadcast([P, NT, NE]), ALU.add))
            for t in range(NT):
                for n in range(NG):
                    last = nc.vector.max(top[:, t, n, :], sel[:, t, n * 8:(n + 1) * 8])
            chain.step(last)
            chain.step(nc.vector.tensor_tensor(gs[:], top[:, :, :, 0], top[:, :, :, 1], ALU.add))
            for t in range(NT):
                last = nc.vector.max(gv[:, t, :], gs[:, t, :])
            chain.step(last)
            for t in range(NT):
                last = nc.vector.max_index(gi[:, t, :], gv[:, t, :], gs[:, t, :])
            chain.step(last)
            chain.step(nc.vector.tensor_copy(gif[:], gi[:]))
            group = iota[:, 0:NG].unsqueeze(1).to_broadcast([P, NT, NG])
            chain.step(nc.vector.tensor_tensor(gmask[:], gif[:, :, 0:1].to_broadcast([P, NT, NG]), group, ALU.is_equal))
            for j in range(1, TOPG):
                chain.step(nc.vector.tensor_tensor(geq[:], gif[:, :, j:j + 1].to_broadcast([P, NT, NG]), group,
                                                   ALU.is_equal))
                chain.step(nc.vector.tensor_tensor(gmask[:], gmask[:], geq[:], ALU.add))
            def by_group(v):
                return v.rearrange("p t (g e) -> p (t g) e", g=NG)
            def over(v):
                return v.rearrange("p t g -> p (t g)").unsqueeze(2).to_broadcast([P, NT * NG, NE // NG])
            chain.step(nc.vector.tensor_tensor(by_group(selm[:]), by_group(sel[:]), over(gmask[:]), ALU.mult))
            chain.step(nc.vector.tensor_scalar(geq[:], gmask[:], 1e30, -1e30, ALU.mult, ALU.add))
            chain.step(nc.vector.tensor_tensor(by_group(selm[:]), by_group(selm[:]), over(geq[:]), ALU.add))
            for t in range(NT):
                last = nc.vector.max(tv[:, t, :], selm[:, t, :])
            chain.step(last)
            for t in range(NT):
                last = nc.vector.max_index(ti[:, t, :], tv[:, t, :], selm[:, t, :])
            chain.step(last)
            chain.step(nc.vector.tensor_copy(tif[:], ti[:]))
            for k in range(TOP_K):
                last = nc.vector.tensor_tensor(eq[:, k].rearrange("p (t e) -> p t e", e=NE),
                                               tif[:, :, k:k + 1].to_broadcast([P, NT, NE]),
                                               iota.unsqueeze(1).to_broadcast([P, NT, NE]), ALU.is_equal)
            chain.step(last)
            nc.vector.tensor_reduce(M[:].rearrange("p t e -> p (t e)"), eq.rearrange("p k c -> p c k"), AX,
                                    ALU.add).then_inc(s_M, 1)

            def choose(out, table):
                chain.step(nc.vector.tensor_tensor(pick, eq, table.rearrange("p t e -> p (t e)").unsqueeze(1)
                                                   .to_broadcast([P, TOP_K, NT * NE]), ALU.mult))
                chain.step(nc.vector.tensor_reduce(out, pick.rearrange("p k (t e) -> p (k t) e", e=NE), AX, ALU.add))

            choose(m.wts[:].rearrange("p k t -> p (k t)"), scores[:])
            chain.step(nc.vector.tensor_reduce(wsum[:], m.wts[:].rearrange("p k t -> p t k"), AX, ALU.add))
            chain.step(nc.vector.reciprocal(wsum[:], wsum[:]))
            chain.step(nc.vector.scalar_tensor_tensor(m.wts[:], m.wts[:], ROUTED_SCALE,
                                                      wsum[:].unsqueeze(1).to_broadcast([P, TOP_K, NT]),
                                                      ALU.mult, ALU.mult))
            dve.wait_ge(s_rank, 1)
            chain.step(nc.vector.tensor_copy(rank.rearrange("p t e -> p (t e)"), g.ps[:, 5, 0:NT * NE]))
            chain.step(nc.vector.tensor_copy(cnt[:], g.ps[:, 5, NT * NE:(NT + 1) * NE]))
            chain.step(nc.vector.tensor_scalar(q, rank, float(BLK), None, ALU.is_ge))
            chain.step(nc.vector.tensor_scalar(more[:], cnt[:], float(BLK + 1), None, ALU.is_ge))
            for j in range(2, TOK // BLK):
                chain.step(nc.vector.scalar_tensor_tensor(q, rank, float(BLK * j), q, ALU.is_ge, ALU.add))
                chain.step(nc.vector.scalar_tensor_tensor(more[:], cnt[:], float(BLK * j + 1), more[:], ALU.is_ge,
                                                          ALU.add))
            chain.step(nc.vector.scalar_tensor_tensor(inblk[:], q, -float(BLK), rank, ALU.mult, ALU.add))
            chain.step(nc.vector.tensor_tensor_scan(upto[:], g.ones[:, 0:NE], more[:], 0.0, ALU.mult, ALU.add))
            chain.step(nc.vector.tensor_tensor(eblk[:], upto[:], more[:], ALU.subtract))
            chain.step(nc.vector.scalar_tensor_tensor(eblk[:], eblk[:], float(NE - 1), iota, ALU.add, ALU.subtract))
            chain.step(nc.vector.tensor_scalar(blk, q, 1.0, None, ALU.min))
            chain.step(nc.vector.tensor_tensor(blk, blk, eblk[:].unsqueeze(1).to_broadcast([P, NT, NE]), ALU.mult))
            chain.step(nc.vector.tensor_tensor(blk, blk, q, ALU.add))
            chain.step(nc.vector.tensor_tensor(blk, blk, iota.unsqueeze(1).to_broadcast([P, NT, NE]), ALU.add))
            choose(place[:].rearrange("p k t -> p (k t)"), inblk[:])
            choose(pblk[:].rearrange("p k t -> p (k t)"), blk)
            for t in range(NT):
                if t >= 2:
                    dve.wait_ge(s_tab, t - 1)
                nc.vector.tensor_tensor(at_place[t % 2], iotaf[:].unsqueeze(1).to_broadcast([P, TOP_K, P]),
                                        place[:, :, t:t + 1].to_broadcast([P, TOP_K, P]),
                                        ALU.is_equal).then_inc(s_ones, 1)
                chain.step(nc.vector.tensor_tensor(at_block[t % 2],
                                                   iotaf[:, 0:NBLK].unsqueeze(1).to_broadcast([P, TOP_K, NBLK]),
                                                   pblk[:, :, t:t + 1].to_broadcast([P, TOP_K, NBLK]), ALU.is_equal))
                nc.vector.tensor_tensor(at_block[t % 2], at_block[t % 2],
                                        rowf[:, :, t:t + 1].to_broadcast([P, TOP_K, NBLK]),
                                        ALU.mult).then_inc(s_ones, 1)
            chain.step(nc.vector.tensor_scalar(iotam[:], iota[:, 0:MORE], 1.0, None, ALU.mult))
            for b in range(2):
                dve.wait_ge(s_h2st[b], 16 * ((NT + 1 - b) // 2))
            chain.step(nc.vector.tensor_tensor(emore, upto[:].unsqueeze(1).to_broadcast([P, MORE, NE]),
                                               iotam[:].unsqueeze(2).to_broadcast([P, MORE, NE]), ALU.is_le))
            chain.step(nc.vector.tensor_reduce(emf[:], emore, AX, ALU.add))
            chain.step(nc.vector.tensor_scalar(emf[:], emf[:], float(NE - 1), None, ALU.min))
            chain.step(nc.vector.tensor_copy(m.emore[:], emf[0:1, :]))
            chain.step(nc.vector.tensor_scalar(emf[:], iotam[:], 2.0, upto[:, NE - 1:NE], ALU.mult, ALU.is_lt))
            chain.step(nc.vector.tensor_reduce(nmf[:], emf[:], AX, ALU.add))
            chain.step(nc.vector.tensor_scalar(nmf[:], nmf[:], 1.0, None, ALU.max))
            chain.step(nc.vector.tensor_copy(m.pairs[:], nmf[0:1, :]))
            dve.wait_ge(s_tab, NT)
            chain.step(nc.vector.tensor_scalar(gap[:], g.ps[:, 6, 0:NBLK], 0.0, float(ROWS + TOP_K), ALU.is_equal,
                                               ALU.mult))
            chain.step(nc.vector.scalar_tensor_tensor(m.rows[:], g.ps[:, 6, 0:NBLK], -1.0, gap[:], ALU.add, ALU.add))
            chain.step(nc.vector.tensor_scalar(m.toks[:], m.rows[:], int(math.log2(TOP_K)), None,
                                               ALU.logical_shift_right))


def load_w13(eng, w, m, e, b):
    for n, name in enumerate(("exp_w1", "exp_w3")):
        src = w[name][0, bass.ds(e, 1)].rearrange("o (p k) f -> p (o k) f", k=KD)
        eng.dma_start(m.w13[b][:, :, n, :], src).then_inc(m.s_w13[b], 16)


def load_w2(eng, w, m, e, b):
    src = w["exp_w2"][0, bass.ds(e, 1)].rearrange("o (p j) d -> p (o j) d", j=2)
    eng.dma_start(m.w2[b][:], src).then_inc(m.s_w2[b], 16)


def stage_experts(nc, g, w, m):
    with ExitStack() as ctx:
        def sb(name, shape, dt=F32):
            return ctx.enter_context(nc.sbuf_tensor(name, shape, dt))

        def sem(name):
            return ctx.enter_context(nc.semaphore(name))

        B2 = range(2)
        w13, w2, s_w13, s_w2 = m.w13, m.w2, m.s_w13, m.s_w2
        ids = [sb(f"ex_ids{b}", [P, 1], I32) for b in B2]
        outs = [sb(f"ex_outs{b}", [P, 1], I32) for b in B2]
        xg = [sb(f"ex_xg{b}", [P, D]) for b in B2]
        xT = [sb(f"ex_xT{b}", [P, KD, P]) for b in B2]
        silu = [sb(f"ex_silu{b}", [P, FF]) for b in B2]
        hid = [sb(f"ex_hid{b}", [P, FF]) for b in B2]
        hT = [sb(f"ex_hT{b}", [P, 2, P]) for b in B2]
        yo = [sb(f"ex_y{b}", [P, D]) for b in B2]

        s_xg, s_st = ([sem(f"ex_s_{n}{b}") for b in B2] for n in ("xg", "st"))
        s_ids, s_outs, s_begun = sem("ex_s_ids"), sem("ex_s_outs"), sem("ex_s_begun")
        names = ("xt", "xT0", "xT1", "up", "silu", "hid", "ht", "hT", "down", "y0", "y1")
        s = {n: sem(f"ex_{n}") for n in names}
        owner = {"xt": "pe", "up": "pe", "ht": "pe", "down": "pe", "xT0": "act", "silu": "act", "y0": "act",
                 "xT1": "dve", "hid": "dve", "hT": "dve", "y1": "dve"}

        def prime(eng, who):
            for n in names:
                if owner[n] == who:
                    eng.nop().then_inc(s[n], 2)

        def done(eng, name, n):
            eng.wait_ge(s[name], n + 3)

        def freed(eng, name, n):
            eng.wait_ge(s[name], n + 1)

        def landed(eng, sems, b, half, count=16):
            eng.wait_ge(sems[b], half * count + count)

        def loops(eng):
            yield NE // U_MAIN, U_MAIN, 0
            yield eng.value_load(m.pairs[0:1, 0:1], min_val=1, max_val=MORE // 2), U_MORE, NE

        block = ctx.enter_context(nc.Block())

        @block.sync
        def _(sp):
            def body(i, U, n0):
                for u in range(U):
                    n, b = i * U + (n0 + u), u % 2
                    if isinstance(i, int):
                        e = n
                    elif n0 == 0:
                        e = sp.snap(n)
                    else:
                        e = sp.value_load(m.emore[0:1, bass.ds(i * U + u, 1)], min_val=0, max_val=NE - 1)
                    if not isinstance(n, int) or n >= 2:
                        freed(sp, "up", n)
                        load_w13(sp, w, m, e, b)
                    if u:
                        before()

                    def before(n=n, b=b, e=e):
                        if not isinstance(n, int) or n >= 2:
                            freed(sp, "down", n)
                            load_w2(sp, w, m, e, b)
                before()

            body(0, U_MAIN, 0)
            for bodies, U, n0 in loops(sp):
                with sp.Fori(0 if n0 else 1, bodies) as i:
                    body(i, U, n0)

        @block.gpsimd
        def _(pool):
            def gather(n, col, b, wait=True):
                if wait:
                    freed(pool, "xt", n)
                nc.gpsimd.tensor_copy(ids[b][:], m.toks[:, col]).then_inc(s_ids, 1)
                if wait:
                    wait_apart(pool, s_ids, n + 1, s_begun)
                else:
                    pool.wait_ge(s_ids, n + 1)
                nc.gpsimd.indirect_dma_start(out=xg[b][:], out_offset=None, in_=m.h_dram,
                                             in_offset=bass.IndirectOffsetOnAxis(ap=ids[b][:, 0:1], axis=0),
                                             bounds_check=TOK - 1, oob_is_err=False).then_inc(s_xg[b], 16)

            def scatter(n, b):
                col = pool.snap(n)
                done(pool, "y0", n)
                done(pool, "y1", n)
                nc.gpsimd.tensor_copy(outs[b][:], m.rows[:, bass.ds(col, 1)]).then_inc(s_outs, 1)
                wait_apart(pool, s_outs, n + 3, s_begun)
                nc.gpsimd.indirect_dma_start(out=m.y_dram,
                                             out_offset=bass.IndirectOffsetOnAxis(ap=outs[b][:, 0:1], axis=0),
                                             in_=yo[b][:], in_offset=None,
                                             bounds_check=ROWS - 1, oob_is_err=False).then_inc(s_st[b], 16)

            for b in B2:
                nc.gpsimd.memset(xg[b][:], 0.0).then_inc(s_begun, 1)
            pool.wait_ge(s_begun, 2)
            pool.nop().then_inc(s_outs, 2)
            for b in B2:
                gather(b, slice(b, b + 1), b, wait=False)
            for bodies, U, n0 in loops(pool):
                with pool.Fori(0, bodies) as i:
                    for u in range(U):
                        n = i * U + (n0 + u)
                        gather(n + 2, bass.ds(pool.snap(n + 2), 1), u % 2)
                        if u:
                            scatter(n - 1, (u - 1) % 2)
                    scatter(n, (U - 1) % 2)
            for b in B2:
                pool.wait_ge(s_st[b], bodies * 16 + 16 * (NE // 2))

        @block.tensor
        def _(pe):
            prime(pe, "pe")

            def transposes(n, b, half):
                landed(pe, s_xg, b, half)
                done(pe, "xT0", n - 1)
                done(pe, "xT1", n - 1)
                for k in range(KD):
                    last = nc.tensor.transpose(g.ps[:, k // 4, (k % 4) * P:(k % 4 + 1) * P],
                                               xg[b][:, k * P:(k + 1) * P], g.blocks[:, 0, :])
                last.then_inc(s["xt"], 1)

            def down(n, b, half):
                done(pe, "hT", n)
                landed(pe, s_w2, b, half)
                done(pe, "y0", n - 1)
                done(pe, "y1", n - 1)
                for c in range(2):
                    for j in range(2):
                        last = nc.tensor.matmul(g.ps[:, 6 + c, :], hT[b][:, j], w2[b][:, j, c * 512:(c + 1) * 512],
                                                start=j == 0, stop=j == 1)
                last.then_inc(s["down"], 1)

            transposes(0, 0, 0)
            for bodies, U, n0 in loops(pe):
                with pe.Fori(0, bodies) as i:
                    for u in range(U):
                        n, b = i * U + (n0 + u), u % 2
                        half = i * (U // 2) + (n0 + u) // 2
                        done(pe, "xT0", n)
                        done(pe, "xT1", n)
                        landed(pe, s_w13, b, half, 32)
                        freed(pe, "hid", n)
                        for k in range(KD):
                            last = nc.tensor.matmul(g.ps[:, 2 + b, :], xT[b][:, k],
                                                    w13[b][:, k].rearrange("p a f -> p (a f)"),
                                                    start=k == 0, stop=k == KD - 1)
                        last.then_inc(s["up"], 1)
                        transposes(n + 1, 1 - b, i * (U // 2) + (n0 + u + 1) // 2)
                        if u:
                            down(n - 1, 1 - b, i * (U // 2) + (n0 + u - 1) // 2)
                        done(pe, "hid", n)
                        freed(pe, "hT", n)
                        for j in range(2):
                            last = nc.tensor.transpose(g.ps[:, 4 + b, j * P:(j + 1) * P],
                                                       hid[b][:, j * P:(j + 1) * P], g.blocks[:, 0, :])
                        last.then_inc(s["ht"], 1)
                    down(n, b, half)

        @block.scalar
        def _(act):
            prime(act, "act")

            def copy_xT(n, b):
                done(act, "xt", n)
                freed(act, "up", n)
                nc.scalar.copy(xT[b][:, 0:4].rearrange("p k a -> p (k a)"), g.ps[:, 0, :]).then_inc(s["xT0"], 1)

            def copy_y(n, b, half):
                done(act, "down", n)
                act.wait_ge(s_st[b], half * 16)
                nc.scalar.copy(yo[b][:, 0:512], g.ps[:, 6, :]).then_inc(s["y0"], 1)

            copy_xT(0, 0)
            for bodies, U, n0 in loops(act):
                with act.Fori(0, bodies) as i:
                    for u in range(U):
                        n, b = i * U + (n0 + u), u % 2
                        done(act, "up", n)
                        freed(act, "hid", n)
                        nc.scalar.activation(silu[b][:], g.ps[:, 2 + b, 0:FF], ACT.Silu).then_inc(s["silu"], 1)
                        copy_xT(n + 1, 1 - b)
                        if u:
                            copy_y(n - 1, 1 - b, i * (U // 2) + (n0 + u - 1) // 2)
                    copy_y(n, b, i * (U // 2) + (n0 + u) // 2)

        @block.vector
        def _(dve):
            prime(dve, "dve")

            def copy_xT(n, b):
                done(dve, "xt", n)
                freed(dve, "up", n)
                nc.vector.tensor_copy(xT[b][:, 4:8].rearrange("p k a -> p (k a)"), g.ps[:, 1, :]).then_inc(s["xT1"], 1)

            def copy_y(n, b, half):
                done(dve, "down", n)
                dve.wait_ge(s_st[b], half * 16)
                nc.vector.tensor_copy(yo[b][:, 512:D], g.ps[:, 7, :]).then_inc(s["y1"], 1)

            copy_xT(0, 0)
            for bodies, U, n0 in loops(dve):
                with dve.Fori(0, bodies) as i:
                    for u in range(U):
                        n, b = i * U + (n0 + u), u % 2
                        done(dve, "silu", n)
                        freed(dve, "ht", n)
                        nc.vector.tensor_tensor(hid[b][:].rearrange("p (j a) -> p a j", j=2),
                                                silu[b][:].rearrange("p (a j) -> p a j", j=2),
                                                g.ps[:, 2 + b, FF:2 * FF].rearrange("p (a j) -> p a j", j=2),
                                                ALU.mult).then_inc(s["hid"], 1)
                        copy_xT(n + 1, 1 - b)
                        if u:
                            copy_y(n - 1, 1 - b, i * (U // 2) + (n0 + u - 1) // 2)
                        done(dve, "ht", n)
                        freed(dve, "down", n)
                        nc.vector.tensor_copy(hT[b][:].rearrange("p j a -> p (j a)"),
                                              g.ps[:, 4 + b, 0:2 * P]).then_inc(s["hT"], 1)
                    copy_y(n, b, i * (U // 2) + (n0 + u) // 2)


def stage_combine(nc, g, w, m):
    NBUF, HD, HK = 3, D // 2, TOP_K // 2
    with ExitStack() as ctx:
        def sb(name, shape, dt=F32):
            return ctx.enter_context(nc.sbuf_tensor(name, shape, dt))

        def sem(name):
            return ctx.enter_context(nc.semaphore(name))

        rows = [[sb(f"cb_rows{b}{half}", [P, HK, D]) for half in range(2)] for b in range(NBUF - 1)]
        rows.append([t.rearrange("p k a f -> p (k a f)").rearrange("p (k d) -> p k d", d=D) for t in m.w13])
        diag = sb("cb_diag", [P, 2, TOP_K, P])
        g2 = sb("cb_g2", [P, 2, D])
        nf = sb("cb_nf", [P, D])
        sq = sb("cb_sq", [P, D])
        ss, rms, rstd = sb("cb_ss", [P, NT]), sb("cb_rms", [P, NT]), sb("cb_rstd", [P, NT])
        s_row = [[sem(f"cb_s_row{b}{half}") for half in range(2)] for b in range(NBUF)]
        s_sum, s_acc, s_in, s_x, s_ms, s_out = (sem("cb_s_sum"), sem("cb_s_acc"), sem("cb_s_in"), sem("cb_s_x"),
                                                sem("cb_s_ms"), sem("cb_s_out"))
        s_st = s_in
        s_pool, pool0, s_act, act0 = g.pool_steps.sem, g.pool_steps.n, g.act_steps.sem, g.act_steps.n

        def squared(eng, t):
            eng.wait_ge(s_act, act0 + 2 * t + 1)

        acc = g.oT[:].rearrange("p a b -> p (a b)").rearrange("p (t d) -> p t d", d=D)
        block = ctx.enter_context(nc.Block())

        def landed(eng, t, k):
            eng.wait_ge(s_row[t % NBUF][k // HK], 16 * (t // NBUF + 1))

        @block.sync
        def _(sp):
            def load(t):
                if t >= NBUF:
                    sp.wait_ge(s_acc, TOP_K * (t - NBUF + 1))
                    sp.wait_ge(s_sum, t - NBUF + 1)
                src = m.y_dram[t * P * TOP_K:(t + 1) * P * TOP_K, :].rearrange("(p k) d -> p k d", k=TOP_K)
                for half in range(2):
                    ks = slice(half * HK, half * HK + HK)
                    sp.dma_start(rows[t % NBUF][half][:], src[:, ks]).then_inc(s_row[t % NBUF][half], 16)

            load(0)
            for s in range(2):
                sp.dma_start(g2[:, s], g.mod_dram[s:s + 1, 5 * D:6 * D].to_broadcast([P, D])).then_inc(s_in, 16)
            sp.dma_start(nf[:], w["norm_f"].rearrange("(o d) -> o d", o=1).to_broadcast([P, D])).then_inc(s_in, 16)
            for t in range(1, NBUF):
                load(t)
            for t in range(NT):
                if t + NBUF < NT:
                    load(t + NBUF)
                sp.wait_ge(s_out, t + 1)
                dst = w["y_prompt"][0] if t == 0 else w["y_sample"][0, (t - 1) * P:t * P, :]
                sp.dma_start(dst, m.x[:, t, :]).then_inc(s_st, 16)
            sp.wait_ge(s_st, 48 + 16 * NT)

        @block.gpsimd
        def _(pool):
            for t in range(NT):
                if t >= 2:
                    pool.wait_ge(s_sum, t - 1)
                nc.gpsimd.tensor_tensor(diag[:, t % 2], g.blocks[:, 0:1, :].to_broadcast([P, TOP_K, P]),
                                        m.wts[:, :, t:t + 1].to_broadcast([P, TOP_K, P]),
                                        ALU.mult).then_inc(s_pool, 1)

        @block.tensor
        def _(pe):
            for t in range(NT):
                pe.wait_ge(s_pool, pool0 + t + 1)
                if t >= 2:
                    pe.wait_ge(s_x, t - 1)
                for k in range(TOP_K):
                    if k % HK == 0:
                        landed(pe, t, k)
                    last = nc.tensor.matmul(g.ps[:, t % 2, :], diag[:, t % 2, k], rows[t % NBUF][k // HK][:, k % HK, 0:HD],
                                            start=k == 0, stop=k == TOP_K - 1)
                last.then_inc(s_sum, 1)

        @block.vector
        def _(dve):
            chain = Chain(dve, g.dve_steps)

            def finish(t):
                dve.wait_ge(s_act, act0 + 2 * t + 2)
                chain.step(nc.vector.reciprocal(rstd[:, t:t + 1], rms[:, t:t + 1]))
                nc.vector.scalar_tensor_tensor(m.x[:, t, :], m.x[:, t, :], rstd[:, t:t + 1], nf[:], ALU.mult,
                                               ALU.mult).then_inc(s_out, 1)
            for t in range(NT):
                for k in range(TOP_K):
                    n = t * TOP_K + k
                    if k % HK == 0:
                        landed(dve, t, k)
                    if k:
                        dve.wait_ge(s_acc, n)
                    nc.vector.scalar_tensor_tensor(acc[:, t, HD:D], rows[t % NBUF][k // HK][:, k % HK, HD:D],
                                                   m.wts[:, k, t:t + 1], acc[:, t, HD:D], ALU.mult, ALU.add).then_inc(s_acc, 1)
                dve.wait_ge(s_acc, (t + 1) * TOP_K)
                dve.wait_ge(s_sum, t + 1)
                chain.step(nc.vector.tensor_tensor(acc[:, t, 0:HD], g.ps[:, t % 2, :], acc[:, t, 0:HD], ALU.add))
                if t == 0:
                    dve.wait_ge(s_in, 48)
                chain.step(nc.vector.tensor_tensor(acc[:, t, :], acc[:, t, :], g2[:, min(t, 1)], ALU.mult))
                nc.vector.tensor_tensor(m.x[:, t, :], m.x[:, t, :], acc[:, t, :], ALU.add).then_inc(s_x, 1)
                squared(dve, t)
                nc.vector.tensor_scalar(rms[:, t:t + 1], ss[:, t:t + 1], 1.0 / D, EPS, ALU.mult,
                                        ALU.add).then_inc(s_ms, 1)
                if t:
                    finish(t - 1)
            finish(NT - 1)

        @block.scalar
        def _(act):
            for t in range(NT):
                act.wait_ge(s_x, t + 1)
                if t:
                    squared(act, t - 1)
                nc.scalar.activation(sq[:], m.x[:, t, :], ACT.Square, accum_out=ss[:, t:t + 1]).then_inc(s_act, 1)
                act.wait_ge(s_ms, t + 1)
                nc.scalar.activation(rms[:, t:t + 1], rms[:, t:t + 1], ACT.Sqrt).then_inc(s_act, 1)


def build(nc, w):
    with ExitStack() as ctx:
        def sb(name, shape, dt=F32):
            return ctx.enter_context(nc.sbuf_tensor(name, shape, dt))

        g, m = Shared(), Shared()
        g.dve_steps = Count(ctx.enter_context(nc.semaphore("dve_steps")))
        g.pool_steps = Count(ctx.enter_context(nc.semaphore("pool_steps")))
        g.act_steps = Count(ctx.enter_context(nc.semaphore("act_steps")))
        g.ps = ctx.enter_context(nc.psum_tensor("ps", [P, 8, 512], F32))
        g.blocks = sb("blocks", [P, 7, P])
        g.levels = sb("levels", [P, 6, P])
        g.tri = sb("tri", [P, 2, 2, P])
        g.ones = sb("ones", [P, P])
        g.hT = sb("hT", [P, KD, TOK])
        g.win = sb("win", [P, 2, KD, 512])
        g.s_win = [ctx.enter_context(nc.semaphore(f"s_win{b}")) for b in range(2)]
        g.s_wout = ctx.enter_context(nc.semaphore("s_wout"))
        g.scT = sb("silu_cT", [P, KD, 2])
        g.oT = sb("oT", [P, KD, TOK])
        g.mod_dram = nc.dram_tensor("mod_dram", [2, MOD], F32, kind="Internal").ap()
        m.h_dram = nc.dram_tensor("h_dram", [TOK, D], F32, kind="Internal").ap()
        m.y_dram = nc.dram_tensor("y_dram", [ROWS, D], F32, kind="Internal").ap()
        stage_modulation(nc, g, w)
        stage_gla(nc, g, w)
        stage_rwkv(nc, g, w)
        m.x = sb("x_res", [P, NT, D])
        m.rows = sb("rows", [P, NBLK], I32)
        m.toks = sb("toks", [P, NBLK], I32)
        m.wts = sb("wts", [P, TOP_K, NT])
        m.emore = sb("emore", [1, MORE], I32)
        m.pairs = sb("pairs", [1, 1], I32)
        m.w13 = [g.win[:, b].rearrange("p k (a f) -> p k a f", a=2) for b in range(2)]
        m.w2 = [sb(f"w2_{b}", [P, 2, D]) for b in range(2)]
        m.s_w13, m.s_w2 = ([ctx.enter_context(nc.semaphore(f"s_{n}{b}")) for b in range(2)] for n in ("w13", "w2"))
        stage_project_and_route(nc, g, w, m)
        stage_experts(nc, g, w, m)
        stage_combine(nc, g, w, m)


_INS = ['x_prompt', 'x_sample', 'c', 'state_gla', 'state_rwkv', 'c_ctx', 'ada_w', 'ada_b', 'norm1', 'norm2', 'norm_f',
        'w_in', 'w_out', 'gla_w_dec', 'gla_b_dec', 'gla_norm', 'rwkv_conv', 'rwkv_w2', 'rwkv_w0', 'rwkv_a2', 'rwkv_a0',
        'rwkv_g2', 'rwkv_k_k', 'rwkv_k_a', 'rwkv_r_k', 'rwkv_ln_g', 'rwkv_ln_b', 'router_w', 'router_b', 'exp_w1',
        'exp_w3', 'exp_w2', 'sh_w1', 'sh_w3', 'sh_w2']
_OUTS = [('y_prompt', (1, CTX, D)), ('y_sample', (1, LAT, D)), ('new_state_gla', (1, 1, 2, GLA_H, GLA_DK, GLA_DV)),
         ('new_state_rwkv', (1, 1, 2, RH, RN, RN))]


def kernel(**inputs):
    import numpy as _np
    import concourse.bacc as _bacc
    from concourse.bass_utils import run_bass_kernel_spmd as _run

    nc = _bacc.Bacc("TRN2", target_bir_lowering=False, num_devices=1)
    arrays, w = {}, {}
    for name in _INS:
        a = _np.ascontiguousarray(inputs[name])
        arrays[f"in_{name}_dram"] = a
        w[name] = nc.dram_tensor(f"in_{name}_dram", a.shape, F32, kind="ExternalInput").ap()
    for name, shape in _OUTS:
        w[name] = nc.dram_tensor(f"out_{name}_dram", shape, F32, kind="ExternalOutput").ap()
    build(nc, w)
    r = _run(nc, [arrays], core_ids=[0])
    return tuple(r.results[0][f"out_{name}_dram"] for name, _ in _OUTS)
```
